# Optimizing a Trainium2 kernel written in Bass

```python
import math
import jax, jax.numpy as jnp
from jax import lax
import numpy as np

D_MODEL = 1024
BATCH = 1
SEQ = 256
DEPTH = 2
DEC_BATCH = 1
DEC_SEQ = 64
PAST_LEN = 512

CHUNK = 64
N_MLSTM_LAYERS = (DEPTH + 1) // 2
N_POOL_LAYERS = DEPTH // 2
MLSTM_HEADS = 4
MLSTM_HEAD_DIM = D_MODEL // MLSTM_HEADS
POOL_WINDOWS = (2, 4, 8, 16)
POOL_GROUP = D_MODEL // len(POOL_WINDOWS)
POOL_STATE = max(POOL_WINDOWS) - 1
N_MEM = 256
XATTN_HEADS = 4
XATTN_HEAD_DIM = D_MODEL // XATTN_HEADS
PEER_HEADS = 8
PEER_N_KEYS = 128
PEER_EXPERTS = PEER_N_KEYS * PEER_N_KEYS
PEER_QUERY_DIM = 256
PEER_HALF = PEER_QUERY_DIM // 2
PEER_TOPK = 16
PEER_BLOCK = 256
EPS = 1e-6

kernel_name = "streaming_mlstm_pool_peer_step"

F32 = jnp.float32

def rmsnorm(x, g):
    xf = x.astype(F32)
    y = xf * lax.rsqrt(jnp.mean(xf * xf, axis=-1, keepdims=True) + EPS) * g.astype(F32)
    return y.astype(x.dtype)

def mlstm_project(u, w_in, b_i, b_f):
    B, T, _ = u.shape
    D, H, dh = D_MODEL, MLSTM_HEADS, MLSTM_HEAD_DIM
    z = u @ w_in
    q = z[..., :D].reshape(B, T, H, dh)
    k = z[..., D:2 * D].reshape(B, T, H, dh) * (dh ** -0.5)
    v = z[..., 2 * D:3 * D].reshape(B, T, H, dh)
    o = z[..., 3 * D:4 * D]
    ig = z[..., 4 * D:4 * D + H].astype(F32) + b_i.astype(F32)
    lf = jax.nn.log_sigmoid(z[..., 4 * D + H:].astype(F32) + b_f.astype(F32))
    return q, k, v, o, ig, lf

def mlstm_chunk(carry, inp):
    C, n, m = carry
    q, k, v, ig, lf = inp
    L = q.shape[1]
    bt = jnp.cumsum(lf, axis=1).transpose(0, 2, 1)
    igt = ig.transpose(0, 2, 1)
    logw = bt[:, :, :, None] - bt[:, :, None, :] + igt[:, :, None, :]
    mask = jnp.tril(jnp.ones((L, L), dtype=bool))
    logw = jnp.where(mask, logw, -jnp.inf)
    inter = bt + m[:, :, None]
    m_t = jnp.maximum(inter, jnp.max(logw, axis=-1))
    w = jnp.exp(logw - m_t[..., None])
    a_inter = jnp.exp(inter - m_t)
    sw = jnp.einsum('blhd,bshd->bhls', q, k).astype(F32) * w
    num = (a_inter[..., None] * jnp.einsum('blhd,bhde->bhle', q, C)
           + jnp.einsum('bhls,bshe->bhle', sw, v))
    den = a_inter * jnp.einsum('blhd,bhd->bhl', q, n) + jnp.sum(sw, axis=-1)
    h = num / jnp.maximum(jnp.abs(den), jnp.exp(-m_t))[..., None]
    m_new = m_t[:, :, -1]
    g_state = jnp.exp(bt[:, :, -1] + m - m_new)
    w_s = jnp.exp(bt[:, :, -1:] - bt + igt - m_new[..., None])
    kw = k * w_s.transpose(0, 2, 1)[..., None]
    C_new = g_state[..., None, None] * C + jnp.einsum('bshd,bshe->bhde', kw, v)
    n_new = g_state[..., None] * n + jnp.sum(kw, axis=1)
    return (C_new, n_new, m_new), h.transpose(0, 2, 1, 3)

def mlstm_output(h, o, g_head, w_out):
    B, T, H, dv = h.shape
    hf = h.astype(F32)
    mu = jnp.mean(hf, axis=-1, keepdims=True)
    var = jnp.mean(jnp.square(hf - mu), axis=-1, keepdims=True)
    hn = ((hf - mu) * lax.rsqrt(var + EPS)).reshape(B, T, H * dv) * g_head.astype(F32)
    y = (hn * jax.nn.sigmoid(o.astype(F32))).astype(o.dtype)
    return y @ w_out

def mlstm_prompt(u, w_in, b_i, b_f, g_head, w_out):
    B, T, _ = u.shape
    nc = T // CHUNK
    H, dh = MLSTM_HEADS, MLSTM_HEAD_DIM
    q, k, v, o, ig, lf = mlstm_project(u, w_in, b_i, b_f)

    def to_chunks(a):
        return jnp.moveaxis(a.reshape((B, nc, CHUNK) + a.shape[2:]), 1, 0)

    init = (jnp.zeros((B, H, dh, dh), F32), jnp.zeros((B, H, dh), F32), jnp.zeros((B, H), F32))
    (C, n, m), h = lax.scan(mlstm_chunk, init,
                            (to_chunks(q), to_chunks(k), to_chunks(v), to_chunks(ig), to_chunks(lf)))
    h = jnp.moveaxis(h, 0, 1).reshape(B, T, H, dh)
    return mlstm_output(h, o, g_head, w_out), C, n, m

def mlstm_sample(u, C, n, m, w_in, b_i, b_f, g_head, w_out):
    q, k, v, o, ig, lf = mlstm_project(u, w_in, b_i, b_f)
    (C, n, m), h = mlstm_chunk((C.astype(F32), n.astype(F32), m.astype(F32)), (q, k, v, ig, lf))
    return mlstm_output(h, o, g_head, w_out), C, n, m

def pool_mix(u, prefix, pos0, w_pool, s_pool):
    B, T, D = u.shape
    P = POOL_STATE
    ext = jnp.concatenate([prefix.astype(F32), u.astype(F32)], axis=1)
    S = jnp.concatenate([jnp.zeros((B, 1, D), F32), jnp.cumsum(ext, axis=1)], axis=1)
    end = S[:, P + 1:P + 1 + T]
    pos = pos0 + jnp.arange(T)
    outs = []
    for g, w in enumerate(POOL_WINDOWS):
        lo, hi = g * POOL_GROUP, (g + 1) * POOL_GROUP
        start = S[:, P + 1 - w:P + 1 - w + T, lo:hi]
        cnt = jnp.minimum(pos + 1, w).astype(F32)[None, :, None]
        p = (end[..., lo:hi] - start) / cnt - u[..., lo:hi].astype(F32)
        outs.append(jnp.einsum('btc,cd->btd', p, w_pool[g].astype(F32)))
    y = jnp.concatenate(outs, axis=-1) * s_pool.astype(F32)
    return y.astype(u.dtype)

def mem_kv(mem, g_mem, w_k, w_v):
    B = mem.shape[0]
    mn = rmsnorm(mem, g_mem)
    k = (mn @ w_k).reshape(B, N_MEM, XATTN_HEADS, XATTN_HEAD_DIM)
    v = (mn @ w_v).reshape(B, N_MEM, XATTN_HEADS, XATTN_HEAD_DIM)
    return k, v

def cross_attend(u, k, v, w_q, w_o):
    B, T, _ = u.shape
    q = (u @ w_q).reshape(B, T, XATTN_HEADS, XATTN_HEAD_DIM)
    s = jnp.einsum('bthd,bmhd->bhtm', q, k).astype(F32) * (XATTN_HEAD_DIM ** -0.5)
    p = jax.nn.softmax(s, axis=-1).astype(v.dtype)
    o = jnp.einsum('bhtm,bmhd->bthd', p, v).reshape(B, T, D_MODEL)
    return o @ w_o

def peer(u, w_q, sub_keys, expert_u, expert_v):
    B, T, D = u.shape
    flat = u.reshape(B * T, D)
    N = flat.shape[0]
    nblk = -(-N // PEER_BLOCK)
    flat_p = jnp.pad(flat, ((0, nblk * PEER_BLOCK - N), (0, 0))).reshape(nblk, PEER_BLOCK, D)

    def block(xb):
        Tb = xb.shape[0]
        q = (xb @ w_q).reshape(Tb, PEER_HEADS, 2, PEER_HALF)
        s = jnp.einsum('thpc,hpnc->thpn', q, sub_keys).astype(F32)
        sv, si = lax.top_k(s, PEER_TOPK)
        cand = (sv[:, :, 0, :, None] + sv[:, :, 1, None, :]).reshape(Tb, PEER_HEADS, PEER_TOPK * PEER_TOPK)
        cidx = (si[:, :, 0, :, None] * PEER_N_KEYS + si[:, :, 1, None, :]).reshape(Tb, PEER_HEADS, PEER_TOPK * PEER_TOPK)
        top, pos = lax.top_k(cand, PEER_TOPK)
        eidx = jnp.take_along_axis(cidx, pos, axis=-1)
        gate = jax.nn.softmax(top, axis=-1)
        ue = expert_u[eidx]
        act = jax.nn.gelu(jnp.einsum('td,thkd->thk', xb, ue).astype(F32), approximate=False)
        ve = expert_v[eidx]
        return jnp.einsum('thk,thkd->td', (gate * act).astype(ve.dtype), ve).astype(xb.dtype)

    out = lax.map(block, flat_p).reshape(nblk * PEER_BLOCK, D)[:N]
    return out.reshape(B, T, D)

def setup_inputs(seed: int = 0) -> dict:
    key = jax.random.key(seed)
    ks = iter(jax.random.split(key, 40))
    D, H, dh = D_MODEL, MLSTM_HEADS, MLSTM_HEAD_DIM

    def nrm(shape, scale=1.0):
        return jax.random.normal(next(ks), shape, F32) * scale

    def gain(shape):
        return 1.0 + 0.02 * jax.random.normal(next(ks), shape, F32)

    return {
        "x_prompt": nrm((BATCH, SEQ, D)),
        "x_sample": nrm((DEC_BATCH, DEC_SEQ, D)),
        "state_mlstm_C": nrm((N_MLSTM_LAYERS, DEC_BATCH, H, dh, dh), 0.1),
        "state_mlstm_n": nrm((N_MLSTM_LAYERS, DEC_BATCH, H, dh), 0.1),
        "state_mlstm_m": nrm((N_MLSTM_LAYERS, DEC_BATCH, H)),
        "state_pool": nrm((N_POOL_LAYERS, DEC_BATCH, POOL_STATE, D)),
        "cache_mem_k": nrm((DEPTH, DEC_BATCH, N_MEM, XATTN_HEADS, XATTN_HEAD_DIM)),
        "cache_mem_v": nrm((DEPTH, DEC_BATCH, N_MEM, XATTN_HEADS, XATTN_HEAD_DIM)),
        "mem_prompt": nrm((BATCH, N_MEM, D)),
        "g_mix": gain((DEPTH, D)),
        "w_mlstm_in": nrm((N_MLSTM_LAYERS, D, 4 * D + 2 * H), D ** -0.5),
        "b_mlstm_i": nrm((N_MLSTM_LAYERS, H), 0.1),
        "b_mlstm_f": jnp.linspace(3.0, 6.0, H, dtype=F32)[None, :] + nrm((N_MLSTM_LAYERS, H), 0.1),
        "g_mlstm_head": gain((N_MLSTM_LAYERS, D)),
        "w_mlstm_out": nrm((N_MLSTM_LAYERS, D, D), D ** -0.5),
        "w_pool": nrm((N_POOL_LAYERS, len(POOL_WINDOWS), POOL_GROUP, POOL_GROUP), POOL_GROUP ** -0.5),
        "s_pool": gain((N_POOL_LAYERS, D)),
        "g_xattn": gain((DEPTH, D)),
        "g_mem": gain((DEPTH, D)),
        "w_xq": nrm((DEPTH, D, D), D ** -0.5),
        "w_xk": nrm((DEPTH, D, D), D ** -0.5),
        "w_xv": nrm((DEPTH, D, D), D ** -0.5),
        "w_xo": nrm((DEPTH, D, D), D ** -0.5),
        "g_ffn": gain((DEPTH, D)),
        "w_peer_q": nrm((DEPTH, D, PEER_HEADS * PEER_QUERY_DIM), D ** -0.5),
        "peer_keys": nrm((DEPTH, PEER_HEADS, 2, PEER_N_KEYS, PEER_HALF), PEER_HALF ** -0.5),
        "peer_u": nrm((DEPTH, PEER_EXPERTS, D), D ** -0.5),
        "peer_v": nrm((DEPTH, PEER_EXPERTS, D), PEER_HEADS ** -0.5),
        "g_final": gain((D,)),
    }

def reference(x_prompt, x_sample, state_mlstm_C, state_mlstm_n, state_mlstm_m, state_pool,
              cache_mem_k, cache_mem_v, mem_prompt, g_mix, w_mlstm_in, b_mlstm_i, b_mlstm_f,
              g_mlstm_head, w_mlstm_out, w_pool, s_pool, g_xattn, g_mem, w_xq, w_xk, w_xv, w_xo,
              g_ffn, w_peer_q, peer_keys, peer_u, peer_v, g_final):
    xp, xs = x_prompt, x_sample
    Bp = xp.shape[0]
    C_p, n_p, m_p, C_s, n_s, m_s = [], [], [], [], [], []
    pool_p, pool_s, mk_p, mv_p = [], [], [], []
    for i in range(DEPTH):
        j = i // 2
        up = rmsnorm(xp, g_mix[i])
        us = rmsnorm(xs, g_mix[i])
        if i % 2 == 0:
            yp, C, n, m = mlstm_prompt(up, w_mlstm_in[j], b_mlstm_i[j], b_mlstm_f[j],
                                       g_mlstm_head[j], w_mlstm_out[j])
            C_p.append(C); n_p.append(n); m_p.append(m)
            ys, C, n, m = mlstm_sample(us, state_mlstm_C[j], state_mlstm_n[j], state_mlstm_m[j],
                                       w_mlstm_in[j], b_mlstm_i[j], b_mlstm_f[j],
                                       g_mlstm_head[j], w_mlstm_out[j])
            C_s.append(C); n_s.append(n); m_s.append(m)
        else:
            prefix = jnp.zeros((Bp, POOL_STATE, D_MODEL), up.dtype)
            yp = pool_mix(up, prefix, 0, w_pool[j], s_pool[j])
            pool_p.append(up[:, -POOL_STATE:])
            ys = pool_mix(us, state_pool[j], PAST_LEN, w_pool[j], s_pool[j])
            pool_s.append(jnp.concatenate([state_pool[j].astype(us.dtype), us], axis=1)[:, -POOL_STATE:])
        xp = xp + yp
        xs = xs + ys
        kp, vp = mem_kv(mem_prompt, g_mem[i], w_xk[i], w_xv[i])
        mk_p.append(kp); mv_p.append(vp)
        xp = xp + cross_attend(rmsnorm(xp, g_xattn[i]), kp, vp, w_xq[i], w_xo[i])
        xs = xs + cross_attend(rmsnorm(xs, g_xattn[i]), cache_mem_k[i], cache_mem_v[i], w_xq[i], w_xo[i])
        xp = xp + peer(rmsnorm(xp, g_ffn[i]), w_peer_q[i], peer_keys[i], peer_u[i], peer_v[i])
        xs = xs + peer(rmsnorm(xs, g_ffn[i]), w_peer_q[i], peer_keys[i], peer_u[i], peer_v[i])
    y_prompt = rmsnorm(xp, g_final)
    y_sample = rmsnorm(xs, g_final)
    return (y_prompt, y_sample,
            jnp.stack(C_p), jnp.stack(n_p), jnp.stack(m_p), jnp.stack(pool_p),
            jnp.stack(mk_p), jnp.stack(mv_p),
            jnp.stack(C_s), jnp.stack(n_s), jnp.stack(m_s), jnp.stack(pool_s))


_drawn_inputs = setup_inputs


def setup_inputs(seed=0):
    import zlib

    import numpy as np

    out = dict(_drawn_inputs(seed))
    spreads = {}
    factors = {'s_pool': 2.821, 'g_xattn': 3.929, 'g_mem': 2.836, 'g_final': 2.733}
    for name, (base, spread) in spreads.items():
        noise = np.random.default_rng([zlib.crc32(name.encode()), seed]).standard_normal(out[name].shape)
        drawn = base * np.exp(spread * noise) if base else spread * noise
        out[name] = __import__('jax').numpy.asarray(drawn.astype(out[name].dtype))
    for name, factor in factors.items():
        out[name] = (out[name] * factor).astype(out[name].dtype)
    return out
```

```python
from contextlib import ExitStack

import numpy as np
import concourse.bass as bass
import concourse.mybir as mybir

F32, F32R, U32 = mybir.dt.float32, mybir.dt.float32r, mybir.dt.uint32
ALU, ACT, AX = mybir.AluOpType, mybir.ActivationFunctionType, mybir.AxisListType

P = 128
D = 1024
KD = D // P
TOK = 320
TILES = ((0, 128), (128, 128), (256, 64))
NP_ = 256
NS = 64
H = 4
DH = D // H
VA = DH + 1
MEM = 256
PH = 8
HP = 2 * PH
NK = 128
TOPK = 16
SLOTS = PH * TOPK
NB = NK
LAG = 48
AHEAD = LAG - 20
UV = (NB - LAG) // 8
GC = 32
NGC = TOK // GC
EPS = 1e-6
NEG = -1e30
POOLW = (2, 4, 8, 16)
POOLST = 15

STAGES = [
    ("mixn0", 6, 0), ("qk", 16, 0), ("v", 6, 0), ("o", 0, 6), ("gates", 2, 0), ("cols", 1, 0),
    ("rb", 4, 0), ("sel", 1, 0), ("qkt", 12, 0), ("ktok", 6, 0), ("mix", 20, 0), ("state", 16, 0),
    ("yT", 6, 0), ("out", 6, 0),
    ("memT0", 4, 0), ("memk0", 4, 0), ("memv0", 4, 0), ("memkT0", 4, 0),
    ("xn0", 6, 0), ("xq0", 8, 0), ("sc0", 12, 0), ("av0", 16, 0), ("xo0", 6, 0),
    ("fn0", 6, 0), ("pq0", HP, HP), ("up0", 0, AHEAD), ("slot0", 3, 0), ("gb0", 0, 100), ("uv0", 0, NB - LAG),
    ("fold0", 2, 0),
    ("pool", 20, 0),
    ("memT1", 4, 0), ("memk1", 4, 0), ("memv1", 4, 0), ("memkT1", 4, 0),
    ("xn1", 6, 0), ("xq1", 8, 0), ("sc1", 12, 0), ("av1", 16, 0), ("xo1", 6, 0),
    ("fn1", 6, 0), ("pq1", HP, HP), ("up1", 0, AHEAD), ("slot1", 3, 0), ("gb1", 0, 100), ("uv1", 0, NB - LAG),
    ("fold1", 2, 0),
]
DJ, AJ = {}, {}
_d = _a = 0
for _n, _dj, _aj in STAGES:
    DJ[_n], AJ[_n] = _d, _a
    _d, _a = _d + _dj, _a + _aj
DJ["end"], AJ["end"] = _d, _a
DBANKS = (2, 3, 4, 5)
ABANKS = (0, 1, 6, 7)

WEIGHTS = [("qk", 4), ("vo", 4), ("out", 2), ("memk0", 2), ("memv0", 2), ("xq0", 2), ("xo0", 2), ("pq0", 4),
           ("U0", 64), ("memk1", 2), ("memv1", 2), ("xq1", 2), ("xo1", 2), ("pq1", 4), ("U1", 64)]
WC = {}
_c = 0
for _n, _k in WEIGHTS:
    WC[_n] = _c
    _c += _k

GAINS = ("mix0", "head", "mem0", "xn0", "fn0", "mix1", "spool", "mem1", "xn1", "fn1", "final")
NORMS = ("mix0", "xn0", "fn0", "mix1", "xn1", "fn1", "final")


def tri():
    return np.where(np.tril(np.ones((P, P), bool)), np.float32(0), np.float32(NEG)).astype(np.float32)


def constants():
    eye = np.eye(P, dtype=np.float32)
    iota = np.broadcast_to(np.arange(P, dtype=np.float32), (P, P))
    sel4 = np.zeros((P, H, P), np.float32)
    for h in range(H):
        sel4[h, h] = 1
    last_p = np.zeros((P, P), np.float32)
    last_p[P - 1] = 1
    last_s = np.zeros((P, P), np.float32)
    last_s[NS - 1] = 1
    fold = np.concatenate([np.eye(NS), np.eye(NS)]).astype(np.float32)
    return np.concatenate([eye, iota, tri(), sel4.reshape(P, -1), last_p, last_s, fold], axis=1)


def bands():
    p = np.zeros((P, 4, 2, NP_), np.float32)
    s = np.zeros((P, 4, NS), np.float32)
    for g, w in enumerate(POOLW):
        for t in range(NP_):
            for a in range(max(0, t - w + 1), t + 1):
                p[a % P, g, a // P, t] += 1.0 / min(t + 1, w)
            p[t % P, g, t // P, t] -= 1
        for t in range(NS):
            for a in range(t - w + 1, t + 1):
                s[a if a >= 0 else NS + POOLST + a, g, t] += 1.0 / w
            s[t, g, t] -= 1
    return np.concatenate([p.reshape(P, -1), s.reshape(P, -1)], axis=1)


class Chain:

    def __init__(self, eng, sem):
        self.eng, self.sem, self.n, self.i, self.per, self.base = eng, sem, 0, None, 0, 0

    def __call__(self, ins):
        self.n += 1
        ins.then_inc(self.sem, 1)
        self.eng.wait_ge(self.sem, self.n if self.i is None else self.i * self.per + self.n)

    def after(self, back):
        if self.n > back:
            self.eng.wait_ge(self.sem, self.n - back)

    def mark(self, ins):
        self.n += 1
        ins.then_inc(self.sem, 1)

    def restart(self):
        self.after(0)
        self.eng.sem_clear(self.sem)
        self.n = 0

    def loop(self, i, per):
        self.i, self.per, self.base = i, per, self.n

    def done(self, iterations):
        assert self.n - self.base == self.per, (self.n - self.base, self.per)
        self.n, self.i = self.base + iterations * self.per, None


def build(nc, t_in, t_out):
    with ExitStack() as ctx:
        def sb(name, cols, dt=F32):
            return ctx.enter_context(nc.sbuf_tensor(name, [P, cols], dt))

        def sem(name):
            return ctx.enter_context(nc.semaphore(name))

        g_dram = [nc.dram_tensor(f"gates_{l}", (NGC, P, NK // 4, 4 * GC), F32, kind="Internal").ap() for l in range(2)]

        x_sb = sb("x_sb", 3 * D)
        uT_sb = sb("uT_sb", KD * TOK)
        w_ring = sb("w_ring", 2 * KD * 512)
        p_f32 = sb("p_f32", 2 * TOK)
        p_hl = sb("p_hl", 2 * 2 * TOK, F32R)
        v_hl = sb("v_hl", 2 * 2 * D, F32R)
        gains = sb("gain_rows", 2 * D)
        cst = sb("cst", 3 * P + H * P + 2 * P + NS)
        picks = sb("picks", 9 * P)
        slotT = sb("slotT", 3 * TOK)
        small = sb("small", 64)
        arena = sb("arena", 27648)
        psum = ctx.enter_context(nc.psum_tensor("psum", [P, 8, 512], F32))

        def view(t, off, *dims):
            n = int(np.prod(dims))
            a = t[:, off:off + n]
            if len(dims) == 2:
                return a.rearrange("p (a b) -> p a b", b=dims[1])
            if len(dims) == 3:
                return a.rearrange("p (a b c) -> p a b c", b=dims[1], c=dims[2])
            if len(dims) == 4:
                return a.rearrange("p (a b c d) -> p a b c d", b=dims[1], c=dims[2], d=dims[3])
            return a

        x = view(x_sb, 0, 3, D)
        uT = view(uT_sb, 0, KD, TOK)
        W = [view(w_ring, s * KD * 512, KD, 512) for s in range(2)]
        Ublk = [view(w_ring, s * KD * 512, 2, KD, P) for s in range(2)]
        gain = view(gains, 0, 2, D)
        ident, iota, tri_m = cst[:, 0:P], cst[:, P:2 * P], cst[:, 2 * P:3 * P]
        sel4 = view(cst, 3 * P, H, P)
        last_p, last_s = cst[:, 7 * P:8 * P], cst[:, 8 * P:9 * P]
        fold = cst[:, 9 * P:9 * P + NS]
        ss, std, rstd = small[:, 0:3], small[:, 3:6], small[:, 6:9]
        mss, mstd, mrstd = small[:, 9:11], small[:, 11:13], small[:, 13:15]
        eps_c, one_c = small[:, 15:16], small[:, 16:17]
        nmx, rsum, rinv_p = small[:, 17:29], small[:, 29:41], small[:, 41:53]
        u = view(arena, 24576, 3, D)
        act4 = view(arena, 0, LAG // 4, 4, TOK)
        act8 = view(arena, 0, LAG // 8, 8, TOK)
        v_raw = view(arena, 17920, 2, 2, D)
        g_ring = view(arena, 22016, 2, NGC, 4 * GC)
        g_stage = view(arena, 17920, 2, NK, GC)
        qT, kT = view(arena, 0, KD, TOK), view(arena, 2560, KD, TOK)
        kw = view(arena, 5120, 3, D)
        v_aug = view(arena, 8192, 3, H, VA)
        wts = view(arena, 11280, H, 448)
        swT = view(arena, 13072, 2, 448)
        hn = view(arena, 13968, 3, H, VA)
        C_aug, C_new = view(arena, 17056, KD, VA), view(arena, 19112, KD, VA)
        R4 = view(arena, 21168, 6, TOK)
        wg = view(arena, 23088, KD, 2 * H)
        br, bm = view(arena, 23152, 3, 2 * H), view(arena, 23176, 3, 2 * H)
        m0c, inter, rmax, negm = (view(arena, 23200 + 12 * k, 3, H) for k in range(4))
        idiff, ainter, emneg, wsarg = (view(arena, 23248 + 12 * k, 3, H) for k in range(4))
        wscol, rinv, sdev, srec = (view(arena, 23296 + 12 * k, 3, H) for k in range(4))
        selev, blm, garg, gstate = arena[:, 23344:23360], view(arena, 23360, 2, H), arena[:, 23368:23372], arena[:, 23372:23376]
        mv = view(arena, 23376, 3, H, 2)
        bnst = view(arena, 23400, 3 * H, 6)
        qc_tmp = view(arena, 23740, 2, VA)
        b4 = arena[:, 23730:23732]
        mkT, mv_ = view(arena, 2560, KD, MEM), view(arena, 4608, 2, D)
        mk = view(arena, 6656, 2, D)
        skT, sv_ = view(arena, 8704, KD, MEM), view(arena, 10752, 2, D)
        probs = view(arena, 12800, H * 3, MEM)
        probsT = view(arena, 15872, 2, 2, TOK)
        memT, memx = view(arena, 17152, KD, MEM), view(arena, 19200, 2, D)
        wpool = view(arena, 0, 4, 2, DH)
        bandp, bands_ = view(arena, 2048, 4, 2, NP_), view(arena, 4096, 4, NS)
        plT = view(arena, 4352, KD, TOK)
        pool_tmp = view(arena, 8192, 2, DH)
        pqT = view(arena, 0, KD, TOK)
        keysT = view(arena, 2560, HP, NK)
        cur = view(arena, 17920, 2, 3, NK)
        spare = view(arena, 18688, 3, 2 * NK)
        cand = view(arena, 19456, 3, TOPK * TOPK)
        v16, i16 = view(arena, 20224, 4, 3, TOPK), view(arena, 20416, 4, 3, TOPK).bitcast(U32)
        sval, sidx = view(arena, 20608, HP, 3, TOPK), view(arena, 21376, HP, 3, TOPK)
        top, tpos = view(arena, 22144, PH, 3, TOPK), view(arena, 22528, PH, 3, TOPK)
        pij = view(arena, 22912, 3, 2, PH, TOPK)
        sume = view(arena, 23680, 3, 2 * PH)
        eq = view(arena, 23728, 2, PH // 2, TOPK, TOPK)
        picked = view(picks, 0, 3, 3, P)
        oh = view(picks, 0, 8, P)
        ohJ = view(arena, 26112, 8, P)
        slots = view(slotT, 0, 3, TOK)
        acc_tmp = view(arena, 17920, 2, 512)
        phl = view(p_hl, 0, 2, 2 * TOK)
        vhl = view(v_hl, 0, 2, 2, D)
        pf = view(p_f32, 0, 2, TOK)

        x_loaded, cst_loaded, mix_loaded = sem("x_loaded"), sem("cst_loaded"), sem("mix_loaded")
        w_loaded = [sem(f"w_loaded{s}") for s in range(2)]
        gain_loaded = [sem(f"gain_loaded{s}") for s in range(2)]
        mem_loaded, cache_loaded, pool_loaded, prefix_loaded, keys_loaded = (
            sem(n) for n in ("mem_loaded", "cache_loaded", "pool_loaded", "prefix_loaded", "keys_loaded"))
        v_loaded = [sem(f"v_loaded{s}") for s in range(2)]
        g_loaded = [sem(f"g_loaded{s}") for s in range(2)]
        g_stored = [sem(f"g_stored{s}") for s in range(2)]
        state_stored, mem_stored, pool_stored, y_stored = (
            sem(n) for n in ("state_stored", "mem_stored", "pool_stored", "y_stored"))
        d_filled, d_emptied, a_filled, a_emptied = (sem(n) for n in ("d_filled", "d_emptied", "a_filled", "a_emptied"))
        dve_step, dve_row_step, act_step = sem("dve_step"), sem("dve_row_step"), sem("act_step")
        init_done, std_ready, u_ready, mstd_ready, mu_ready = (
            sem(n) for n in ("init_done", "std_ready", "u_ready", "mstd_ready", "mu_ready"))
        gate_abs, gate_ln, gate_rows, m_ready, w_ready, mexp_ready = (
            sem(n) for n in ("gate_abs", "gate_ln", "gate_rows", "m_ready", "w_ready", "mexp_ready"))
        ws_arg, ws_ready, var_ready, sdev_ready, y_ready = (
            sem(n) for n in ("ws_arg", "ws_ready", "var_ready", "sdev_ready", "y_ready"))
        mx_ready, p_exp, p_ready, pooled = (sem(n) for n in ("mx_ready", "p_exp", "p_ready", "pooled"))
        top_ready, exp_ready, picked_ready, oh_ready = (
            sem(n) for n in ("top_ready", "exp_ready", "picked_ready", "oh_ready"))
        vhi_ready, v_split, p_split, v_summed, acc_emptied, acc_copied = (
            sem(n) for n in ("vhi_ready", "v_split", "p_split", "v_summed", "acc_emptied", "acc_copied"))
        prefix_clear, zero_ready, blm_ready = sem("prefix_clear"), sem("zero_ready"), sem("blm_ready")

        block = ctx.enter_context(nc.Block())

        def x_ready(norm, t):
            if norm == "mix0":
                return x_loaded, 48
            if norm in ("xn0", "xn1"):
                return (d_emptied, DJ["out"] + 4 + t) if norm == "xn0" else (pooled, 9 + t + 1)
            if norm in ("fn0", "fn1"):
                return d_emptied, DJ["xo" + norm[2]] + 4 + t
            l = 0 if norm == "mix1" else 1
            return (acc_emptied, 4 * l + 2 * t + 2) if t < 2 else (d_emptied, DJ[f"fold{l}"] + 2)

        @block.sync
        def _(sp):
            for k, (off, rows) in enumerate(TILES):
                src = t_in["x_prompt"][0, off:off + rows] if k < 2 else t_in["x_sample"][0]
                sp.dma_start(x[0:rows, k, :], src).then_inc(x_loaded, 16)

            def released(stage, local):
                if stage == "qk":
                    return d_filled, DJ["qk"] + 4 * (local + 1)
                if stage == "vo":
                    return (d_filled, DJ["v"] + 3 * (local + 1)) if local < 2 else (a_filled, AJ["o"] + 3 * (local - 1))
                if stage[:4] in ("memk", "memv"):
                    return d_filled, DJ[stage] + 2 * (local + 1)
                if stage[:2] == "xq":
                    return d_filled, DJ[stage] + 4 * (local + 1)
                if stage[:2] == "pq":
                    return a_filled, AJ[stage] + 4 * (local + 1)
                if stage[0] == "U":
                    assert 2 * local >= LAG
                    return a_filled, AJ["uv" + stage[1]] + 2 * (local + 1) - LAG
                return d_filled, DJ[stage] + 3 * (local + 1)

            flat = [(n, k) for n, cnt in WEIGHTS for k in range(cnt)]

            def chunk(stage, local, src):
                c = WC[stage] + local
                if c >= 2:
                    s, v = released(*flat[c - 2])
                    sp.wait_ge(s, v)
                sp.dma_start(W[c % 2], src).then_inc(w_loaded[c % 2], 16)

            def stage(name, src):
                for k in range(src.shape[0]):
                    chunk(name, k, src[k])

            stage("qk", t_in["w_qk"])
            stage("vo", t_in["w_vo"])
            stage("out", t_in["w_out"])
            for l in range(2):
                stage(f"memk{l}", t_in["w_xk"][l])
                stage(f"memv{l}", t_in["w_xv"][l])
                stage(f"xq{l}", t_in["w_xq"][l])
                stage(f"xo{l}", t_in["w_xo"][l])
                stage(f"pq{l}", t_in["w_pq"][l])
                U, V = t_in["peer_u"][l], t_in["peer_v"][l]
                ubase = WC[f"U{l}"]

                for k in range(2):
                    sm, v = released(f"pq{l}", 2 + k)
                    sp.wait_ge(sm, v)
                    sp.dma_start(Ublk[k], U[k]).then_inc(w_loaded[k], 16)
                with sp.Fori(0, AHEAD // 4) as i:
                    for s in range(2):
                        sp.wait_ge(a_filled, i * 4 + (AJ[f"up{l}"] + 2 * s + 2))
                        sp.dma_start(Ublk[s], U[i * 2 + (2 + s)]).then_inc(w_loaded[s], 16)
                with sp.Fori(0, 5) as i:
                    for s in range(2):
                        sp.wait_ge(a_filled, i * 20 + (AJ[f"gb{l}"] + 10 * s + 6))
                        sp.dma_start(Ublk[s], U[i * 2 + (AHEAD // 2 + 2 + s)]).then_inc(w_loaded[s], 16)

                for s in range(2):
                    sp.wait_ge(g_stored[s], 16 * (NGC // 2) * (l + 1))

                def u_load(i, q):
                    sp.wait_ge(a_filled, i * 8 + (AJ[f"uv{l}"] + 2 * q + 2))
                    sp.dma_start(Ublk[q % 2], U[i * 4 + (LAG // 2 + 2 + q)]).then_inc(w_loaded[q % 2], 16)

                def v_load(i, q):
                    sp.wait_ge(v_split, i * 8 + (NB * l + 2 * q + 2))
                    sp.dma_start(v_raw[:, q % 2], V[i * 4 + (2 + q)]).then_inc(v_loaded[q % 2], 16)

                def g_load(i, s):
                    sp.wait_ge(p_split, i * 8 + (NB * l + 4 * s + 4))
                    sp.dma_start(g_ring[:, s], g_dram[l][:, :, i * 2 + (2 + s)].rearrange("c j x -> j c x")
                                 ).then_inc(g_loaded[s], 16)

                for s in range(2):
                    sp.dma_start(v_raw[:, s], V[s]).then_inc(v_loaded[s], 16)
                    sp.dma_start(g_ring[:, s], g_dram[l][:, :, s].rearrange("c j x -> j c x")
                                 ).then_inc(g_loaded[s], 16)
                with sp.Fori(0, UV - 1) as i:
                    for q in range(4):
                        u_load(i, q)
                        v_load(i, q)
                        if q % 2:
                            g_load(i, q // 2)
                for q in range(4):
                    if q < 2:
                        u_load(UV - 1, q)
                    v_load(UV - 1, q)
                    if q % 2:
                        g_load(UV - 1, q // 2)
                with sp.Fori(UV, 15) as i:
                    for q in range(4):
                        v_load(i, q)
                        if q % 2:
                            g_load(i, q // 2)
                for q in range(2):
                    v_load(15, q)

        @block.gpsimd
        def _(pool):
            pool.dma_start(cst[:], t_in["constants"]).then_inc(cst_loaded, 16)

            def gain_load(k):
                if k >= 2:
                    sm, v = {"mix0": (u_ready, 3), "head": (y_ready, 12), "mem0": (mu_ready, 2), "xn0": (u_ready, 6),
                             "fn0": (u_ready, 9), "mix1": (u_ready, 12), "spool": (pooled, 12),
                             "mem1": (mu_ready, 4), "xn1": (u_ready, 15)}[GAINS[k - 2]]
                    pool.wait_ge(sm, v)
                pool.dma_start(gain[:, k % 2], t_in["gains"][k].partition_broadcast(P)).then_inc(gain_loaded[k % 2], 16)

            gain_load(0)
            gain_load(1)
            pool.dma_start(wg, t_in["w_gates"]).then_inc(mix_loaded, 16)
            pool.dma_start(b4[0:4, :], t_in["b_gates"]).then_inc(mix_loaded, 16)
            pool.wait_ge(init_done, 1)
            pool.dma_start(m0c[:, 2, :], t_in["state_m"].partition_broadcast(P)).then_inc(mix_loaded, 16)
            pool.dma_start(C_aug, t_in["state_Cn"].rearrange("(b p) e -> p b e", p=P)).then_inc(mix_loaded, 16)
            gain_load(2)
            pool.wait_ge(d_emptied, DJ["state"] + 16)
            for buf, out in ((C_new, "Cn_p"), (C_aug, "Cn_s")):
                pool.dma_start(t_out[out].rearrange("(b p) e -> p b e", p=P), buf).then_inc(state_stored, 16)
            pool.dma_start(t_out["m_p"], selev[0:1, H:2 * H]).then_inc(state_stored, 16)
            pool.dma_start(t_out["m_s"], selev[0:1, 3 * H:4 * H]).then_inc(state_stored, 16)
            gain_load(3)
            for l in range(2):
                if l == 0:
                    pool.wait_ge(state_stored, 64)
                    pool.wait_ge(d_filled, DJ["yT"] + 6)
                else:
                    pool.wait_ge(acc_emptied, 4)
                    pool.dma_start(wpool, t_in["w_pool"]).then_inc(pool_loaded, 16)
                    pool.dma_start(arena[:, 2048:4352], t_in["bands"]).then_inc(pool_loaded, 16)
                    pool.wait_ge(prefix_clear, 1)
                    pool.dma_start(u[NS:NS + POOLST, 2, :], t_in["state_pool"]).then_inc(prefix_loaded, 16)
                pool.dma_start(memx, t_in["mem_prompt"].rearrange("(b p) d -> p b d", p=P)).then_inc(mem_loaded, 16)
                pool.dma_start(skT, t_in["cache_kT"][l].rearrange("(b p) m -> p b m", p=P)).then_inc(cache_loaded, 16)
                pool.dma_start(sv_, t_in["cache_v"][l].rearrange("(b p) d -> p b d", p=P)).then_inc(cache_loaded, 16)
                if l == 1:
                    pool.wait_ge(u_ready, 12)
                    pool.dma_start(t_out["pool_p"], u[P - POOLST:P, 1, :]).then_inc(pool_stored, 16)
                    pool.dma_start(t_out["pool_s"], u[NS - POOLST:NS, 2, :]).then_inc(pool_stored, 16)
                    gain_load(7)
                    gain_load(8)
                    gain_load(9)
                else:
                    gain_load(4)
                pool.wait_ge(d_emptied, DJ[f"memk{l}"] + 4)
                pool.dma_start(t_out["mem_k"][l].rearrange("(b p) d -> p b d", p=P), mk).then_inc(mem_stored, 16)
                pool.wait_ge(d_emptied, DJ[f"memv{l}"] + 4)
                pool.dma_start(t_out["mem_v"][l].rearrange("(b p) d -> p b d", p=P), mv_).then_inc(mem_stored, 16)
                pool.wait_ge(d_filled, DJ[f"sc{l}"] + 12)
                pool.dma_start(keysT, t_in["peer_keys"][l]).then_inc(keys_loaded, 16)
                if l == 0:
                    gain_load(5)
                    gain_load(6)
                else:
                    gain_load(10)
                with pool.Fori(0, NGC // 2) as i:
                    for s in range(2):
                        pool.wait_ge(a_emptied, i * 20 + (AJ[f"gb{l}"] + 10 * s + 10))
                        pool.dma_start(g_dram[l][i * 2 + s], g_stage[:, s].rearrange("p (a b) t -> p a (b t)", b=4)
                                       ).then_inc(g_stored[s], 16)
            for t, (off, rows) in enumerate(TILES):
                pool.wait_ge(u_ready, 18 + t + 1)
                dst = t_out["y_p"][off:off + rows] if t < 2 else t_out["y_s"]
                pool.dma_start(dst, u[0:rows, t, :]).then_inc(y_stored, 16)
            pool.wait_ge(y_stored, 48)
            pool.wait_ge(mem_stored, 64)
            pool.wait_ge(pool_stored, 32)
            pool.wait_ge(state_stored, 64)

        @block.tensor
        def _(pe):
            def d_bank(n, i=None, per=0):
                if i is None:
                    if n >= 4:
                        pe.wait_ge(d_emptied, n - 3)
                else:
                    assert per % 4 == 0 and n >= 4
                    pe.wait_ge(d_emptied, i * per + (n - 3))
                return psum[:, DBANKS[n % 4], :]

            def a_bank(n, i=None, per=0):
                if i is None:
                    if n >= 4:
                        pe.wait_ge(a_emptied, n - 3)
                else:
                    assert per % 4 == 0 and n >= 4
                    pe.wait_ge(a_emptied, i * per + (n - 3))
                return psum[:, ABANKS[n % 4], :]

            def w_wait(stage, local, i=None):
                c = WC[stage] + local
                if i is None:
                    pe.wait_ge(w_loaded[c % 2], 16 * (c // 2 + 1))
                else:
                    pe.wait_ge(w_loaded[c % 2], i * 16 + 16 * (c // 2 + 1))
                return W[c % 2]

            def transposes(stage, src, tiles, n_ready, ready, first=0):
                n = DJ[stage]
                for t, (off, rows) in enumerate(tiles):
                    pe.wait_ge(ready, n_ready + t + 1)
                    for q in range(2):
                        bank = d_bank(n)
                        for b in range(4):
                            last = pe.transpose(bank[:, b * P:b * P + rows], src(t, rows, 4 * q + b), ident[0:rows, 0:rows])
                        last.then_inc(d_filled, 1)
                        n += 1

            def u_transposes(stage, norm):
                transposes(stage, lambda t, rows, b: u[0:rows, t, b * P:(b + 1) * P], TILES, 3 * norm, u_ready)

            def feature_major(stage, wstage, n_chunks, stage_first=0):
                def pair(i):
                    for s in range(2):
                        w = w_wait(wstage, s, i)
                        for m in range(4):
                            bank = d_bank(DJ[stage] + 4 * s + m, i, 8)
                            for k in range(KD):
                                last = pe.matmul(bank[:, 0:TOK], w[:, k, m * P:(m + 1) * P], uT[:, k, :],
                                                 start=k == 0, stop=k == KD - 1)
                            last.then_inc(d_filled, 1)
                if n_chunks == 2:
                    pair(None)
                else:
                    with pe.Fori(0, n_chunks // 2) as i:
                        pair(i)

            def token_major(stage, wstage, local, srcT, tiles, bank_of=d_bank, filled=d_filled, jobs=DJ, base=0):
                w = w_wait(wstage, local)
                for t, (off, rows) in enumerate(tiles):
                    bank = bank_of(jobs[stage] + base + t)
                    for k in range(KD):
                        last = pe.matmul(bank[0:rows, :], srcT[:, k, off:off + rows], w[:, k, :],
                                         start=k == 0, stop=k == KD - 1)
                    last.then_inc(filled, 1)

            pe.wait_ge(cst_loaded, 16)
            u_transposes("mixn0", 0)
            pe.wait_ge(d_emptied, DJ["mixn0"] + 6)
            feature_major("qk", "qk", 4)
            for c in range(2):
                token_major("v", "vo", c, uT, TILES, base=3 * c)
            for c in range(2):
                token_major("o", "vo", 2 + c, uT, TILES, a_bank, a_filled, AJ, 3 * c)
            pe.wait_ge(mix_loaded, 64)
            for g in range(2):
                bank = d_bank(DJ["gates"] + g)
                for k in range(KD):
                    last = pe.matmul(bank[0:H, 0:TOK], wg[:, k, H * g:H * g + H], uT[:, k, :], start=k == 0, stop=k == KD - 1)
                last.then_inc(d_filled, 1)
            pe.wait_ge(gate_rows, 1)
            bank = d_bank(DJ["cols"])
            for t, (off, rows) in enumerate(TILES):
                for a in range(2):
                    last = pe.transpose(bank[0:rows, t * 8 + a * H:t * 8 + a * H + H], R4[0:H, 4 + a, off:off + rows], ident[0:H, 0:H])
            last.then_inc(d_filled, 1)
            for h in range(H):
                bank = d_bank(DJ["rb"] + h)
                pe.matmul(bank[:, 0:TOK], sel4[0:H, h, :], R4[0:H, 5, :], start=True, stop=True).then_inc(d_filled, 1)
            pe.wait_ge(m_ready, 1)
            bank = d_bank(DJ["sel"])
            pe.matmul(bank[:, 0:8], last_p, bm[:, 1, :], start=True, stop=True)
            pe.matmul(bank[:, 8:16], last_s[0:NS, :], bm[0:NS, 2, :], start=True, stop=True).then_inc(d_filled, 1)
            keys = ((0, 128), (0, 256), (256, 64))
            for h in range(H):
                for t, (off, rows) in enumerate(TILES):
                    bank = d_bank(DJ["qkt"] + 3 * h + t)
                    k0, kn = keys[t]
                    for d in range(2):
                        last = pe.matmul(bank[0:rows, 0:kn], qT[:, 2 * h + d, off:off + rows], kT[:, 2 * h + d, k0:k0 + kn],
                                         start=d == 0, stop=d == 1)
                    last.then_inc(d_filled, 1)
            n = DJ["ktok"]
            for t, (off, rows) in enumerate(TILES):
                for q in range(2):
                    bank = d_bank(n)
                    for b in range(4):
                        last = pe.transpose(bank[0:rows, b * P:(b + 1) * P], kT[:, 4 * q + b, off:off + rows], ident)
                    last.then_inc(d_filled, 1)
                    n += 1

            def mix_job(h, k):
                return DJ["mix"] + (5 * h + (0 if k == 0 else k + (1 if h < H - 1 else 0)) if k == 0 or h < H - 1
                                    else 5 * h + k)

            def mix_order():
                n = DJ["mix"]
                for h in range(H + 1):
                    if h < H:
                        yield n, h, 0
                        n += 1
                    if h >= 1:
                        for k in range(1, 5):
                            yield n, h - 1, k
                            n += 1

            pe.wait_ge(d_emptied, DJ["qkt"] + 12)
            swT_job = {}
            for n, h, k in mix_order():
                bank = d_bank(n)
                sT = swT[:, h % 2, :]
                if k == 0:
                    swT_job[h] = n
                    for dst, t, src in ((0, 0, 0), (128, 1, 128), (256, 1, 256)):
                        last = pe.transpose(bank[:, dst:dst + P], wts[:, h, src:src + P], ident)
                    last = pe.transpose(bank[0:NS, 384:448], wts[0:NS, h, 384:448], ident[0:NS, 0:NS])
                elif k == 1:
                    pe.wait_ge(d_emptied, swT_job[h] + 1)
                    last = pe.matmul(bank[:, 0:VA], sT[:, 0:P], v_aug[:, 0, h, :], start=True, stop=True)
                elif k == 2:
                    pe.matmul(bank[:, 0:VA], sT[:, P:2 * P], v_aug[:, 0, h, :], start=True, stop=False)
                    last = pe.matmul(bank[:, 0:VA], sT[:, 2 * P:3 * P], v_aug[:, 1, h, :], start=False, stop=True)
                elif k == 3:
                    for d in range(2):
                        last = pe.matmul(bank[0:NS, 0:VA], qT[:, 2 * h + d, NP_:TOK], C_aug[:, 2 * h + d, :],
                                         start=d == 0, stop=d == 1)
                else:
                    last = pe.matmul(bank[0:NS, 0:VA], sT[0:NS, 384:448], v_aug[0:NS, 2, h, :], start=True, stop=True)
                last.then_inc(d_filled, 1)
            for b in range(KD):
                bank = d_bank(DJ["state"] + b)
                for t in range(2):
                    last = pe.matmul(bank[:, 0:VA], kw[:, t, b * P:(b + 1) * P], v_aug[:, t, b // 2, :], start=t == 0, stop=t == 1)
                last.then_inc(d_filled, 1)
            for b in range(KD):
                bank = d_bank(DJ["state"] + KD + b)
                pe.matmul(bank[:, 0:VA], kw[0:NS, 2, b * P:(b + 1) * P], v_aug[0:NS, 2, b // 2, :], start=True, stop=True
                          ).then_inc(d_filled, 1)
            n = DJ["yT"]
            for t, (off, rows) in enumerate(TILES):
                pe.wait_ge(y_ready, 4 * (t + 1))
                for q in range(2):
                    bank = d_bank(n)
                    for b in range(4):
                        h, c = (4 * q + b) // 2, b % 2
                        last = pe.transpose(bank[:, b * P:b * P + rows], hn[0:rows, t, h, c * P:(c + 1) * P], ident[0:rows, 0:rows])
                    last.then_inc(d_filled, 1)
                    n += 1
            pe.wait_ge(d_emptied, DJ["yT"] + 6)
            for c in range(2):
                token_major("out", "out", c, uT, TILES, base=3 * c)

            def memory(l):
                mt = ((0, P), (P, P))
                transposes(f"memT{l}", lambda t, rows, b: u[0:rows, t, b * P:(b + 1) * P], mt, 2 * l, mu_ready)
                pe.wait_ge(d_emptied, DJ[f"memT{l}"] + 4)
                for c in range(2):
                    token_major(f"memk{l}", f"memk{l}", c, memT, mt, base=2 * c)
                for c in range(2):
                    token_major(f"memv{l}", f"memv{l}", c, memT, mt, base=2 * c)
                pe.wait_ge(d_emptied, DJ[f"memk{l}"] + 4)
                for j in range(4):
                    bank = d_bank(DJ[f"memkT{l}"] + j)
                    for b in range(2):
                        for t in range(2):
                            last = pe.transpose(bank[:, b * MEM + t * P:b * MEM + (t + 1) * P],
                                                mk[:, t, (2 * j + b) * P:(2 * j + b + 1) * P], ident)
                    last.then_inc(d_filled, 1)

            def attend(l, norm):
                u_transposes(f"xn{l}", norm)
                pe.wait_ge(d_emptied, DJ[f"xn{l}"] + 6)
                feature_major(f"xq{l}", f"xq{l}", 2)
                pe.wait_ge(cache_loaded, 32 * (l + 1))
                for h in range(H):
                    pe.wait_ge(d_emptied, DJ[f"xq{l}"] + 2 * h + 2)
                    for t, (off, rows) in enumerate(TILES):
                        bank = d_bank(DJ[f"sc{l}"] + 3 * h + t)
                        kk = mkT if t < 2 else skT
                        for d in range(2):
                            last = pe.matmul(bank[0:rows, 0:MEM], qT[:, 2 * h + d, off:off + rows], kk[:, 2 * h + d, :],
                                             start=d == 0, stop=d == 1)
                        last.then_inc(d_filled, 1)
                for n, h, k in av_order(l):
                    bank = d_bank(n)
                    if k < 2:
                        pe.wait_ge(p_ready, 12 * l + 3 * h + 3)
                        for t, (off, rows) in enumerate(TILES):
                            last = pe.transpose(bank[:, off:off + rows], probs[0:rows, 3 * h + t, k * P:(k + 1) * P],
                                                ident[0:rows, 0:rows])
                    else:
                        pe.wait_ge(d_emptied, av_pt_done(l, h))
                        c0 = (2 * h + k - 2) * P
                        for vv, a, z in ((mv_, 0, NP_), (sv_, NP_, TOK)):
                            for m in range(2):
                                last = pe.matmul(bank[:, a:z], vv[:, m, c0:c0 + P], probsT[:, h % 2, m, a:z],
                                                 start=m == 0, stop=m == 1)
                    last.then_inc(d_filled, 1)
                pe.wait_ge(d_emptied, DJ[f"av{l}"] + 16)
                for c in range(2):
                    token_major(f"xo{l}", f"xo{l}", c, uT, TILES, base=3 * c)

            def u_block(slot, b, bank):
                for k in range(KD):
                    last = pe.matmul(bank[:, 0:TOK], Ublk[slot][:, b, k, :], uT[:, k, :], start=k == 0, stop=k == KD - 1)
                last.then_inc(a_filled, 1)

            def v_block(l, i, r, last_block=False):
                pe.wait_ge(p_split, i * 8 + (NB * l + r + 1))
                pe.wait_ge(v_split, i * 8 + (NB * l + r + 1))
                ph, vh = phl[:, r % 2], vhl[:, r % 2]
                for t in range(2):
                    hi, lo = ph[:, t * P:(t + 1) * P], ph[:, TOK + NS + t * P:TOK + NS + (t + 1) * P]
                    for lhs, part in ((hi, 0), (hi, 1), (lo, 0)):
                        for n in range(2):
                            pe.matmul(psum[:, 2 + 2 * t + n, :], lhs, vh[:, part, n * 512:(n + 1) * 512],
                                      start=False, stop=False, skip_group_check=True)
                for part in range(2):
                    for n in range(2):
                        last = pe.matmul(psum[:, 6 + n, :], ph[:, NP_:NP_ + P], vh[:, part, n * 512:(n + 1) * 512],
                                         start=False, stop=False, skip_group_check=True)
                last.then_inc(v_summed, 1)

            def peer(l, norm):
                u_transposes(f"fn{l}", norm)
                pe.wait_ge(d_emptied, DJ[f"fn{l}"] + 6)
                pe.wait_ge(keys_loaded, 16 * (l + 1))
                with pe.Fori(0, 2) as i:
                    for kind, m in PQ_ORDER:
                        if kind == "q":
                            w = w_wait(f"pq{l}", m // 4, i) if m % 4 == 0 else W[(WC[f"pq{l}"] + m // 4) % 2]
                            bank = a_bank(AJ[f"pq{l}"] + m, i, 8)
                            for k in range(KD):
                                last = pe.matmul(bank[:, 0:TOK], w[:, k, (m % 4) * P:(m % 4 + 1) * P], uT[:, k, :],
                                                 start=k == 0, stop=k == KD - 1)
                            last.then_inc(a_filled, 1)
                        else:
                            pe.wait_ge(a_emptied, i * 8 + (AJ[f"pq{l}"] + m + 1))
                            bank = d_bank(DJ[f"pq{l}"] + m, i, 8)
                            for t, (off, rows) in enumerate(TILES):
                                last = pe.matmul(bank[0:rows, t * P:(t + 1) * P], pqT[:, m, off:off + rows],
                                                 keysT[:, i * 8 + m, :], start=True, stop=True)
                            last.then_inc(d_filled, 1)
                pe.wait_ge(a_emptied, AJ[f"up{l}"])
                wl = 16 * (WC[f"U{l}"] // 2 + 1)
                with pe.Fori(0, AHEAD // 4) as i:
                    for r in range(4):
                        if r % 2 == 0:
                            pe.wait_ge(w_loaded[r // 2], i * 16 + wl)
                        u_block(r // 2, r % 2, a_bank(AJ[f"up{l}"] + r, i, 4))
                for t, (off, rows) in enumerate(TILES):
                    pe.wait_ge(picked_ready, 3 * l + t + 1)
                    bank = d_bank(DJ[f"slot{l}"] + t)
                    for a in range(3):
                        last = pe.transpose(bank[:, a * P:a * P + rows], picked[0:rows, t, a, :], ident[0:rows, 0:rows])
                    last.then_inc(d_filled, 1)
                with pe.Fori(0, 5) as i:
                    for r in range(4):
                        if r % 2 == 0:
                            pe.wait_ge(w_loaded[r // 2], i * 16 + (wl + 16 * (AHEAD // 4)))
                        u_block(r // 2, r % 2, a_bank(AJ[f"gb{l}"] + 5 * r, i, 20))
                        for g in range(4):
                            bank = a_bank(AJ[f"gb{l}"] + 5 * r + 1 + g, i, 20)
                            pe.wait_ge(oh_ready, i * 64 + (TOK * l + 16 * r + 4 * g + 4))
                            for q in range(4):
                                s = (4 * g + q) % 8
                                last = pe.matmul(bank[:, q * P:(q + 1) * P], ohJ[:, s, :], oh[:, s, :], start=True, stop=True)
                            last.then_inc(a_filled, 1)
                pe.wait_ge(zero_ready, l + 1)
                pe.wait_ge(a_emptied, AJ[f"uv{l}"])
                pe.wait_ge(d_emptied, DJ[f"slot{l}"] + 3)
                for n in range(6):
                    last = pe.matmul(psum[:, 2 + n, :], phl[:, 0, 0:P], vhl[:, 0, 0, 0:512], start=True, stop=False,
                                     skip_group_check=True)
                last.then_inc(v_summed, 2)
                with pe.Fori(0, UV) as i:
                    for r in range(8):
                        if r % 2 == 0:
                            pe.wait_ge(w_loaded[(r // 2) % 2], i * 32 + (wl + 16 * (LAG // 4 + r // 4)))
                        pe.wait_ge(a_emptied, i * 8 + (AJ[f"uv{l}"] + r - 1))
                        u_block((r // 2) % 2, r % 2, psum[:, r % 2, :])
                        v_block(l, i, r)
                with pe.Fori(UV, 16) as i:
                    for r in range(8):
                        v_block(l, i, r)
                pe.wait_ge(acc_emptied, 4 * (l + 1))
                for n in range(2):
                    pe.wait_ge(acc_copied, 2 * l + n + 1)
                    pe.matmul(d_bank(DJ[f"fold{l}"] + n)[0:NS, :], fold, acc_tmp[:, n, :], start=True, stop=True
                              ).then_inc(d_filled, 1)

            memory(0)
            attend(0, 1)
            peer(0, 2)
            pe.wait_ge(pool_loaded, 32)
            pe.wait_ge(prefix_loaded, 16)
            pe.wait_ge(u_ready, 12)
            for b in range(KD):
                bank = d_bank(DJ["pool"] + b)
                for s in range(2):
                    pe.matmul(bank[:, 0:NP_], u[:, s, b * P:(b + 1) * P], bandp[:, b // 2, s, :], start=s == 0, stop=s == 1)
                pe.matmul(bank[:, NP_:TOK], u[:, 2, b * P:(b + 1) * P], bands_[:, b // 2, :], start=True, stop=True
                          ).then_inc(d_filled, 1)
            for g in range(4):
                pe.wait_ge(d_emptied, DJ["pool"] + 2 * g + 2)
                for t, (off, rows) in enumerate(TILES):
                    bank = d_bank(DJ["pool"] + KD + 3 * g + t)
                    for c in range(2):
                        last = pe.matmul(bank[0:rows, 0:DH], plT[:, 2 * g + c, off:off + rows], wpool[:, g, c, :],
                                         start=c == 0, stop=c == 1)
                    last.then_inc(d_filled, 1)
            memory(1)
            attend(1, 4)
            peer(1, 5)

        @block.scalar
        def _(act):
            step = Chain(act, act_step)

            def norm_stats(norm, index, extra=()):
                for sm, v in extra:
                    act.wait_ge(sm, v)
                for t, (off, rows) in enumerate(TILES):
                    sm, v = x_ready(norm, t)
                    act.wait_ge(sm, v)
                    step(act.activation(u[0:rows, t, :], x[0:rows, t, :], ACT.Square, accum_out=ss[0:rows, t:t + 1]))
                    act.activation(std[0:rows, t:t + 1], ss[0:rows, t:t + 1], ACT.Sqrt, bias=eps_c[0:rows, :], scale=1.0 / D
                                   ).then_inc(std_ready, 1)

            def mem_stats(l):
                if l == 0:
                    act.wait_ge(y_ready, 12)
                else:
                    act.wait_ge(d_filled, DJ["pool"] + 8)
                    act.wait_ge(pool_stored, 32)
                act.wait_ge(mem_loaded, 16 * (l + 1))
                for t in range(2):
                    step(act.activation(u[:, t, :], memx[:, t, :], ACT.Square, accum_out=mss[:, t:t + 1]))
                    act.activation(mstd[:, t:t + 1], mss[:, t:t + 1], ACT.Sqrt, bias=eps_c, scale=1.0 / D
                                   ).then_inc(mstd_ready, 1)

            act.wait_ge(init_done, 1)
            norm_stats("mix0", 0)
            for c in range(2):
                for t, (off, rows) in enumerate(TILES):
                    n = AJ["o"] + 3 * c + t
                    act.wait_ge(a_filled, n + 1)
                    act.activation(u[0:rows, t, c * 512:(c + 1) * 512], psum[0:rows, ABANKS[n % 4], :], ACT.Sigmoid
                                   ).then_inc(a_emptied, 1)
            act.wait_ge(gate_abs, 1)
            step(act.activation(R4[0:H, 2, :], R4[0:H, 2, :], ACT.Exp, scale=-1.0))
            act.activation(R4[0:H, 2, :], R4[0:H, 2, :], ACT.Ln, bias=one_c[0:H, :]).then_inc(gate_ln, 1)
            act.wait_ge(m_ready, 1)
            for h in range(H):
                for t, (off, rows) in enumerate(TILES):
                    a, z = ((0, 128), (128, 384), (384, 448))[t]
                    act.activation(wts[0:rows, h, a:z], wts[0:rows, h, a:z], ACT.Exp, bias=negm[0:rows, t, h:h + 1]
                                   ).then_inc(w_ready, 1)
                if h == 0:
                    act.activation(ainter, idiff, ACT.Exp).then_inc(mexp_ready, 1)
                    act.activation(emneg, negm, ACT.Exp).then_inc(mexp_ready, 1)
                    act.wait_ge(ws_arg, 1)
                    act.activation(wscol, wsarg, ACT.Exp).then_inc(ws_ready, 1)
                    act.activation(gstate, garg, ACT.Exp).then_inc(ws_ready, 1)
            act.wait_ge(var_ready, 1)
            act.activation(sdev, mv[:, :, :, 1], ACT.Sqrt, bias=eps_c).then_inc(sdev_ready, 1)

            def attend(l):
                for j in range(3 * H):
                    rows = TILES[j % 3][1]
                    act.wait_ge(mx_ready, 12 * l + j + 1)
                    act.activation(probs[0:rows, j, :], probs[0:rows, j, :], ACT.Exp, bias=nmx[0:rows, j:j + 1],
                                   accum_out=rsum[0:rows, j:j + 1]).then_inc(p_exp, 1)

            def peer(l):
                with act.Fori(0, 2) as i:
                    for m in range(8):
                        n = AJ[f"pq{l}"] + m
                        act.wait_ge(a_filled, i * 8 + (n + 1))
                        act.activation(pqT[:, m, :], psum[:, ABANKS[n % 4], 0:TOK], ACT.Copy).then_inc(a_emptied, 1)
                act.wait_ge(mem_stored, 32 * (l + 1))
                with act.Fori(0, AHEAD // 4) as i:
                    for r in range(4):
                        n = AJ[f"up{l}"] + r
                        act.wait_ge(a_filled, i * 4 + (n + 1))
                        act.activation(act4[:, i, r, :], psum[:, ABANKS[n % 4], 0:TOK], ACT.Gelu).then_inc(a_emptied, 1)
                for t, (off, rows) in enumerate(TILES):
                    act.wait_ge(top_ready, 3 * l + t + 1)
                    act.activation(picked[0:rows, t, 2, :], picked[0:rows, t, 2, :], ACT.Exp).then_inc(exp_ready, 1)
                def spread(i, first=False):
                    for r in range(4):
                        n = AJ[f"gb{l}"] + 5 * r
                        act.wait_ge(a_filled, i * 20 + (n + 1))
                        act.activation(act4[:, i + AHEAD // 4, r, :], psum[:, ABANKS[n % 4], 0:TOK], ACT.Gelu
                                       ).then_inc(a_emptied, 1)
                        if r % 2 == 0 and not first:
                            act.wait_ge(g_stored[r // 2], i * 16 + 16 * (NGC // 2) * l)
                        for g in range(4):
                            n += 1
                            act.wait_ge(a_filled, i * 20 + (n + 1))
                            t0 = 16 * (r % 2) + 4 * g
                            act.activation(g_stage[:, r // 2, :, t0:t0 + 4].rearrange("p i t -> p t i"),
                                           psum[:, ABANKS[n % 4], :].rearrange("p (t i) -> p t i", i=NK), ACT.Copy
                                           ).then_inc(a_emptied, 1)

                spread(0, first=l == 0)
                with act.Fori(1, NGC // 2) as i:
                    spread(i)

                def vhi(i, r):
                    if r % 2 == 0:
                        act.wait_ge(v_loaded[(r // 2) % 2], i * 32 + 16 * (32 * l + r // 4 + 1))
                    act.wait_ge(v_summed, i * 8 + ((NB + 2) * l + r + 1))
                    act.activation(vhl[:, r % 2, 0, :], v_raw[:, (r // 2) % 2, r % 2, :], ACT.Copy).then_inc(vhi_ready, 1)

                with act.Fori(0, UV) as i:
                    for r in range(8):
                        vhi(i, r)
                        act.wait_ge(a_filled, i * 8 + (AJ[f"uv{l}"] + r + 1))
                        act.wait_ge(p_split, i * 8 + (NB * l + r + 1))
                        act.activation(act8[:, i % (LAG // 8), r, :], psum[:, r % 2, 0:TOK], ACT.Gelu).then_inc(a_emptied, 1)
                with act.Fori(UV, 16) as i:
                    for r in range(8):
                        vhi(i, r)

            mem_stats(0)
            norm_stats("xn0", 1, extra=((d_filled, DJ["memT0"] + 4),))
            attend(0)
            norm_stats("fn0", 2)
            peer(0)
            norm_stats("mix1", 3)
            mem_stats(1)
            norm_stats("xn1", 4, extra=((d_filled, DJ["memT1"] + 4),))
            attend(1)
            norm_stats("fn1", 5)
            peer(1)
            norm_stats("final", 6)

        @block.vector
        def _(dve):
            step = Chain(dve, dve_step)
            row_step = Chain(dve, dve_row_step)

            def full(n, i=None, per=0):
                dve.wait_ge(d_filled, n + 1 if i is None else i * per + (n + 1))
                return psum[:, DBANKS[n % 4], :]

            def scale_rows(norm, index, gidx):
                dve.wait_ge(gain_loaded[gidx % 2], 16 * (gidx // 2 + 1))
                for t, (off, rows) in enumerate(TILES):
                    dve.wait_ge(std_ready, 3 * index + t + 1)
                    step(dve.reciprocal(rstd[0:rows, t:t + 1], std[0:rows, t:t + 1]))
                    dve.scalar_tensor_tensor(out=u[0:rows, t, :], in0=x[0:rows, t, :], scalar=rstd[0:rows, t:t + 1],
                                             in1=gain[0:rows, gidx % 2, :], op0=ALU.mult, op1=ALU.mult).then_inc(u_ready, 1)

            def empty_transposes(stage, dstT, tiles):
                n = DJ[stage]
                for t, (off, rows) in enumerate(tiles):
                    for q in range(2):
                        bank = full(n).rearrange("p (b c) -> p b c", c=P)
                        dve.tensor_copy(dstT[:, 4 * q:4 * q + 4, off:off + rows], bank[:, :, 0:rows]).then_inc(d_emptied, 1)
                        n += 1

            def add_to_x(stage):
                for c in range(2):
                    for t, (off, rows) in enumerate(TILES):
                        dst = x[0:rows, t, c * 512:(c + 1) * 512]
                        dve.tensor_tensor(dst, full(DJ[stage] + 3 * c + t)[0:rows, :], dst, ALU.add).then_inc(d_emptied, 1)

            step(dve.memset(small[:], 1.0))
            step(dve.memset(eps_c, EPS))
            step(dve.memset(arena[:, 23152:23472], 0.0))
            step(dve.memset(hn[:, 2], 1.0))
            step(dve.memset(v_aug[:, :, :, DH:VA], 1.0))
            dve.memset(mv, 1.0).then_inc(init_done, 1)
            dve.wait_ge(init_done, 1)
            dve.wait_ge(x_loaded, 48)
            scale_rows("mix0", 0, 0)
            empty_transposes("mixn0", uT, TILES)
            with dve.Fori(0, 2) as i:
                for m in range(8):
                    bank = full(DJ["qk"] + m, i, 8)
                    dve.tensor_copy(view(arena, 0, 2, KD, TOK)[:, i, m, :], bank[:, 0:TOK]).then_inc(d_emptied, 1)
            for c in range(2):
                for t, (off, rows) in enumerate(TILES):
                    bank = full(DJ["v"] + 3 * c + t)
                    dve.tensor_copy(v_aug[0:rows, t, 2 * c:2 * c + 2, 0:DH], bank[0:rows, :].rearrange("p (h e) -> p h e", e=DH)
                                    ).then_inc(d_emptied, 1)
            dve.wait_ge(mix_loaded, 64)
            for g in range(2):
                dve.tensor_scalar(R4[0:H, g, :], full(DJ["gates"] + g)[0:H, 0:TOK], b4[0:H, g:g + 1], None, ALU.add
                                  ).then_inc(d_emptied, 1)
            dve.wait_ge(d_emptied, DJ["gates"] + 2)
            dve.scalar_tensor_tensor(out=R4[0:H, 2, :], in0=R4[0:H, 1, :], scalar=-1.0, in1=R4[0:H, 1, :], op0=ALU.mult, op1=ALU.max
                                     ).then_inc(gate_abs, 1)
            step(dve.tensor_scalar(R4[0:H, 3, :], R4[0:H, 1, :], 0.0, None, ALU.min))
            dve.wait_ge(gate_ln, 1)
            step(dve.tensor_tensor(R4[0:H, 3, :], R4[0:H, 3, :], R4[0:H, 2, :], ALU.subtract))
            step(dve.memset(R4[0:H, 2, :], 1.0))
            for a, z in ((0, NP_), (NP_, TOK)):
                step(dve.tensor_tensor_scan(out=R4[0:H, 4, a:z], data0=R4[0:H, 2, a:z], data1=R4[0:H, 3, a:z], initial=0.0,
                                            op0=ALU.mult, op1=ALU.add))
            dve.tensor_tensor(R4[0:H, 5, :], R4[0:H, 0, :], R4[0:H, 4, :], ALU.subtract).then_inc(gate_rows, 1)
            bank = full(DJ["cols"])
            step(dve.tensor_copy(br[:, 0:2, :], bank[:, 0:16].rearrange("p (t c) -> p t c", c=8)))
            dve.tensor_copy(br[0:NS, 2, :], bank[0:NS, 16:24]).then_inc(d_emptied, 1)
            dve.wait_ge(d_emptied, DJ["cols"] + 1)
            for h in range(H):
                bank = full(DJ["rb"] + h)
                b0, b1, b2 = br[:, 0, h:h + 1], br[:, 1, h:h + 1], br[0:NS, 2, h:h + 1]
                dve.scalar_tensor_tensor(out=wts[:, h, 0:128], in0=bank[:, 0:128], scalar=b0, in1=tri_m, op0=ALU.add, op1=ALU.add)
                dve.tensor_scalar(wts[:, h, 128:256], bank[:, 0:128], b1, None, ALU.add)
                dve.scalar_tensor_tensor(out=wts[:, h, 256:384], in0=bank[:, 128:256], scalar=b1, in1=tri_m, op0=ALU.add, op1=ALU.add)
                dve.scalar_tensor_tensor(out=wts[0:NS, h, 384:448], in0=bank[0:NS, NP_:TOK], scalar=b2, in1=tri_m[0:NS, 0:NS],
                                         op0=ALU.add, op1=ALU.add).then_inc(d_emptied, 1)
            dve.wait_ge(d_emptied, DJ["rb"] + H)
            for h in range(H):
                for t, (off, rows) in enumerate(TILES):
                    a, z = ((0, 128), (128, 384), (384, 448))[t]
                    ins = dve.tensor_reduce(rmax[0:rows, t, h:h + 1], wts[0:rows, h, a:z], AX.X, ALU.max)
            step(ins)
            step(dve.tensor_tensor(inter, br[:, :, 0:H], m0c, ALU.add))
            step(dve.tensor_copy(bm[:, :, 0:H], br[:, :, 0:H]))
            step(dve.tensor_tensor(bm[:, :, H:2 * H], rmax, inter, ALU.max))
            step(dve.tensor_tensor(idiff, inter, bm[:, :, H:2 * H], ALU.subtract))
            dve.tensor_scalar(negm, bm[:, :, H:2 * H], -1.0, None, ALU.mult).then_inc(m_ready, 1)
            bank = full(DJ["sel"])
            dve.tensor_copy(selev, bank[:, 0:16]).then_inc(d_emptied, 1)
            dve.wait_ge(d_emptied, DJ["sel"] + 1)
            se = selev.rearrange("p (g a h) -> p g a h", g=2, a=2)
            step(dve.tensor_tensor(blm, se[:, :, 0, :], se[:, :, 1, :], ALU.subtract))
            step(dve.tensor_tensor(wsarg[:, 0:2, :], br[:, 0:2, H:2 * H], blm[:, 0:1, :].to_broadcast([P, 2, H]), ALU.add))
            step(dve.tensor_tensor(wsarg[:, 2, :], br[:, 2, H:2 * H], blm[:, 1, :], ALU.add))
            dve.tensor_tensor(garg, blm[:, 1, :], m0c[:, 2, :], ALU.add).then_inc(ws_arg, 1)
            for h in range(H):
                for t, (off, rows) in enumerate(TILES):
                    a, z = ((0, 128), (128, 384), (384, 448))[t]
                    bank = full(DJ["qkt"] + 3 * h + t)
                    dve.wait_ge(w_ready, 3 * h + t + 1)
                    dve.scalar_tensor_tensor(out=wts[0:rows, h, a:z], in0=bank[0:rows, 0:z - a], scalar=DH ** -0.5,
                                             in1=wts[0:rows, h, a:z], op0=ALU.mult, op1=ALU.mult).then_inc(d_emptied, 1)
            n = DJ["ktok"]
            dve.wait_ge(ws_ready, 2)
            for t, (off, rows) in enumerate(TILES):
                for q in range(2):
                    bank = full(n)
                    for hh in range(2):
                        h = 2 * q + hh
                        ins = dve.tensor_scalar(kw[0:rows, t, h * DH:(h + 1) * DH], bank[0:rows, hh * DH:(hh + 1) * DH],
                                                wscol[0:rows, t, h:h + 1], DH ** -0.5, ALU.mult, ALU.mult)
                    ins.then_inc(d_emptied, 1)
                    n += 1
            dve.wait_ge(mexp_ready, 2)
            n = DJ["mix"]
            for hh in range(H + 1):
                if hh < H:
                    bank = full(n)
                    dve.tensor_copy(swT[:, hh % 2, 0:384], bank[:, 0:384])
                    dve.tensor_copy(swT[0:NS, hh % 2, 384:448], bank[0:NS, 384:448]).then_inc(d_emptied, 1)
                    n += 1
                if hh >= 1:
                    h = hh - 1
                    for t in range(2):
                        dve.tensor_copy(hn[:, t, h, :], full(n)[:, 0:VA]).then_inc(d_emptied, 1)
                        n += 1
                    dve.tensor_scalar(qc_tmp[0:NS, h % 2, :], full(n)[0:NS, 0:VA], ainter[0:NS, 2, h:h + 1], None, ALU.mult
                                      ).then_inc(d_emptied, 1)
                    n += 1
                    dve.wait_ge(d_emptied, n)
                    dve.tensor_tensor(hn[0:NS, 2, h, :], full(n)[0:NS, 0:VA], qc_tmp[0:NS, h % 2, :], ALU.add).then_inc(d_emptied, 1)
                    n += 1
            dve.wait_ge(d_emptied, n)
            step(dve.scalar_tensor_tensor(out=rinv, in0=hn[:, :, :, DH], scalar=-1.0, in1=hn[:, :, :, DH], op0=ALU.mult, op1=ALU.max))
            step(dve.tensor_tensor(rinv, rinv, emneg, ALU.max))
            step(dve.reciprocal(rinv, rinv))
            for t, (off, rows) in enumerate(TILES):
                for h in range(H):
                    ins = dve.tensor_scalar(hn[0:rows, t, h, 0:DH], hn[0:rows, t, h, 0:DH], rinv[0:rows, t, h:h + 1], None, ALU.mult)
            step(ins)
            for t, (off, rows) in enumerate(TILES):
                for h in range(H):
                    ins = dve.bn_stats(bnst[0:rows, 4 * t + h, :], hn[0:rows, t, h, 0:DH])
            step(ins)
            for t, (off, rows) in enumerate(TILES):
                for h in range(H):
                    ins = dve.bn_aggr(mv[0:rows, t, h, :], bnst[0:rows, 4 * t + h, :])
            ins.then_inc(var_ready, 1)
            for b in range(KD):
                dve.tensor_copy(C_new[:, b, :], full(DJ["state"] + b)[:, 0:VA]).then_inc(d_emptied, 1)
            for b in range(KD):
                dve.scalar_tensor_tensor(out=C_aug[:, b, :], in0=C_aug[:, b, :], scalar=gstate[:, b // 2:b // 2 + 1],
                                         in1=full(DJ["state"] + KD + b)[:, 0:VA], op0=ALU.mult, op1=ALU.add
                                         ).then_inc(d_emptied, 1)
            dve.wait_ge(sdev_ready, 1)
            step(dve.reciprocal(srec, sdev))
            dve.wait_ge(a_emptied, AJ["o"] + 6)
            dve.wait_ge(gain_loaded[1], 16)
            dve.wait_ge(var_ready, 1)
            for t, (off, rows) in enumerate(TILES):
                for h in range(H):
                    y = hn[0:rows, t, h, 0:DH]
                    ins = dve.scalar_tensor_tensor(out=y, in0=y, scalar=mv[0:rows, t, h, 0:1],
                                                   in1=gain[0:rows, 1, h * DH:(h + 1) * DH], op0=ALU.subtract, op1=ALU.mult)
                step(ins)
                for h in range(H):
                    y = hn[0:rows, t, h, 0:DH]
                    dve.scalar_tensor_tensor(out=y, in0=y, scalar=srec[0:rows, t, h:h + 1],
                                             in1=u[0:rows, t, h * DH:(h + 1) * DH], op0=ALU.mult, op1=ALU.mult
                                             ).then_inc(y_ready, 1)
            empty_transposes("yT", uT, TILES)
            add_to_x("out")

            def memory(l):
                gidx = 2 if l == 0 else 7
                dve.wait_ge(gain_loaded[gidx % 2], 16 * (gidx // 2 + 1))
                for t in range(2):
                    dve.wait_ge(mstd_ready, 2 * l + t + 1)
                    step(dve.reciprocal(mrstd[:, t:t + 1], mstd[:, t:t + 1]))
                    dve.scalar_tensor_tensor(out=u[:, t, :], in0=memx[:, t, :], scalar=mrstd[:, t:t + 1], in1=gain[:, gidx % 2, :],
                                             op0=ALU.mult, op1=ALU.mult).then_inc(mu_ready, 1)
                if l == 0:
                    dve.wait_ge(state_stored, 64)
                empty_transposes(f"memT{l}", memT, ((0, P), (P, P)))
                for name, dst in ((f"memk{l}", mk), (f"memv{l}", mv_)):
                    for c in range(2):
                        for t in range(2):
                            dve.tensor_copy(dst[:, t, c * 512:(c + 1) * 512], full(DJ[name] + 2 * c + t)).then_inc(d_emptied, 1)
                for j in range(4):
                    dve.tensor_copy(mkT[:, 2 * j:2 * j + 2, :], full(DJ[f"memkT{l}"] + j).rearrange("p (b m) -> p b m", m=MEM)
                                    ).then_inc(d_emptied, 1)

            def attend(l, norm):
                scale_rows(f"xn{l}", norm, 3 if l == 0 else 8)
                empty_transposes(f"xn{l}", uT, TILES)
                for m in range(8):
                    dve.tensor_copy(qT[:, m, :], full(DJ[f"xq{l}"] + m)[:, 0:TOK]).then_inc(d_emptied, 1)

                def normalise(j):
                    rows = TILES[j % 3][1]
                    dve.wait_ge(p_exp, 12 * l + j + 1)
                    step(dve.reciprocal(rinv_p[0:rows, j:j + 1], rsum[0:rows, j:j + 1]))
                    dve.tensor_scalar(probs[0:rows, j, :], probs[0:rows, j, :], rinv_p[0:rows, j:j + 1], None, ALU.mult
                                      ).then_inc(p_ready, 1)

                for j in range(3 * H):
                    rows = TILES[j % 3][1]
                    n = DJ[f"sc{l}"] + j
                    dve.tensor_scalar(probs[0:rows, j, :], full(n)[0:rows, 0:MEM], DH ** -0.5, None, ALU.mult).then_inc(d_emptied, 1)
                    dve.wait_ge(d_emptied, n + 1)
                    dve.tensor_reduce(nmx[0:rows, j:j + 1], probs[0:rows, j, :], AX.X, ALU.max, negate=True).then_inc(mx_ready, 1)
                    if j >= 2:
                        normalise(j - 2)
                normalise(3 * H - 2)
                normalise(3 * H - 1)
                for n, h, k in av_order(l):
                    if k < 2:
                        dve.tensor_copy(probsT[:, h % 2, k, :], full(n)[:, 0:TOK]).then_inc(d_emptied, 1)
                    else:
                        dve.tensor_copy(uT[:, 2 * h + k - 2, :], full(n)[:, 0:TOK]).then_inc(d_emptied, 1)
                add_to_x(f"xo{l}")

            def best16(r, values):
                def each(op):
                    for t, (off, rows) in enumerate(TILES):
                        row_step.after(2)
                        row_step.mark(op(t, rows))

                each(lambda t, rows: dve.max(v16[0:rows, r, t, 0:8], values[0:rows, t, :]))
                each(lambda t, rows: dve.max_index(i16[0:rows, r, t, 0:8], v16[0:rows, r, t, 0:8], values[0:rows, t, :]))
                n = values.shape[-1]
                each(lambda t, rows: dve.match_replace(spare[0:rows, t, 0:n], v16[0:rows, r, t, 0:8], values[0:rows, t, :],
                                                       -3.0e38))
                each(lambda t, rows: dve.max(v16[0:rows, r, t, 8:16], spare[0:rows, t, 0:n]))
                each(lambda t, rows: dve.max_index(i16[0:rows, r, t, 8:16], v16[0:rows, r, t, 8:16], spare[0:rows, t, 0:n]))

            def choose(l):
                with dve.Fori(0, HP // 4) as i:
                    for r in range(4):
                        row_step.after(15)
                        bank = full(DJ[f"pq{l}"] + r, i, 4)[:, 0:3 * P].rearrange("p (t n) -> p t n", n=P)
                        row_step.mark(dve.tensor_copy(cur[:, r % 2, 0:2, :], bank[:, 0:2, :]))
                        row_step.mark(dve.tensor_copy(cur[0:NS, r % 2, 2, :], bank[0:NS, 2, :]))
                        row_step.after(0)
                        dve.sem_inc(d_emptied, 1)
                        best16(r, cur[:, r % 2])
                    row_step.after(0)
                    row_step.mark(dve.tensor_copy(sval[:, bass.ds(i * 4, 4)], v16))
                    row_step.mark(dve.tensor_copy(sidx[:, bass.ds(i * 4, 4)], i16))
                    row_step.restart()
                sv2 = sval.rearrange("p (h a) t k -> p h a t k", a=2)
                si2 = sidx.rearrange("p (h a) t k -> p h a t k", a=2)
                with dve.Fori(0, PH) as i:
                    for t, (off, rows) in enumerate(TILES):
                        row_step.mark(dve.tensor_tensor(cand[0:rows, t, :].rearrange("p (a b) -> p a b", b=TOPK),
                                                        sv2[0:rows, i, 0, t, :].unsqueeze(2).to_broadcast([rows, TOPK, TOPK]),
                                                        sv2[0:rows, i, 1, t, :].unsqueeze(1).to_broadcast([rows, TOPK, TOPK]),
                                                        ALU.add))
                    best16(0, cand)
                    row_step.after(0)
                    row_step.mark(dve.tensor_copy(top[:, i], v16[:, 0]))
                    row_step.mark(dve.tensor_copy(tpos.bitcast(U32)[:, i], i16[:, 0]))
                    row_step.restart()
                for t, (off, rows) in enumerate(TILES):
                    gate = picked[0:rows, t, 2, :].rearrange("p (h k) -> p h k", k=TOPK)
                    dve.tensor_tensor(gate, top[0:rows, :, t, :], top[0:rows, :, t, 0:1].to_broadcast([rows, PH, TOPK]),
                                      ALU.subtract).then_inc(top_ready, 1)
                for t in range(3):
                    bits = cand.bitcast(U32)[:, t, :].rearrange("p (a h k) -> p a h k", a=2, k=TOPK)
                    tp = tpos.bitcast(U32)[:, :, t, :]
                    dve.tensor_scalar(bits[:, 0], tp, 4, None, ALU.logical_shift_right)
                    ins = dve.tensor_scalar(bits[:, 1], tp, 15, None, ALU.bitwise_and)
                step(ins)
                step(dve.tensor_copy(pij, cand.bitcast(U32).rearrange("p t (a h k) -> p t a h k", a=2, k=TOPK)))
                for t, (off, rows) in enumerate(TILES):
                    shape = [rows, 4, TOPK, TOPK]
                    for a in range(2):
                        for q in range(2):
                            hs = slice(4 * q, 4 * q + 4)
                            ins = dve.tensor_tensor(eq[0:rows, q], pij[0:rows, t, a, hs, :].unsqueeze(3).to_broadcast(shape),
                                                    iota[0:rows, 0:TOPK].unsqueeze(1).unsqueeze(1).to_broadcast(shape),
                                                    ALU.is_equal)
                        step(ins)
                        for q in range(2):
                            hs = slice(4 * q, 4 * q + 4)
                            ins = dve.tensor_tensor(eq[0:rows, q], eq[0:rows, q],
                                                    si2[0:rows, hs, a, t, :].unsqueeze(2).to_broadcast(shape), ALU.mult)
                        step(ins)
                        for q in range(2):
                            hs = slice(4 * q, 4 * q + 4)
                            out = picked[0:rows, t, a, :].rearrange("p (h k) -> p h k", k=TOPK)[:, hs, :]
                            ins = dve.tensor_reduce(out, eq[0:rows, q], AX.X, ALU.add)
                        step(ins)

            def peer(l, norm):
                scale_rows(f"fn{l}", norm, 4 if l == 0 else 9)
                empty_transposes(f"fn{l}", uT, TILES)
                step(dve.memset(v16, 0.0))
                step(dve.memset(i16.bitcast(F32), 0.0))
                choose(l)
                for t, (off, rows) in enumerate(TILES):
                    dve.wait_ge(exp_ready, 3 * l + t + 1)
                    gate = picked[0:rows, t, 2, :].rearrange("p (h k) -> p h k", k=TOPK)
                    step(dve.tensor_reduce(sume[0:rows, t, 0:PH], gate, AX.X, ALU.add))
                    step(dve.reciprocal(sume[0:rows, t, PH:2 * PH], sume[0:rows, t, 0:PH]))
                    dve.tensor_tensor(gate, gate, sume[0:rows, t, PH:2 * PH].unsqueeze(2).to_broadcast([rows, PH, TOPK]), ALU.mult
                                      ).then_inc(picked_ready, 1)
                for t, (off, rows) in enumerate(TILES):
                    bank = full(DJ[f"slot{l}"] + t)[:, 0:3 * P].rearrange("p (a c) -> p a c", c=P)
                    dve.tensor_copy(slots[:, :, off:off + rows], bank[:, :, 0:rows]).then_inc(d_emptied, 1)
                dve.wait_ge(d_emptied, DJ[f"slot{l}"] + 3)
                with dve.Fori(0, 5) as i:
                    for c in range(64):
                        r, g, q = c // 16, (c % 16) // 4, c % 4
                        if q == 0:
                            dve.wait_ge(a_filled, i * 20 + (AJ[f"gb{l}"] + 5 * r + (g if g >= 2 else g - 1)))
                        ti, tj, tg = (slots[:, a, bass.ds(i * 64 + c, 1)] for a in range(3))
                        dve.tensor_scalar(ohJ[:, c % 8, :], iota, tj, None, ALU.is_equal)
                        dve.tensor_scalar(oh[:, c % 8, :], iota, ti, tg, ALU.is_equal, ALU.mult).then_inc(oh_ready, 1)
                step(dve.memset(phl[:, 0, 0:P].bitcast(F32), 0.0))
                dve.memset(vhl[:, 0, 0, 0:512].bitcast(F32), 0.0).then_inc(zero_ready, 1)
                dve.wait_ge(zero_ready, l + 1)

                def product_parts(i, r):
                    if r % 4 == 0:
                        dve.wait_ge(g_loaded[r // 4], i * 16 + 16 * (16 * l + 1))
                    dve.wait_ge(a_emptied, i * 8 + (AJ[f"uv{l}"] + r + 1 - LAG))
                    dve.wait_ge(v_summed, i * 8 + ((NB + 2) * l + r + 1))
                    p, ph = pf[:, r % 2, :], phl[:, r % 2, :]
                    step(dve.tensor_tensor(p.rearrange("p (c t) -> p c t", t=GC),
                                           act8[:, i % (LAG // 8), r, :].rearrange("p (c t) -> p c t", t=GC),
                                           g_ring[:, r // 4, :, (r % 4) * GC:(r % 4 + 1) * GC], ALU.mult))
                    step(dve.tensor_copy(ph[:, 0:TOK], p))
                    hi = ph[:, 0:TOK].bitcast(F32)
                    dve.tensor_tensor(ph[:, TOK:TOK + NS], p[:, NP_:TOK], hi[:, NP_:TOK], ALU.subtract)
                    dve.tensor_tensor(ph[:, TOK + NS:2 * TOK], p[:, 0:NP_], hi[:, 0:NP_], ALU.subtract).then_inc(p_split, 1)
                    dve.wait_ge(vhi_ready, i * 8 + (NB * l + r + 1))
                    dve.tensor_tensor(vhl[:, r % 2, 1, :], v_raw[:, (r // 2) % 2, r % 2, :],
                                      vhl[:, r % 2, 0, :].bitcast(F32), ALU.subtract).then_inc(v_split, 1)

                with dve.Fori(0, 16) as i:
                    step.loop(i, 16)
                    for r in range(8):
                        product_parts(i, r)
                step.done(16)
                dve.wait_ge(v_summed, (NB + 2) * (l + 1))
                for n in range(2):
                    dve.tensor_copy(acc_tmp[:, n, :], psum[:, 6 + n, :]).then_inc(acc_copied, 1)
                for t in range(2):
                    for n in range(2):
                        dst = x[:, t, n * 512:(n + 1) * 512]
                        dve.tensor_tensor(dst, psum[:, 2 + 2 * t + n, :], dst, ALU.add).then_inc(acc_emptied, 1)
                for n in range(2):
                    dst = x[0:NS, 2, n * 512:(n + 1) * 512]
                    dve.tensor_tensor(dst, full(DJ[f"fold{l}"] + n)[0:NS, :], dst, ALU.add).then_inc(d_emptied, 1)

            memory(0)
            attend(0, 1)
            peer(0, 2)
            dve.memset(u[NS:P, 2, :], 0.0).then_inc(prefix_clear, 1)
            scale_rows("mix1", 3, 5)
            for b in range(KD):
                dve.tensor_copy(plT[:, b, :], full(DJ["pool"] + b)[:, 0:TOK]).then_inc(d_emptied, 1)
            dve.wait_ge(gain_loaded[0], 16 * 4)
            for g in range(4):
                for t, (off, rows) in enumerate(TILES):
                    n = DJ["pool"] + KD + 3 * g + t
                    if 3 * g + t >= 2:
                        dve.wait_ge(pooled, 3 * g + t - 1)
                    tmp, dst = pool_tmp[0:rows, (3 * g + t) % 2, :], x[0:rows, t, g * DH:(g + 1) * DH]
                    dve.tensor_tensor(tmp, full(n)[0:rows, 0:DH], gain[0:rows, 0, g * DH:(g + 1) * DH], ALU.mult
                                      ).then_inc(d_emptied, 1)
                    dve.wait_ge(d_emptied, n + 1)
                    dve.tensor_tensor(dst, dst, tmp, ALU.add).then_inc(pooled, 1)
            memory(1)
            attend(1, 4)
            peer(1, 5)
            scale_rows("final", 6, 10)


def av_order(l):
    n = DJ[f"av{l}"]
    for h in range(H + 1):
        for k in ((0, 1) if h < H else ()):
            yield n, h, k
            n += 1
        for k in ((2, 3) if h >= 1 else ()):
            yield n, h - 1, k
            n += 1


def av_pt_done(l, h):
    return max(n for n, hh, k in av_order(l) if hh == h and k < 2) + 1


PQ_ORDER = [("q", 0)] + [x for m in range(7) for x in (("q", m + 1), ("s", m))] + [("s", 7)]


OUTPUTS = {"y_p": (NP_, D), "y_s": (NS, D), "Cn_p": (D, VA), "m_p": (1, H), "pool_p": (POOLST, D),
           "mem_k": (2, MEM, D), "mem_v": (2, MEM, D), "Cn_s": (D, VA), "m_s": (1, H), "pool_s": (POOLST, D)}


def chunks(w):
    return np.ascontiguousarray(w.reshape(KD, P, -1, 512).transpose(2, 1, 0, 3))


def layout(inp):
    a = {k: np.asarray(v) for k, v in inp.items()}
    w_in = a["w_mlstm_in"][0]
    t = {
        "x_prompt": a["x_prompt"], "x_sample": a["x_sample"],
        "w_qk": chunks(w_in[:, :2 * D]), "w_vo": chunks(w_in[:, 2 * D:4 * D]),
        "w_gates": w_in[:, 4 * D:].reshape(KD, P, 2 * H).transpose(1, 0, 2),
        "b_gates": np.stack([a["b_mlstm_i"][0], a["b_mlstm_f"][0]], axis=1),
        "state_m": a["state_mlstm_m"][0, 0], "state_Cn": np.concatenate([a["state_mlstm_C"].reshape(D, DH), a["state_mlstm_n"].reshape(D, 1)], axis=1),
        "state_pool": a["state_pool"][0, 0],
        "w_out": chunks(a["w_mlstm_out"][0]),
        "mem_prompt": a["mem_prompt"][0],
        "cache_kT": a["cache_mem_k"].reshape(2, MEM, D).transpose(0, 2, 1),
        "cache_v": a["cache_mem_v"].reshape(2, MEM, D),
        "gains": np.stack([a["g_mix"][0], a["g_mlstm_head"][0], a["g_mem"][0], a["g_xattn"][0], a["g_ffn"][0],
                           a["g_mix"][1], a["s_pool"][0], a["g_mem"][1], a["g_xattn"][1], a["g_ffn"][1], a["g_final"]]),
        "w_pool": a["w_pool"][0].reshape(4, 2, P, DH).transpose(2, 0, 1, 3),
        "peer_keys": a["peer_keys"].reshape(2, HP, NK, P).transpose(0, 3, 1, 2),
        "peer_u": a["peer_u"].reshape(2, NB // 2, 2, P, KD, P).transpose(0, 1, 5, 2, 4, 3),
        "peer_v": a["peer_v"].reshape(2, NB // 2, 2, P, D).transpose(0, 1, 3, 2, 4),
        "constants": constants(), "bands": bands(),
    }
    for name, key in (("w_xk", "w_xk"), ("w_xv", "w_xv"), ("w_xq", "w_xq"), ("w_xo", "w_xo"), ("w_pq", "w_peer_q")):
        t[name] = np.stack([chunks(a[key][l]) for l in range(2)])
    return {k: np.ascontiguousarray(v) for k, v in t.items()}


def results(r):
    def state(cn, m):
        return (cn[:, 0:DH].reshape(1, 1, H, DH, DH), cn[:, DH].reshape(1, 1, H, DH), m.reshape(1, 1, H))

    return (r["y_p"].reshape(1, NP_, D), r["y_s"].reshape(1, NS, D), *state(r["Cn_p"], r["m_p"]),
            r["pool_p"].reshape(1, 1, POOLST, D), r["mem_k"].reshape(2, 1, MEM, H, DH), r["mem_v"].reshape(2, 1, MEM, H, DH),
            *state(r["Cn_s"], r["m_s"]), r["pool_s"].reshape(1, 1, POOLST, D))


def kernel(**inputs):
    import concourse.bacc as bacc
    from concourse.bass_utils import run_bass_kernel_spmd

    nc = bacc.Bacc("TRN2", target_bir_lowering=False, num_devices=1)
    arrays = layout(inputs)
    t_in = {k: nc.dram_tensor(k, v.shape, F32, kind="ExternalInput").ap() for k, v in arrays.items()}
    t_out = {k: nc.dram_tensor(k, shape, F32, kind="ExternalOutput").ap() for k, shape in OUTPUTS.items()}
    build(nc, t_in, t_out)
    r = run_bass_kernel_spmd(nc, [arrays], core_ids=[0])
    return results(r.results[0])
```

```python
from contextlib import ExitStack

import numpy as np
import concourse.bass as bass
import concourse.mybir as mybir

F32, F32R, BF16, U32 = mybir.dt.float32, mybir.dt.float32r, mybir.dt.bfloat16, mybir.dt.uint32
ALU, ACT, AX = mybir.AluOpType, mybir.ActivationFunctionType, mybir.AxisListType

P = 128
D = 1024
KD = D // P
TOK = 320
TILES = ((0, 128), (128, 128), (256, 64))
NP_ = 256
NS = 64
H = 4
DH = D // H
VA = DH + 1
MEM = 256
PH = 8
HP = 2 * PH
NK = 128
TOPK = 16
SLOTS = PH * TOPK
NB = NK
LAG = 56
GB = 20
XU = 4
AHEAD = LAG - GB - XU
UV = (NB - LAG) // 8
GC = 16
NGC = TOK // GC
EPS = 1e-6
NEG = -1e30
POOLW = (2, 4, 8, 16)
POOLST = 15

STAGES = [
    ("mixn0", 6, 0), ("qk", 16, 0), ("v", 6, 0), ("o", 0, 6), ("gates", 2, 0), ("cols", 1, 0),
    ("rb", 4, 0), ("sel", 1, 0), ("qkt", 12, 0), ("ktok", 6, 0), ("mix", 20, 0), ("state", 16, 0),
    ("yT", 6, 0), ("out", 6, 0),
    ("memT0", 4, 0), ("memk0", 4, 0), ("memv0", 4, 0), ("memkT0", 4, 0),
    ("xn0", 6, 0), ("xq0", 8, 0), ("sc0", 12, 0), ("av0", 16, 0), ("xo0", 6, 0),
    ("fn0", 6, 0), ("pq0", HP, HP), ("up0", 0, AHEAD), ("slot0", 3, 0), ("gb0", 0, 5 * GB), ("ux0", 0, XU), ("uv0", 0, NB - LAG),
    ("fold0", 2, 0),
    ("pool", 20, 0),
    ("memT1", 4, 0), ("memk1", 4, 0), ("memv1", 4, 0), ("memkT1", 4, 0),
    ("xn1", 6, 0), ("xq1", 8, 0), ("sc1", 12, 0), ("av1", 16, 0), ("xo1", 6, 0),
    ("fn1", 6, 0), ("pq1", HP, HP), ("up1", 0, AHEAD), ("slot1", 3, 0), ("gb1", 0, 5 * GB), ("ux1", 0, XU), ("uv1", 0, NB - LAG),
    ("fold1", 2, 0),
]
DJ, AJ = {}, {}
_d = _a = 0
for _n, _dj, _aj in STAGES:
    DJ[_n], AJ[_n] = _d, _a
    _d, _a = _d + _dj, _a + _aj
DJ["end"], AJ["end"] = _d, _a
G_JOBS, U_JOB = (0, 1, 2, 4), 3
GB_UBANKS = (2, 3)
DBANKS = (2, 3, 4, 5)
ABANKS = (0, 1, 6, 7)

WEIGHTS = [("qk", 4), ("vo", 4), ("out", 2), ("memk0", 2), ("memv0", 2), ("xq0", 2), ("xo0", 2), ("pq0", 4),
           ("U0", 64), ("memk1", 2), ("memv1", 2), ("xq1", 2), ("xo1", 2), ("pq1", 4), ("U1", 64)]
WC = {}
_c = 0
for _n, _k in WEIGHTS:
    WC[_n] = _c
    _c += _k

GAINS = ("mix0", "head", "mem0", "xn0", "fn0", "mix1", "spool", "mem1", "xn1", "fn1", "final")
NORMS = ("mix0", "xn0", "fn0", "mix1", "xn1", "fn1", "final")


def tri():
    return np.where(np.tril(np.ones((P, P), bool)), np.float32(0), np.float32(NEG)).astype(np.float32)


def constants():
    eye = np.eye(P, dtype=np.float32)
    iota = np.broadcast_to(np.arange(P, dtype=np.float32), (P, P))
    sel4 = np.zeros((P, H, P), np.float32)
    for h in range(H):
        sel4[h, h] = 1
    last_p = np.zeros((P, P), np.float32)
    last_p[P - 1] = 1
    last_s = np.zeros((P, P), np.float32)
    last_s[NS - 1] = 1
    fold = np.concatenate([np.eye(NS), np.eye(NS)]).astype(np.float32)
    return np.concatenate([eye, iota, tri(), sel4.reshape(P, -1), last_p, last_s, fold], axis=1)


def bands():
    p = np.zeros((P, 4, 2, NP_), np.float32)
    s = np.zeros((P, 4, NS), np.float32)
    for g, w in enumerate(POOLW):
        for t in range(NP_):
            for a in range(max(0, t - w + 1), t + 1):
                p[a % P, g, a // P, t] += 1.0 / min(t + 1, w)
            p[t % P, g, t // P, t] -= 1
        for t in range(NS):
            for a in range(t - w + 1, t + 1):
                s[a if a >= 0 else NS + POOLST + a, g, t] += 1.0 / w
            s[t, g, t] -= 1
    return np.concatenate([p.reshape(P, -1), s.reshape(P, -1)], axis=1)


class Chain:

    def __init__(self, eng, sem):
        self.eng, self.sem, self.n, self.i, self.per, self.base = eng, sem, 0, None, 0, 0

    def __call__(self, ins):
        self.n += 1
        ins.then_inc(self.sem, 1)
        self.eng.wait_ge(self.sem, self.n if self.i is None else self.i * self.per + self.n)

    def after(self, back):
        if self.n > back:
            self.eng.wait_ge(self.sem, self.n - back)

    def mark(self, ins):
        self.n += 1
        ins.then_inc(self.sem, 1)

    def restart(self):
        self.after(0)
        self.eng.sem_clear(self.sem)
        self.n = 0

    def loop(self, i, per):
        self.i, self.per, self.base = i, per, self.n

    def done(self, iterations):
        assert self.n - self.base == self.per, (self.n - self.base, self.per)
        self.n, self.i = self.base + iterations * self.per, None


def build(nc, t_in, t_out):
    with ExitStack() as ctx:
        def sb(name, cols, dt=F32):
            return ctx.enter_context(nc.sbuf_tensor(name, [P, cols], dt))

        def sem(name):
            return ctx.enter_context(nc.semaphore(name))

        g_dram = [nc.dram_tensor(f"gates_{l}", (NGC, P, NK // 8, 8 * GC), F32, kind="Internal").ap() for l in range(2)]

        x_sb = sb("x_sb", 3 * D)
        uT_split = sb("uT_split", 2 * KD * TOK, F32R)
        w_split = sb("w_split", 4 * 2 * 2 * P, F32R)
        w_ring = sb("w_ring", 2 * KD * 512)
        p_hl = sb("p_hl", 2 * 2 * TOK, F32R)
        v_hl = sb("v_hl", 2 * 2 * D, F32R)
        gains = sb("gain_rows", 2 * D)
        cst = sb("cst", 3 * P + H * P + 2 * P + NS)
        shared = sb("shared", 9 * P + 3 * TOK + 2 * TOK)
        small = sb("small", 64)
        arena = sb("arena", 23104)
        psum = ctx.enter_context(nc.psum_tensor("psum", [P, 8, 512], F32))

        def view(t, off, *dims):
            n = int(np.prod(dims))
            a = t[:, off:off + n]
            if len(dims) == 2:
                return a.rearrange("p (a b) -> p a b", b=dims[1])
            if len(dims) == 3:
                return a.rearrange("p (a b c) -> p a b c", b=dims[1], c=dims[2])
            if len(dims) == 4:
                return a.rearrange("p (a b c d) -> p a b c d", b=dims[1], c=dims[2], d=dims[3])
            return a

        x = view(x_sb, 0, 3, D)
        uT = view(shared, 0, KD, TOK)
        uT_hi, uT_lo = view(uT_split, 0, KD, TOK), view(uT_split, KD * TOK, KD, TOK)
        wq = view(w_split, 0, 4, 2, 2, P)
        W = [view(w_ring, s * KD * 512, KD, 512) for s in range(2)]
        Ublk = [view(w_ring, s * KD * 512, 2, KD, P) for s in range(2)]
        v_raw = [view(w_ring, s * KD * 512 + 2 * D, 2, D) for s in range(2)]
        g_stage = [view(w_ring, s * KD * 512 + 2 * D, NK, GC) for s in range(2)]
        gain = view(gains, 0, 2, D)
        ident, iota, tri_m = cst[:, 0:P], cst[:, P:2 * P], cst[:, 2 * P:3 * P]
        sel4 = view(cst, 3 * P, H, P)
        last_p, last_s = cst[:, 7 * P:8 * P], cst[:, 8 * P:9 * P]
        fold = cst[:, 9 * P:9 * P + NS]
        ss, std, rstd = small[:, 0:3], small[:, 3:6], small[:, 6:9]
        mss, mstd, mrstd = small[:, 9:11], small[:, 11:13], small[:, 13:15]
        eps_c, one_c = small[:, 15:16], small[:, 16:17]
        nmx, rsum, rinv_p = small[:, 17:29], small[:, 29:41], small[:, 41:53]
        u = view(arena, 20032, 3, D)
        act4 = view(arena, 0, LAG // 4, 4, TOK)
        act8 = view(arena, 0, LAG // 8, 8, TOK)
        g_ring = view(arena, LAG * TOK, 2, NGC, 8 * GC)
        qT, kT = view(arena, 0, KD, TOK), view(arena, 2560, KD, TOK)
        kw = view(arena, 5120, 3, D)
        v_aug = view(arena, 8192, 3, H, VA)
        wts = view(arena, 11280, H, 448)
        swT = view(arena, 13072, 2, 448)
        hn = view(arena, 13968, 3, H, VA)
        C_new = view(arena, 0, KD, VA)
        C_aug = view(arena, 17056, KD, VA)
        R4 = view(arena, 13968, 6, TOK)
        wg = view(arena, 19112, KD, 2 * H)
        br, bm = view(arena, 19176, 3, 2 * H), view(arena, 19200, 3, 2 * H)
        m0c, inter, rmax, negm = (view(arena, 19224 + 12 * k, 3, H) for k in range(4))
        idiff, ainter, emneg, wsarg = (view(arena, 19272 + 12 * k, 3, H) for k in range(4))
        wscol, rinv, sdev, srec = (view(arena, 19320 + 12 * k, 3, H) for k in range(4))
        selev, blm, garg, gstate = arena[:, 19368:19384], view(arena, 19384, 2, H), arena[:, 19392:19396], arena[:, 19396:19400]
        mv = view(arena, 19400, 3, H, 2)
        bnst = view(arena, 19424, 3 * H, 6)
        qc_tmp = view(arena, 2560, 2, VA)
        b4 = arena[:, 19754:19756]
        mkT, mv_ = view(arena, 2560, KD, MEM), view(arena, 4608, 2, D)
        mk = view(arena, 6656, 2, D)
        skT, sv_ = view(arena, 8704, KD, MEM), view(arena, 10752, 2, D)
        probs = view(arena, 12800, H * 3, MEM)
        probsT = view(arena, 15872, 2, 2, TOK)
        memT, memx = view(arena, 12800, KD, MEM), view(arena, 17152, 2, D)
        wpool = view(arena, 0, 4, 2, DH)
        bandp, bands_ = view(arena, 2048, 4, 2, NP_), view(arena, 4096, 4, NS)
        plT = view(arena, 4352, KD, TOK)
        pool_tmp = view(arena, 8192, 2, DH)
        pqT = view(arena, 0, KD, TOK)
        keysT = view(arena, 2560, HP, NK)
        top0 = AHEAD * TOK
        cur = view(arena, top0, 2, 3, NK)
        spare = view(arena, top0 + 768, 3, 2 * NK)
        v16, i16 = view(arena, top0 + 1536, 4, 3, TOPK), view(arena, top0 + 1728, 4, 3, TOPK).bitcast(U32)
        eq = arena[:, top0:top0 + 1024].bitcast(BF16).rearrange("p (q h k c) -> p q h k c", q=2, k=TOPK, c=TOPK)
        cand = view(arena, top0 + 2048, 3, TOPK * TOPK)
        sval, sidx = view(arena, top0 + 2816, HP, 3, TOPK), view(arena, top0 + 3584, HP, 3, TOPK)
        top, tpos = view(arena, top0 + 4352, PH, 3, TOPK), view(arena, top0 + 4736, PH, 3, TOPK)
        pij = arena[:, top0 + 5120:top0 + 5504].bitcast(BF16).rearrange("p (t a h k) -> p t a h k", t=3, a=2, k=TOPK)
        sidx16 = arena[:, top0 + 5504:top0 + 5888].bitcast(BF16).rearrange("p (g t k) -> p g t k", t=3, k=TOPK)
        iota16 = arena[:, top0 + 5936:top0 + 5944].bitcast(BF16)
        sume = view(arena, top0 + 5888, 3, 2 * PH)
        picked = view(shared, 0, 3, 3, P)
        oh = view(shared, 0, 8, P)
        ohJ = view(arena, LAG * TOK, 8, P)
        slots = view(shared, 9 * P, 3, TOK)
        acc_tmp = view(arena, 0, 2, 512)
        phl = view(p_hl, 0, 2, 2 * TOK)
        vhl = view(v_hl, 0, 2, 2, D)
        pf = view(shared, 9 * P + 3 * TOK, 2, TOK)

        x_loaded, cst_loaded, mix_loaded = sem("x_loaded"), sem("cst_loaded"), sem("mix_loaded")
        w_loaded = [sem(f"w_loaded{s}") for s in range(2)]
        gain_loaded = [sem(f"gain_loaded{s}") for s in range(2)]
        mem_loaded, cache_loaded, pool_loaded, prefix_loaded, keys_loaded = (
            sem(n) for n in ("mem_loaded", "cache_loaded", "pool_loaded", "prefix_loaded", "keys_loaded"))
        v_loaded = [sem(f"v_loaded{s}") for s in range(2)]
        g_loaded = sem("g_loaded")
        g_stored = [sem(f"g_stored{s}") for s in range(2)]
        state_stored, mem_stored, pool_stored, y_stored = (
            sem(n) for n in ("state_stored", "mem_stored", "pool_stored", "y_stored"))
        d_filled, d_emptied, a_filled, a_emptied = (sem(n) for n in ("d_filled", "d_emptied", "a_filled", "a_emptied"))
        dve_step, dve_row_step, act_step = sem("dve_step"), sem("dve_row_step"), sem("act_step")
        init_done, std_ready, u_ready, mstd_ready, mu_ready = (
            sem(n) for n in ("init_done", "std_ready", "u_ready", "mstd_ready", "mu_ready"))
        gate_abs, gate_ln, gate_rows, m_ready, w_ready, mexp_ready = (
            sem(n) for n in ("gate_abs", "gate_ln", "gate_rows", "m_ready", "w_ready", "mexp_ready"))
        ws_arg, ws_ready, var_ready, sdev_ready, y_ready = (
            sem(n) for n in ("ws_arg", "ws_ready", "var_ready", "sdev_ready", "y_ready"))
        mx_ready, p_exp, p_ready, pooled = (sem(n) for n in ("mx_ready", "p_exp", "p_ready", "pooled"))
        top_ready, exp_ready, picked_ready, oh_ready = (
            sem(n) for n in ("top_ready", "exp_ready", "picked_ready", "oh_ready"))
        w_hi_ready, w_lo_ready, quarter_used = (sem(n) for n in ("w_hi_ready", "w_lo_ready", "quarter_used"))
        vhi_ready, v_split, p_split, v_summed, acc_emptied, acc_copied = (
            sem(n) for n in ("vhi_ready", "v_split", "p_split", "v_summed", "acc_emptied", "acc_copied"))
        prefix_clear, zero_ready, blm_ready = sem("prefix_clear"), sem("zero_ready"), sem("blm_ready")

        block = ctx.enter_context(nc.Block())

        def at(i, per, n):
            return n if i is None else i * per + n

        def quarter(block, m, q):
            return block[:, 2 * q:2 * q + 2, m * P:(m + 1) * P] if block.shape[-1] == 512 else block[:, m, 2 * q:2 * q + 2, :]

        def x_ready(norm, t):
            if norm == "mix0":
                return x_loaded, 48
            if norm in ("xn0", "xn1"):
                return (d_emptied, DJ["out"] + 4 + t) if norm == "xn0" else (pooled, 9 + t + 1)
            if norm in ("fn0", "fn1"):
                return d_emptied, DJ["xo" + norm[2]] + 4 + t
            l = 0 if norm == "mix1" else 1
            return (acc_emptied, 4 * l + 2 * t + 2) if t < 2 else (d_emptied, DJ[f"fold{l}"] + 2)

        @block.sync
        def _(sp):
            for k, (off, rows) in enumerate(TILES):
                src = t_in["x_prompt"][0, off:off + rows] if k < 2 else t_in["x_sample"][0]
                sp.dma_start(x[0:rows, k, :], src).then_inc(x_loaded, 16)

            def released(stage, local):
                if stage == "qk":
                    return d_filled, DJ["qk"] + 4 * (local + 1)
                if stage == "vo":
                    return (d_filled, DJ["v"] + 3 * (local + 1)) if local < 2 else (a_filled, AJ["o"] + 3 * (local - 1))
                if stage[:4] in ("memk", "memv"):
                    return d_filled, DJ[stage] + 2 * (local + 1)
                if stage[:2] == "xq":
                    return d_filled, DJ[stage] + 4 * (local + 1)
                if stage[:2] == "pq":
                    return w_lo_ready, split_base(int(stage[2]), 4 * (local + 1))
                if stage[0] == "U":
                    return w_lo_ready, split_base(int(stage[1]), HP + 2 * (local + 1))
                return d_filled, DJ[stage] + 3 * (local + 1)

            flat = [(n, k) for n, cnt in WEIGHTS for k in range(cnt)]

            def chunk(stage, local, src):
                c = WC[stage] + local
                if c >= 2:
                    s, v = released(*flat[c - 2])
                    sp.wait_ge(s, v)
                    if flat[c - 2][0][0] == "U":
                        sp.wait_ge(v_split, NB * (int(flat[c - 2][0][1]) + 1))
                sp.dma_start(W[c % 2], src).then_inc(w_loaded[c % 2], 16)

            def stage(name, src):
                for k in range(src.shape[0]):
                    chunk(name, k, src[k])

            stage("qk", t_in["w_qk"])
            stage("vo", t_in["w_vo"])
            stage("out", t_in["w_out"])
            for l in range(2):
                stage(f"memk{l}", t_in["w_xk"][l])
                stage(f"memv{l}", t_in["w_xv"][l])
                stage(f"xq{l}", t_in["w_xq"][l])
                stage(f"xo{l}", t_in["w_xo"][l])
                stage(f"pq{l}", t_in["w_pq"][l])
                U, V = t_in["peer_u"][l], t_in["peer_v"][l]
                for k in range(2):
                    sm, v = released(f"pq{l}", 2 + k)
                    sp.wait_ge(sm, v)
                    sp.dma_start(Ublk[k], U[k]).then_inc(w_loaded[k], 16)
                ubase = split_base(l, HP)
                with sp.Fori(0, (LAG - XU) // 4) as i:
                    for s in range(2):
                        sp.wait_ge(w_lo_ready, i * 16 + (ubase + 8 * (s + 1)))
                        sp.dma_start(Ublk[s], U[i * 2 + (2 + s)]).then_inc(w_loaded[s], 16)

                def u_load(i, q):
                    sp.wait_ge(w_lo_ready, i * 32 + (ubase + 4 * LAG + 8 * (q + 1)))
                    sp.dma_start(Ublk[q % 2], U[i * 4 + (LAG // 2 + 2 + q)]).then_inc(w_loaded[q % 2], 16)

                def v_load(i, q):
                    sp.wait_ge(v_split, i * 8 + (NB * l + 2 * q + 2))
                    sp.dma_start(v_raw[q % 2], V[i * 4 + (2 + q)]).then_inc(v_loaded[q % 2], 16)

                def g_load(i):
                    sp.wait_ge(p_split, i * 8 + NB * l)
                    sp.wait_ge(g_loaded, i * 16 + 16 * (16 * l + 1))
                    sp.dma_start(g_ring[:, (i + 1) % 2], g_dram[l][:, :, i + 1].rearrange("c j x -> j c x")
                                 ).then_inc(g_loaded, 16)

                def round_loads(i, u_chunks):
                    for q in range(4):
                        if q < u_chunks:
                            u_load(i, q)
                        v_load(i, q)

                for s in range(2):
                    sp.wait_ge(g_stored[s], 16 * (NGC // 2) * (l + 1))
                    sp.dma_start(v_raw[s], V[s]).then_inc(v_loaded[s], 16)
                sp.dma_start(g_ring[:, 0], g_dram[l][:, :, 0].rearrange("c j x -> j c x")).then_inc(g_loaded, 16)
                sp.wait_ge(g_loaded, 16 * (16 * l + 1))
                sp.dma_start(g_ring[:, 1], g_dram[l][:, :, 1].rearrange("c j x -> j c x")).then_inc(g_loaded, 16)
                for s in range(2):
                    sp.wait_ge(w_lo_ready, ubase + 4 * (LAG - XU) + 8 * (s + 1))
                    sp.dma_start(Ublk[s], U[LAG // 2 + s]).then_inc(w_loaded[s], 16)
                round_loads(0, 4)
                with sp.Fori(1, UV - 1) as i:
                    g_load(i)
                    round_loads(i, 4)
                g_load(UV - 1)
                round_loads(UV - 1, 2)
                with sp.Fori(UV, 15) as i:
                    g_load(i)
                    round_loads(i, 0)
                for q in range(2):
                    v_load(15, q)

        @block.gpsimd
        def _(pool):
            pool.dma_start(cst[:], t_in["constants"]).then_inc(cst_loaded, 16)

            def gain_load(k):
                if k >= 2:
                    sm, v = {"mix0": (u_ready, 3), "head": (y_ready, 12), "mem0": (mu_ready, 2), "xn0": (u_ready, 6),
                             "fn0": (u_ready, 9), "mix1": (u_ready, 12), "spool": (pooled, 12),
                             "mem1": (mu_ready, 4), "xn1": (u_ready, 15)}[GAINS[k - 2]]
                    pool.wait_ge(sm, v)
                pool.dma_start(gain[:, k % 2], t_in["gains"][k].partition_broadcast(P)).then_inc(gain_loaded[k % 2], 16)

            gain_load(0)
            gain_load(1)
            pool.dma_start(wg, t_in["w_gates"]).then_inc(mix_loaded, 16)
            pool.dma_start(b4[0:4, :], t_in["b_gates"]).then_inc(mix_loaded, 16)
            pool.wait_ge(init_done, 1)
            pool.dma_start(m0c[:, 2, :], t_in["state_m"].partition_broadcast(P)).then_inc(mix_loaded, 16)
            pool.dma_start(C_aug, t_in["state_Cn"].rearrange("(b p) e -> p b e", p=P)).then_inc(mix_loaded, 16)
            gain_load(2)
            pool.wait_ge(d_emptied, DJ["state"] + 16)
            for buf, out in ((C_new, "Cn_p"), (C_aug, "Cn_s")):
                pool.dma_start(t_out[out].rearrange("(b p) e -> p b e", p=P), buf).then_inc(state_stored, 16)
            pool.dma_start(t_out["m_p"], selev[0:1, H:2 * H]).then_inc(state_stored, 16)
            pool.dma_start(t_out["m_s"], selev[0:1, 3 * H:4 * H]).then_inc(state_stored, 16)
            gain_load(3)
            for l in range(2):
                if l == 0:
                    pool.wait_ge(state_stored, 64)
                    pool.wait_ge(d_filled, DJ["yT"] + 6)
                else:
                    pool.wait_ge(acc_emptied, 4)
                    pool.wait_ge(d_filled, DJ["fold0"] + 2)
                    pool.dma_start(wpool, t_in["w_pool"]).then_inc(pool_loaded, 16)
                    pool.dma_start(arena[:, 2048:4352], t_in["bands"]).then_inc(pool_loaded, 16)
                    pool.wait_ge(prefix_clear, 1)
                    pool.dma_start(u[NS:NS + POOLST, 2, :], t_in["state_pool"]).then_inc(prefix_loaded, 16)
                pool.dma_start(memx, t_in["mem_prompt"].rearrange("(b p) d -> p b d", p=P)).then_inc(mem_loaded, 16)
                pool.dma_start(skT, t_in["cache_kT"][l].rearrange("(b p) m -> p b m", p=P)).then_inc(cache_loaded, 16)
                pool.dma_start(sv_, t_in["cache_v"][l].rearrange("(b p) d -> p b d", p=P)).then_inc(cache_loaded, 16)
                if l == 1:
                    pool.wait_ge(u_ready, 12)
                    pool.dma_start(t_out["pool_p"], u[P - POOLST:P, 1, :]).then_inc(pool_stored, 16)
                    pool.dma_start(t_out["pool_s"], u[NS - POOLST:NS, 2, :]).then_inc(pool_stored, 16)
                    gain_load(7)
                    gain_load(8)
                    gain_load(9)
                else:
                    gain_load(4)
                pool.wait_ge(d_emptied, DJ[f"memk{l}"] + 4)
                pool.dma_start(t_out["mem_k"][l].rearrange("(b p) d -> p b d", p=P), mk).then_inc(mem_stored, 16)
                pool.wait_ge(d_emptied, DJ[f"memv{l}"] + 4)
                pool.dma_start(t_out["mem_v"][l].rearrange("(b p) d -> p b d", p=P), mv_).then_inc(mem_stored, 16)
                pool.wait_ge(d_filled, DJ[f"sc{l}"] + 12)
                pool.dma_start(keysT, t_in["peer_keys"][l]).then_inc(keys_loaded, 16)
                if l == 0:
                    gain_load(5)
                    gain_load(6)
                else:
                    gain_load(10)

                def lower_parts(i, per, block, raw, m):
                    for q in range(4):
                        pool.wait_ge(w_hi_ready, at(i, 4 * per, split_base(l, block) + q + 1))
                        pool.tensor_tensor(wq[:, q, 1], quarter(raw, m, q), wq[:, q, 0].bitcast(F32), ALU.subtract
                                           ).then_inc(w_lo_ready, 1)

                with pool.Fori(0, 2) as i:
                    for m in range(8):
                        lower_parts(i, 8, m, W[(WC[f"pq{l}"] + m // 4) % 2], m % 4)
                with pool.Fori(0, AHEAD // 4) as i:
                    for r in range(4):
                        lower_parts(i, 4, HP + r, Ublk[r // 2], r % 2)

                def store_gates(i, r):
                    pool.wait_ge(a_emptied, i * 20 + (AJ[f"gb{l}"] + 5 * r + 5))
                    pool.dma_start(g_dram[l][i * 4 + r], g_stage[r % 2].rearrange("p (a b) t -> p a (b t)", b=8)
                                   ).then_inc(g_stored[r % 2], 16)

                for r in range(4):
                    lower_parts(None, 0, HP + AHEAD + r, Ublk[r // 2], r % 2)
                    if r:
                        store_gates(0, r - 1)
                with pool.Fori(1, 5) as i:
                    for r in range(4):
                        lower_parts(i, 4, HP + AHEAD + r, Ublk[r // 2], r % 2)
                        store_gates(i if r else i - 1, (r - 1) % 4)
                store_gates(4, 3)
                with pool.Fori(0, (NB - LAG + XU) // 4) as i:
                    for r in range(4):
                        lower_parts(i, 4, HP + LAG - XU + r, Ublk[r // 2], r % 2)
            for t, (off, rows) in enumerate(TILES):
                pool.wait_ge(u_ready, 18 + t + 1)
                dst = t_out["y_p"][off:off + rows] if t < 2 else t_out["y_s"]
                pool.dma_start(dst, u[0:rows, t, :]).then_inc(y_stored, 16)
            pool.wait_ge(y_stored, 48)
            pool.wait_ge(mem_stored, 64)
            pool.wait_ge(pool_stored, 32)
            pool.wait_ge(state_stored, 64)

        @block.tensor
        def _(pe):
            def d_bank(n, i=None, per=0):
                if i is None:
                    if n >= 4:
                        pe.wait_ge(d_emptied, n - 3)
                else:
                    assert per % 4 == 0 and n >= 4
                    pe.wait_ge(d_emptied, i * per + (n - 3))
                return psum[:, DBANKS[n % 4], :]

            def a_bank(n, i=None, per=0):
                if i is None:
                    if n >= 4:
                        pe.wait_ge(a_emptied, n - 3)
                else:
                    assert per % 4 == 0 and n >= 4
                    pe.wait_ge(a_emptied, i * per + (n - 3))
                return psum[:, ABANKS[n % 4], :]

            def w_wait(stage, local, i=None):
                c = WC[stage] + local
                if i is None:
                    pe.wait_ge(w_loaded[c % 2], 16 * (c // 2 + 1))
                else:
                    pe.wait_ge(w_loaded[c % 2], i * 16 + 16 * (c // 2 + 1))
                return W[c % 2]

            def transposes(stage, src, tiles, n_ready, ready, first=0):
                n = DJ[stage]
                for t, (off, rows) in enumerate(tiles):
                    pe.wait_ge(ready, n_ready + t + 1)
                    for q in range(2):
                        bank = d_bank(n)
                        for b in range(4):
                            last = pe.transpose(bank[:, b * P:b * P + rows], src(t, rows, 4 * q + b), ident[0:rows, 0:rows])
                        last.then_inc(d_filled, 1)
                        n += 1

            def u_transposes(stage, norm):
                transposes(stage, lambda t, rows, b: u[0:rows, t, b * P:(b + 1) * P], TILES, 3 * norm, u_ready)

            def feature_major(stage, wstage, n_chunks, stage_first=0):
                def pair(i):
                    for s in range(2):
                        w = w_wait(wstage, s, i)
                        for m in range(4):
                            bank = d_bank(DJ[stage] + 4 * s + m, i, 8)
                            for k in range(KD):
                                last = pe.matmul(bank[:, 0:TOK], w[:, k, m * P:(m + 1) * P], uT[:, k, :],
                                                 start=k == 0, stop=k == KD - 1)
                            last.then_inc(d_filled, 1)
                if n_chunks == 2:
                    pair(None)
                else:
                    with pe.Fori(0, n_chunks // 2) as i:
                        pair(i)

            def token_major(stage, wstage, local, srcT, tiles, bank_of=d_bank, filled=d_filled, jobs=DJ, base=0):
                w = w_wait(wstage, local)
                for t, (off, rows) in enumerate(tiles):
                    bank = bank_of(jobs[stage] + base + t)
                    for k in range(KD):
                        last = pe.matmul(bank[0:rows, :], srcT[:, k, off:off + rows], w[:, k, :],
                                         start=k == 0, stop=k == KD - 1)
                    last.then_inc(filled, 1)

            pe.wait_ge(cst_loaded, 16)
            u_transposes("mixn0", 0)
            pe.wait_ge(d_emptied, DJ["mixn0"] + 6)
            feature_major("qk", "qk", 4)
            for c in range(2):
                token_major("v", "vo", c, uT, TILES, base=3 * c)
            for c in range(2):
                token_major("o", "vo", 2 + c, uT, TILES, a_bank, a_filled, AJ, 3 * c)
            pe.wait_ge(mix_loaded, 64)
            for g in range(2):
                bank = d_bank(DJ["gates"] + g)
                for k in range(KD):
                    last = pe.matmul(bank[0:H, 0:TOK], wg[:, k, H * g:H * g + H], uT[:, k, :], start=k == 0, stop=k == KD - 1)
                last.then_inc(d_filled, 1)
            pe.wait_ge(gate_rows, 1)
            bank = d_bank(DJ["cols"])
            for t, (off, rows) in enumerate(TILES):
                for a in range(2):
                    last = pe.transpose(bank[0:rows, t * 8 + a * H:t * 8 + a * H + H], R4[0:H, 4 + a, off:off + rows], ident[0:H, 0:H])
            last.then_inc(d_filled, 1)
            for h in range(H):
                bank = d_bank(DJ["rb"] + h)
                pe.matmul(bank[:, 0:TOK], sel4[0:H, h, :], R4[0:H, 5, :], start=True, stop=True).then_inc(d_filled, 1)
            pe.wait_ge(m_ready, 1)
            bank = d_bank(DJ["sel"])
            pe.matmul(bank[:, 0:8], last_p, bm[:, 1, :], start=True, stop=True)
            pe.matmul(bank[:, 8:16], last_s[0:NS, :], bm[0:NS, 2, :], start=True, stop=True).then_inc(d_filled, 1)
            keys = ((0, 128), (0, 256), (256, 64))
            for h in range(H):
                for t, (off, rows) in enumerate(TILES):
                    bank = d_bank(DJ["qkt"] + 3 * h + t)
                    k0, kn = keys[t]
                    for d in range(2):
                        last = pe.matmul(bank[0:rows, 0:kn], qT[:, 2 * h + d, off:off + rows], kT[:, 2 * h + d, k0:k0 + kn],
                                         start=d == 0, stop=d == 1)
                    last.then_inc(d_filled, 1)
            n = DJ["ktok"]
            for t, (off, rows) in enumerate(TILES):
                for q in range(2):
                    bank = d_bank(n)
                    for b in range(4):
                        last = pe.transpose(bank[0:rows, b * P:(b + 1) * P], kT[:, 4 * q + b, off:off + rows], ident)
                    last.then_inc(d_filled, 1)
                    n += 1

            def mix_job(h, k):
                return DJ["mix"] + (5 * h + (0 if k == 0 else k + (1 if h < H - 1 else 0)) if k == 0 or h < H - 1
                                    else 5 * h + k)

            def mix_order():
                n = DJ["mix"]
                for h in range(H + 1):
                    if h < H:
                        yield n, h, 0
                        n += 1
                    if h >= 1:
                        for k in range(1, 5):
                            yield n, h - 1, k
                            n += 1

            pe.wait_ge(d_emptied, DJ["qkt"] + 12)
            swT_job = {}
            for n, h, k in mix_order():
                bank = d_bank(n)
                sT = swT[:, h % 2, :]
                if k == 0:
                    swT_job[h] = n
                    for dst, t, src in ((0, 0, 0), (128, 1, 128), (256, 1, 256)):
                        last = pe.transpose(bank[:, dst:dst + P], wts[:, h, src:src + P], ident)
                    last = pe.transpose(bank[0:NS, 384:448], wts[0:NS, h, 384:448], ident[0:NS, 0:NS])
                elif k == 1:
                    pe.wait_ge(d_emptied, swT_job[h] + 1)
                    last = pe.matmul(bank[:, 0:VA], sT[:, 0:P], v_aug[:, 0, h, :], start=True, stop=True)
                elif k == 2:
                    pe.matmul(bank[:, 0:VA], sT[:, P:2 * P], v_aug[:, 0, h, :], start=True, stop=False)
                    last = pe.matmul(bank[:, 0:VA], sT[:, 2 * P:3 * P], v_aug[:, 1, h, :], start=False, stop=True)
                elif k == 3:
                    for d in range(2):
                        last = pe.matmul(bank[0:NS, 0:VA], qT[:, 2 * h + d, NP_:TOK], C_aug[:, 2 * h + d, :],
                                         start=d == 0, stop=d == 1)
                else:
                    last = pe.matmul(bank[0:NS, 0:VA], sT[0:NS, 384:448], v_aug[0:NS, 2, h, :], start=True, stop=True)
                last.then_inc(d_filled, 1)
            for b in range(KD):
                bank = d_bank(DJ["state"] + b)
                for t in range(2):
                    last = pe.matmul(bank[:, 0:VA], kw[:, t, b * P:(b + 1) * P], v_aug[:, t, b // 2, :], start=t == 0, stop=t == 1)
                last.then_inc(d_filled, 1)
            for b in range(KD):
                bank = d_bank(DJ["state"] + KD + b)
                pe.matmul(bank[:, 0:VA], kw[0:NS, 2, b * P:(b + 1) * P], v_aug[0:NS, 2, b // 2, :], start=True, stop=True
                          ).then_inc(d_filled, 1)
            n = DJ["yT"]
            for t, (off, rows) in enumerate(TILES):
                pe.wait_ge(y_ready, 4 * (t + 1))
                for q in range(2):
                    bank = d_bank(n)
                    for b in range(4):
                        h, c = (4 * q + b) // 2, b % 2
                        last = pe.transpose(bank[:, b * P:b * P + rows], hn[0:rows, t, h, c * P:(c + 1) * P], ident[0:rows, 0:rows])
                    last.then_inc(d_filled, 1)
                    n += 1
            pe.wait_ge(d_emptied, DJ["yT"] + 6)
            for c in range(2):
                token_major("out", "out", c, uT, TILES, base=3 * c)

            def memory(l):
                mt = ((0, P), (P, P))
                transposes(f"memT{l}", lambda t, rows, b: u[0:rows, t, b * P:(b + 1) * P], mt, 2 * l, mu_ready)
                pe.wait_ge(d_emptied, DJ[f"memT{l}"] + 4)
                for c in range(2):
                    token_major(f"memk{l}", f"memk{l}", c, memT, mt, base=2 * c)
                for c in range(2):
                    token_major(f"memv{l}", f"memv{l}", c, memT, mt, base=2 * c)
                pe.wait_ge(d_emptied, DJ[f"memk{l}"] + 4)
                for j in range(4):
                    bank = d_bank(DJ[f"memkT{l}"] + j)
                    for b in range(2):
                        for t in range(2):
                            last = pe.transpose(bank[:, b * MEM + t * P:b * MEM + (t + 1) * P],
                                                mk[:, t, (2 * j + b) * P:(2 * j + b + 1) * P], ident)
                    last.then_inc(d_filled, 1)

            def attend(l, norm):
                u_transposes(f"xn{l}", norm)
                pe.wait_ge(d_emptied, DJ[f"xn{l}"] + 6)
                feature_major(f"xq{l}", f"xq{l}", 2)
                pe.wait_ge(cache_loaded, 32 * (l + 1))
                for h in range(H):
                    pe.wait_ge(d_emptied, DJ[f"xq{l}"] + 2 * h + 2)
                    for t, (off, rows) in enumerate(TILES):
                        bank = d_bank(DJ[f"sc{l}"] + 3 * h + t)
                        kk = mkT if t < 2 else skT
                        for d in range(2):
                            last = pe.matmul(bank[0:rows, 0:MEM], qT[:, 2 * h + d, off:off + rows], kk[:, 2 * h + d, :],
                                             start=d == 0, stop=d == 1)
                        last.then_inc(d_filled, 1)
                for n, h, k in av_order(l):
                    bank = d_bank(n)
                    if k < 2:
                        pe.wait_ge(p_ready, 12 * l + 3 * h + 3)
                        for t, (off, rows) in enumerate(TILES):
                            last = pe.transpose(bank[:, off:off + rows], probs[0:rows, 3 * h + t, k * P:(k + 1) * P],
                                                ident[0:rows, 0:rows])
                    else:
                        pe.wait_ge(d_emptied, av_pt_done(l, h))
                        c0 = (2 * h + k - 2) * P
                        for vv, a, z in ((mv_, 0, NP_), (sv_, NP_, TOK)):
                            for m in range(2):
                                last = pe.matmul(bank[:, a:z], vv[:, m, c0:c0 + P], probsT[:, h % 2, m, a:z],
                                                 start=m == 0, stop=m == 1)
                    last.then_inc(d_filled, 1)
                pe.wait_ge(d_emptied, DJ[f"av{l}"] + 16)
                for c in range(2):
                    token_major(f"xo{l}", f"xo{l}", c, uT, TILES, base=3 * c)

            def split_block(l, i, per, block, bank, quarters=range(4)):
                for q in quarters:
                    pe.wait_ge(w_lo_ready, at(i, 4 * per, split_base(l, block) + q + 1))
                    for kk in range(2):
                        k = 2 * q + kk
                        hi, lo = wq[:, q, 0, kk, :], wq[:, q, 1, kk, :]
                        pe.matmul(bank[:, 0:TOK], hi, uT_hi[:, k, :], start=k == 0, stop=False)
                        pe.matmul(bank[:, 0:TOK], hi, uT_lo[:, k, :], start=False, stop=False)
                        last = pe.matmul(bank[:, 0:TOK], lo, uT_hi[:, k, :], start=False, stop=k == KD - 1)
                    last.then_inc(quarter_used if q < 3 else a_filled, 1)

            def v_block(l, i, r, last_block=False):
                pe.wait_ge(p_split, i * 8 + (NB * l + r + 1))
                pe.wait_ge(v_split, i * 8 + (NB * l + r + 1))
                ph, vh = phl[:, r % 2], vhl[:, r % 2]
                for t in range(2):
                    hi, lo = ph[:, t * P:(t + 1) * P], ph[:, TOK + NS + t * P:TOK + NS + (t + 1) * P]
                    for lhs, part in ((hi, 0), (hi, 1), (lo, 0)):
                        for n in range(2):
                            pe.matmul(psum[:, 2 + 2 * t + n, :], lhs, vh[:, part, n * 512:(n + 1) * 512],
                                      start=False, stop=False, skip_group_check=True)
                for part in range(2):
                    for n in range(2):
                        last = pe.matmul(psum[:, 6 + n, :], ph[:, NP_:NP_ + P], vh[:, part, n * 512:(n + 1) * 512],
                                         start=False, stop=False, skip_group_check=True)
                last.then_inc(v_summed, 1)

            def peer(l, norm):
                u_transposes(f"fn{l}", norm)
                pe.wait_ge(d_emptied, DJ[f"fn{l}"] + 6)
                pe.wait_ge(keys_loaded, 16 * (l + 1))
                with pe.Fori(0, 2) as i:
                    for kind, m in PQ_ORDER:
                        if kind == "q":
                            split_block(l, i, 8, m, a_bank(AJ[f"pq{l}"] + m, i, 8))
                        else:
                            pe.wait_ge(a_emptied, i * 8 + (AJ[f"pq{l}"] + m + 1))
                            bank = d_bank(DJ[f"pq{l}"] + m, i, 8)
                            for t, (off, rows) in enumerate(TILES):
                                last = pe.matmul(bank[0:rows, t * P:(t + 1) * P], pqT[:, m, off:off + rows],
                                                 keysT[:, i * 8 + m, :], start=True, stop=True)
                            last.then_inc(d_filled, 1)
                pe.wait_ge(a_emptied, AJ[f"up{l}"])
                with pe.Fori(0, AHEAD // 4) as i:
                    for r in range(4):
                        split_block(l, i, 4, HP + r, a_bank(AJ[f"up{l}"] + r, i, 4))
                for t, (off, rows) in enumerate(TILES):
                    pe.wait_ge(picked_ready, 3 * l + t + 1)
                    bank = d_bank(DJ[f"slot{l}"] + t)
                    for a in range(3):
                        last = pe.transpose(bank[:, a * P:a * P + rows], picked[0:rows, t, a, :], ident[0:rows, 0:rows])
                    last.then_inc(d_filled, 1)
                pe.wait_ge(a_emptied, AJ[f"gb{l}"])
                pe.wait_ge(d_emptied, DJ[f"slot{l}"] + 3)
                with pe.Fori(0, 5) as i:
                    for r in range(4):
                        n = AJ[f"gb{l}"] + 5 * r
                        pe.wait_ge(a_emptied, i * 20 + (n + U_JOB - 10 + 1))
                        for g in range(4):
                            split_block(l, i, 4, HP + AHEAD + r, psum[:, GB_UBANKS[r % 2], :], quarters=(g,))
                            pe.wait_ge(a_emptied, i * 20 + (n + G_JOBS[g] - 5 + 1))
                            bank = psum[:, ABANKS[g], :]
                            pe.wait_ge(oh_ready, i * 64 + (TOK * l + 16 * r + 4 * g + 4))
                            for q in range(4):
                                s = (4 * g + q) % 8
                                last = pe.matmul(bank[:, q * P:(q + 1) * P], ohJ[:, s, :], oh[:, s, :], start=True, stop=True)
                            last.then_inc(a_filled, 1)
                pe.wait_ge(a_emptied, AJ[f"ux{l}"])
                for r in range(XU):
                    split_block(l, None, 0, HP + LAG - XU + r, a_bank(AJ[f"ux{l}"] + r))
                pe.wait_ge(zero_ready, l + 1)
                pe.wait_ge(a_emptied, AJ[f"uv{l}"])
                for n in range(6):
                    last = pe.matmul(psum[:, 2 + n, :], phl[:, 0, 0:P], vhl[:, 0, 0, 0:512], start=True, stop=False,
                                     skip_group_check=True)
                last.then_inc(v_summed, 2)
                with pe.Fori(0, UV) as i:
                    for r in range(8):
                        pe.wait_ge(a_emptied, i * 8 + (AJ[f"uv{l}"] + r - 1))
                        split_block(l, i, 8, HP + LAG + r, psum[:, r % 2, :])
                        v_block(l, i, r)
                with pe.Fori(UV, 16) as i:
                    for r in range(8):
                        v_block(l, i, r)
                pe.wait_ge(acc_emptied, 4 * (l + 1))
                for n in range(2):
                    pe.wait_ge(acc_copied, 2 * l + n + 1)
                    pe.matmul(d_bank(DJ[f"fold{l}"] + n)[0:NS, :], fold, acc_tmp[:, n, :], start=True, stop=True
                              ).then_inc(d_filled, 1)

            memory(0)
            attend(0, 1)
            peer(0, 2)
            pe.wait_ge(pool_loaded, 32)
            pe.wait_ge(prefix_loaded, 16)
            pe.wait_ge(u_ready, 12)
            for b in range(KD):
                bank = d_bank(DJ["pool"] + b)
                for s in range(2):
                    pe.matmul(bank[:, 0:NP_], u[:, s, b * P:(b + 1) * P], bandp[:, b // 2, s, :], start=s == 0, stop=s == 1)
                pe.matmul(bank[:, NP_:TOK], u[:, 2, b * P:(b + 1) * P], bands_[:, b // 2, :], start=True, stop=True
                          ).then_inc(d_filled, 1)
            for g in range(4):
                pe.wait_ge(d_emptied, DJ["pool"] + 2 * g + 2)
                for t, (off, rows) in enumerate(TILES):
                    bank = d_bank(DJ["pool"] + KD + 3 * g + t)
                    for c in range(2):
                        last = pe.matmul(bank[0:rows, 0:DH], plT[:, 2 * g + c, off:off + rows], wpool[:, g, c, :],
                                         start=c == 0, stop=c == 1)
                    last.then_inc(d_filled, 1)
            memory(1)
            attend(1, 4)
            peer(1, 5)

        @block.scalar
        def _(act):
            step = Chain(act, act_step)

            def norm_stats(norm, index, extra=()):
                for sm, v in extra:
                    act.wait_ge(sm, v)
                for t, (off, rows) in enumerate(TILES):
                    sm, v = x_ready(norm, t)
                    act.wait_ge(sm, v)
                    step(act.activation(u[0:rows, t, :], x[0:rows, t, :], ACT.Square, accum_out=ss[0:rows, t:t + 1]))
                    act.activation(std[0:rows, t:t + 1], ss[0:rows, t:t + 1], ACT.Sqrt, bias=eps_c[0:rows, :], scale=1.0 / D
                                   ).then_inc(std_ready, 1)

            def mem_stats(l):
                if l == 0:
                    act.wait_ge(y_ready, 12)
                else:
                    act.wait_ge(d_filled, DJ["pool"] + 8)
                    act.wait_ge(pool_stored, 32)
                act.wait_ge(mem_loaded, 16 * (l + 1))
                for t in range(2):
                    step(act.activation(u[:, t, :], memx[:, t, :], ACT.Square, accum_out=mss[:, t:t + 1]))
                    act.activation(mstd[:, t:t + 1], mss[:, t:t + 1], ACT.Sqrt, bias=eps_c, scale=1.0 / D
                                   ).then_inc(mstd_ready, 1)

            act.wait_ge(init_done, 1)
            norm_stats("mix0", 0)
            for c in range(2):
                for t, (off, rows) in enumerate(TILES):
                    n = AJ["o"] + 3 * c + t
                    act.wait_ge(a_filled, n + 1)
                    act.activation(u[0:rows, t, c * 512:(c + 1) * 512], psum[0:rows, ABANKS[n % 4], :], ACT.Sigmoid
                                   ).then_inc(a_emptied, 1)
            act.wait_ge(gate_abs, 1)
            step(act.activation(R4[0:H, 2, :], R4[0:H, 2, :], ACT.Exp, scale=-1.0))
            act.activation(R4[0:H, 2, :], R4[0:H, 2, :], ACT.Ln, bias=one_c[0:H, :]).then_inc(gate_ln, 1)
            act.wait_ge(m_ready, 1)
            for h in range(H):
                for t, (off, rows) in enumerate(TILES):
                    a, z = ((0, 128), (128, 384), (384, 448))[t]
                    act.activation(wts[0:rows, h, a:z], wts[0:rows, h, a:z], ACT.Exp, bias=negm[0:rows, t, h:h + 1]
                                   ).then_inc(w_ready, 1)
                if h == 0:
                    act.activation(ainter, idiff, ACT.Exp).then_inc(mexp_ready, 1)
                    act.activation(emneg, negm, ACT.Exp).then_inc(mexp_ready, 1)
                    act.wait_ge(ws_arg, 1)
                    act.activation(wscol, wsarg, ACT.Exp).then_inc(ws_ready, 1)
                    act.activation(gstate, garg, ACT.Exp).then_inc(ws_ready, 1)
            act.wait_ge(var_ready, 1)
            act.activation(sdev, mv[:, :, :, 1], ACT.Sqrt, bias=eps_c).then_inc(sdev_ready, 1)

            def attend(l):
                for j in range(3 * H):
                    rows = TILES[j % 3][1]
                    act.wait_ge(mx_ready, 12 * l + j + 1)
                    act.activation(probs[0:rows, j, :], probs[0:rows, j, :], ACT.Exp, bias=nmx[0:rows, j:j + 1],
                                   accum_out=rsum[0:rows, j:j + 1]).then_inc(p_exp, 1)

            def peer(l):
                def upper_parts(i, per, block, raw, m, load, prev_job, first=False, quarters=range(4)):
                    if load is not None and 0 in quarters:
                        c = load[1]
                        act.wait_ge(w_loaded[c % 2], at(i, load[0], 16 * (c // 2 + 1)))
                    for q in quarters:
                        if not first:
                            if q < 3:
                                act.wait_ge(quarter_used, at(i, 3 * per, 3 * (split_base(l, block) // 4 - 1) + q + 1))
                            else:
                                act.wait_ge(a_filled, at(i, prev_job[0], prev_job[1] + 1))
                        act.activation(wq[:, q, 0], quarter(raw, m, q), ACT.Copy).then_inc(w_hi_ready, 1)

                def upper_pq(m, prev):
                    c = WC[f"pq{l}"] + m // 4
                    upper_parts(None, 0, m, W[c % 2], m % 4, (0, c) if m % 4 == 0 else None, (0, prev), first=l == 0 and m == 0)

                def upper_u(i, per, r, at_block, prev, prev_per, quarters=range(4)):
                    b = at_block + r
                    upper_parts(i, per, HP + b, Ublk[(b // 2) % 2], b % 2,
                                (4 * per, WC[f"U{l}"] + b // 2) if b % 2 == 0 else None, (prev_per, prev),
                                quarters=quarters)

                upper_pq(0, AJ["pq1"] - 1 if l == 0 else AJ["uv0"] + NB - LAG - 1)
                for m in range(HP):
                    n = AJ[f"pq{l}"] + m
                    if m + 1 < HP:
                        upper_pq(m + 1, n)
                    else:
                        upper_u(None, 0, 0, 0, n, 0)
                    act.wait_ge(a_filled, n + 1)
                    act.activation(pqT[:, m % 8, :], psum[:, ABANKS[n % 4], 0:TOK], ACT.Copy).then_inc(a_emptied, 1)
                act.wait_ge(mem_stored, 32 * (l + 1))
                with act.Fori(0, AHEAD // 4) as i:
                    for r in range(4):
                        n = AJ[f"up{l}"] + r
                        upper_u(i, 4, r + 1, 0, n, 4)
                        act.wait_ge(a_filled, i * 4 + (n + 1))
                        act.activation(act4[:, i, r, :], psum[:, ABANKS[n % 4], 0:TOK], ACT.Gelu).then_inc(a_emptied, 1)
                for t, (off, rows) in enumerate(TILES):
                    act.wait_ge(top_ready, 3 * l + t + 1)
                    act.activation(picked[0:rows, t, 2, :], picked[0:rows, t, 2, :], ACT.Exp).then_inc(exp_ready, 1)
                def spread(i, first=False):
                    for r in range(4):
                        n = AJ[f"gb{l}"] + 5 * r
                        if not (first and r < 2):
                            act.wait_ge(g_stored[r % 2], i * 32 + 16 * (NGC // 2 * l + r // 2))
                        for g in range(4):
                            upper_u(i, 4, r + 1, AHEAD, n + U_JOB, 20, quarters=(g,))
                            if g == 3:
                                act.wait_ge(a_filled, i * 20 + (n + U_JOB + 1))
                                act.activation(act4[:, i + AHEAD // 4, r, :], psum[:, GB_UBANKS[r % 2], 0:TOK], ACT.Gelu
                                               ).then_inc(a_emptied, 1)
                            gn = n + G_JOBS[g]
                            act.wait_ge(a_filled, i * 20 + (gn + 1))
                            act.activation(g_stage[r % 2][:, :, 4 * g:4 * g + 4].rearrange("p i t -> p t i"),
                                           psum[:, ABANKS[g], :].rearrange("p (t i) -> p t i", i=NK), ACT.Copy
                                           ).then_inc(a_emptied, 1)

                spread(0, first=l == 0)
                with act.Fori(1, 5) as i:
                    spread(i)

                for r in range(XU):
                    n = AJ[f"ux{l}"] + r
                    upper_u(None, 0, r + 1, LAG - XU, n, 0)
                    act.wait_ge(a_filled, n + 1)
                    act.activation(act4[:, (LAG - XU) // 4, r, :], psum[:, ABANKS[n % 4], 0:TOK], ACT.Gelu).then_inc(a_emptied, 1)

                def vhi(i, r):
                    if r % 2 == 0:
                        act.wait_ge(v_loaded[(r // 2) % 2], i * 32 + 16 * (32 * l + r // 4 + 1))
                    act.wait_ge(v_summed, i * 8 + ((NB + 2) * l + r + 1))
                    act.activation(vhl[:, r % 2, 0, :], v_raw[(r // 2) % 2][:, r % 2, :], ACT.Copy).then_inc(vhi_ready, 1)

                def uv_round(i, last=False):
                    for r in range(8):
                        n = AJ[f"uv{l}"] + r
                        vhi(i, r)
                        if not (last and r == 7):
                            upper_u(i, 8, r + 1, LAG, n, 8)
                        act.wait_ge(a_filled, i * 8 + (n + 1))
                        act.wait_ge(p_split, i * 8 + (NB * l + r + 1))
                        act.activation(act8[:, i % (LAG // 8), r, :], psum[:, r % 2, 0:TOK], ACT.Gelu).then_inc(a_emptied, 1)

                with act.Fori(0, UV - 1) as i:
                    uv_round(i)
                uv_round(UV - 1, last=True)
                with act.Fori(UV, 16) as i:
                    for r in range(8):
                        vhi(i, r)

            mem_stats(0)
            norm_stats("xn0", 1, extra=((d_filled, DJ["memT0"] + 4),))
            attend(0)
            norm_stats("fn0", 2)
            peer(0)
            norm_stats("mix1", 3)
            mem_stats(1)
            norm_stats("xn1", 4, extra=((d_filled, DJ["memT1"] + 4),))
            attend(1)
            norm_stats("fn1", 5)
            peer(1)
            norm_stats("final", 6)

        @block.vector
        def _(dve):
            step = Chain(dve, dve_step)
            row_step = Chain(dve, dve_row_step)

            def full(n, i=None, per=0):
                dve.wait_ge(d_filled, n + 1 if i is None else i * per + (n + 1))
                return psum[:, DBANKS[n % 4], :]

            def scale_rows(norm, index, gidx):
                dve.wait_ge(gain_loaded[gidx % 2], 16 * (gidx // 2 + 1))
                for t, (off, rows) in enumerate(TILES):
                    dve.wait_ge(std_ready, 3 * index + t + 1)
                    step(dve.reciprocal(rstd[0:rows, t:t + 1], std[0:rows, t:t + 1]))
                    dve.scalar_tensor_tensor(out=u[0:rows, t, :], in0=x[0:rows, t, :], scalar=rstd[0:rows, t:t + 1],
                                             in1=gain[0:rows, gidx % 2, :], op0=ALU.mult, op1=ALU.mult).then_inc(u_ready, 1)

            def empty_transposes(stage, dstT, tiles):
                n = DJ[stage]
                for t, (off, rows) in enumerate(tiles):
                    for q in range(2):
                        bank = full(n).rearrange("p (b c) -> p b c", c=P)
                        dve.tensor_copy(dstT[:, 4 * q:4 * q + 4, off:off + rows], bank[:, :, 0:rows]).then_inc(d_emptied, 1)
                        n += 1

            def add_to_x(stage):
                for c in range(2):
                    for t, (off, rows) in enumerate(TILES):
                        dst = x[0:rows, t, c * 512:(c + 1) * 512]
                        dve.tensor_tensor(dst, full(DJ[stage] + 3 * c + t)[0:rows, :], dst, ALU.add).then_inc(d_emptied, 1)

            step(dve.memset(small[:], 1.0))
            step(dve.memset(eps_c, EPS))
            step(dve.memset(arena[:, 19176:19496], 0.0))
            step(dve.memset(hn[:, 2], 1.0))
            step(dve.memset(v_aug[:, :, :, DH:VA], 1.0))
            dve.memset(mv, 1.0).then_inc(init_done, 1)
            dve.wait_ge(init_done, 1)
            dve.wait_ge(x_loaded, 48)
            scale_rows("mix0", 0, 0)
            empty_transposes("mixn0", uT, TILES)
            with dve.Fori(0, 2) as i:
                for m in range(8):
                    bank = full(DJ["qk"] + m, i, 8)
                    dve.tensor_copy(view(arena, 0, 2, KD, TOK)[:, i, m, :], bank[:, 0:TOK]).then_inc(d_emptied, 1)
            for c in range(2):
                for t, (off, rows) in enumerate(TILES):
                    bank = full(DJ["v"] + 3 * c + t)
                    dve.tensor_copy(v_aug[0:rows, t, 2 * c:2 * c + 2, 0:DH], bank[0:rows, :].rearrange("p (h e) -> p h e", e=DH)
                                    ).then_inc(d_emptied, 1)
            dve.wait_ge(mix_loaded, 64)
            for g in range(2):
                dve.tensor_scalar(R4[0:H, g, :], full(DJ["gates"] + g)[0:H, 0:TOK], b4[0:H, g:g + 1], None, ALU.add
                                  ).then_inc(d_emptied, 1)
            dve.wait_ge(d_emptied, DJ["gates"] + 2)
            dve.scalar_tensor_tensor(out=R4[0:H, 2, :], in0=R4[0:H, 1, :], scalar=-1.0, in1=R4[0:H, 1, :], op0=ALU.mult, op1=ALU.max
                                     ).then_inc(gate_abs, 1)
            step(dve.tensor_scalar(R4[0:H, 3, :], R4[0:H, 1, :], 0.0, None, ALU.min))
            dve.wait_ge(gate_ln, 1)
            step(dve.tensor_tensor(R4[0:H, 3, :], R4[0:H, 3, :], R4[0:H, 2, :], ALU.subtract))
            step(dve.memset(R4[0:H, 2, :], 1.0))
            for a, z in ((0, NP_), (NP_, TOK)):
                step(dve.tensor_tensor_scan(out=R4[0:H, 4, a:z], data0=R4[0:H, 2, a:z], data1=R4[0:H, 3, a:z], initial=0.0,
                                            op0=ALU.mult, op1=ALU.add))
            dve.tensor_tensor(R4[0:H, 5, :], R4[0:H, 0, :], R4[0:H, 4, :], ALU.subtract).then_inc(gate_rows, 1)
            bank = full(DJ["cols"])
            step(dve.tensor_copy(br[:, 0:2, :], bank[:, 0:16].rearrange("p (t c) -> p t c", c=8)))
            dve.tensor_copy(br[0:NS, 2, :], bank[0:NS, 16:24]).then_inc(d_emptied, 1)
            dve.wait_ge(d_emptied, DJ["cols"] + 1)
            for h in range(H):
                bank = full(DJ["rb"] + h)
                b0, b1, b2 = br[:, 0, h:h + 1], br[:, 1, h:h + 1], br[0:NS, 2, h:h + 1]
                dve.scalar_tensor_tensor(out=wts[:, h, 0:128], in0=bank[:, 0:128], scalar=b0, in1=tri_m, op0=ALU.add, op1=ALU.add)
                dve.tensor_scalar(wts[:, h, 128:256], bank[:, 0:128], b1, None, ALU.add)
                dve.scalar_tensor_tensor(out=wts[:, h, 256:384], in0=bank[:, 128:256], scalar=b1, in1=tri_m, op0=ALU.add, op1=ALU.add)
                dve.scalar_tensor_tensor(out=wts[0:NS, h, 384:448], in0=bank[0:NS, NP_:TOK], scalar=b2, in1=tri_m[0:NS, 0:NS],
                                         op0=ALU.add, op1=ALU.add).then_inc(d_emptied, 1)
            dve.wait_ge(d_emptied, DJ["rb"] + H)
            for h in range(H):
                for t, (off, rows) in enumerate(TILES):
                    a, z = ((0, 128), (128, 384), (384, 448))[t]
                    ins = dve.tensor_reduce(rmax[0:rows, t, h:h + 1], wts[0:rows, h, a:z], AX.X, ALU.max)
            step(ins)
            step(dve.tensor_tensor(inter, br[:, :, 0:H], m0c, ALU.add))
            step(dve.tensor_copy(bm[:, :, 0:H], br[:, :, 0:H]))
            step(dve.tensor_tensor(bm[:, :, H:2 * H], rmax, inter, ALU.max))
            step(dve.tensor_tensor(idiff, inter, bm[:, :, H:2 * H], ALU.subtract))
            dve.tensor_scalar(negm, bm[:, :, H:2 * H], -1.0, None, ALU.mult).then_inc(m_ready, 1)
            bank = full(DJ["sel"])
            dve.tensor_copy(selev, bank[:, 0:16]).then_inc(d_emptied, 1)
            dve.wait_ge(d_emptied, DJ["sel"] + 1)
            se = selev.rearrange("p (g a h) -> p g a h", g=2, a=2)
            step(dve.tensor_tensor(blm, se[:, :, 0, :], se[:, :, 1, :], ALU.subtract))
            step(dve.tensor_tensor(wsarg[:, 0:2, :], br[:, 0:2, H:2 * H], blm[:, 0:1, :].to_broadcast([P, 2, H]), ALU.add))
            step(dve.tensor_tensor(wsarg[:, 2, :], br[:, 2, H:2 * H], blm[:, 1, :], ALU.add))
            dve.tensor_tensor(garg, blm[:, 1, :], m0c[:, 2, :], ALU.add).then_inc(ws_arg, 1)
            for h in range(H):
                for t, (off, rows) in enumerate(TILES):
                    a, z = ((0, 128), (128, 384), (384, 448))[t]
                    bank = full(DJ["qkt"] + 3 * h + t)
                    dve.wait_ge(w_ready, 3 * h + t + 1)
                    dve.scalar_tensor_tensor(out=wts[0:rows, h, a:z], in0=bank[0:rows, 0:z - a], scalar=DH ** -0.5,
                                             in1=wts[0:rows, h, a:z], op0=ALU.mult, op1=ALU.mult).then_inc(d_emptied, 1)
            n = DJ["ktok"]
            dve.wait_ge(ws_ready, 2)
            for t, (off, rows) in enumerate(TILES):
                for q in range(2):
                    bank = full(n)
                    for hh in range(2):
                        h = 2 * q + hh
                        ins = dve.tensor_scalar(kw[0:rows, t, h * DH:(h + 1) * DH], bank[0:rows, hh * DH:(hh + 1) * DH],
                                                wscol[0:rows, t, h:h + 1], DH ** -0.5, ALU.mult, ALU.mult)
                    ins.then_inc(d_emptied, 1)
                    n += 1
            dve.wait_ge(mexp_ready, 2)
            n = DJ["mix"]
            for hh in range(H + 1):
                if hh < H:
                    bank = full(n)
                    dve.tensor_copy(swT[:, hh % 2, 0:384], bank[:, 0:384])
                    dve.tensor_copy(swT[0:NS, hh % 2, 384:448], bank[0:NS, 384:448]).then_inc(d_emptied, 1)
                    n += 1
                if hh >= 1:
                    h = hh - 1
                    for t in range(2):
                        dve.tensor_copy(hn[:, t, h, :], full(n)[:, 0:VA]).then_inc(d_emptied, 1)
                        n += 1
                    dve.tensor_scalar(qc_tmp[0:NS, h % 2, :], full(n)[0:NS, 0:VA], ainter[0:NS, 2, h:h + 1], None, ALU.mult
                                      ).then_inc(d_emptied, 1)
                    n += 1
                    dve.wait_ge(d_emptied, n)
                    dve.tensor_tensor(hn[0:NS, 2, h, :], full(n)[0:NS, 0:VA], qc_tmp[0:NS, h % 2, :], ALU.add).then_inc(d_emptied, 1)
                    n += 1
            dve.wait_ge(d_emptied, n)
            step(dve.scalar_tensor_tensor(out=rinv, in0=hn[:, :, :, DH], scalar=-1.0, in1=hn[:, :, :, DH], op0=ALU.mult, op1=ALU.max))
            step(dve.tensor_tensor(rinv, rinv, emneg, ALU.max))
            step(dve.reciprocal(rinv, rinv))
            for t, (off, rows) in enumerate(TILES):
                for h in range(H):
                    ins = dve.tensor_scalar(hn[0:rows, t, h, 0:DH], hn[0:rows, t, h, 0:DH], rinv[0:rows, t, h:h + 1], None, ALU.mult)
            step(ins)
            for t, (off, rows) in enumerate(TILES):
                for h in range(H):
                    ins = dve.bn_stats(bnst[0:rows, 4 * t + h, :], hn[0:rows, t, h, 0:DH])
            step(ins)
            for t, (off, rows) in enumerate(TILES):
                for h in range(H):
                    ins = dve.bn_aggr(mv[0:rows, t, h, :], bnst[0:rows, 4 * t + h, :])
            ins.then_inc(var_ready, 1)
            for b in range(KD):
                dve.tensor_copy(C_new[:, b, :], full(DJ["state"] + b)[:, 0:VA]).then_inc(d_emptied, 1)
            for b in range(KD):
                dve.scalar_tensor_tensor(out=C_aug[:, b, :], in0=C_aug[:, b, :], scalar=gstate[:, b // 2:b // 2 + 1],
                                         in1=full(DJ["state"] + KD + b)[:, 0:VA], op0=ALU.mult, op1=ALU.add
                                         ).then_inc(d_emptied, 1)
            dve.wait_ge(sdev_ready, 1)
            step(dve.reciprocal(srec, sdev))
            dve.wait_ge(a_emptied, AJ["o"] + 6)
            dve.wait_ge(gain_loaded[1], 16)
            dve.wait_ge(var_ready, 1)
            for t, (off, rows) in enumerate(TILES):
                for h in range(H):
                    y = hn[0:rows, t, h, 0:DH]
                    ins = dve.scalar_tensor_tensor(out=y, in0=y, scalar=mv[0:rows, t, h, 0:1],
                                                   in1=gain[0:rows, 1, h * DH:(h + 1) * DH], op0=ALU.subtract, op1=ALU.mult)
                step(ins)
                for h in range(H):
                    y = hn[0:rows, t, h, 0:DH]
                    dve.scalar_tensor_tensor(out=y, in0=y, scalar=srec[0:rows, t, h:h + 1],
                                             in1=u[0:rows, t, h * DH:(h + 1) * DH], op0=ALU.mult, op1=ALU.mult
                                             ).then_inc(y_ready, 1)
            empty_transposes("yT", uT, TILES)
            add_to_x("out")

            def memory(l):
                gidx = 2 if l == 0 else 7
                dve.wait_ge(gain_loaded[gidx % 2], 16 * (gidx // 2 + 1))
                for t in range(2):
                    dve.wait_ge(mstd_ready, 2 * l + t + 1)
                    step(dve.reciprocal(mrstd[:, t:t + 1], mstd[:, t:t + 1]))
                    dve.scalar_tensor_tensor(out=u[:, t, :], in0=memx[:, t, :], scalar=mrstd[:, t:t + 1], in1=gain[:, gidx % 2, :],
                                             op0=ALU.mult, op1=ALU.mult).then_inc(mu_ready, 1)
                if l == 0:
                    dve.wait_ge(state_stored, 64)
                empty_transposes(f"memT{l}", memT, ((0, P), (P, P)))
                for name, dst in ((f"memk{l}", mk), (f"memv{l}", mv_)):
                    for c in range(2):
                        for t in range(2):
                            dve.tensor_copy(dst[:, t, c * 512:(c + 1) * 512], full(DJ[name] + 2 * c + t)).then_inc(d_emptied, 1)
                for j in range(4):
                    dve.tensor_copy(mkT[:, 2 * j:2 * j + 2, :], full(DJ[f"memkT{l}"] + j).rearrange("p (b m) -> p b m", m=MEM)
                                    ).then_inc(d_emptied, 1)

            def attend(l, norm):
                scale_rows(f"xn{l}", norm, 3 if l == 0 else 8)
                empty_transposes(f"xn{l}", uT, TILES)
                for m in range(8):
                    dve.tensor_copy(qT[:, m, :], full(DJ[f"xq{l}"] + m)[:, 0:TOK]).then_inc(d_emptied, 1)

                def normalise(j):
                    rows = TILES[j % 3][1]
                    dve.wait_ge(p_exp, 12 * l + j + 1)
                    step(dve.reciprocal(rinv_p[0:rows, j:j + 1], rsum[0:rows, j:j + 1]))
                    dve.tensor_scalar(probs[0:rows, j, :], probs[0:rows, j, :], rinv_p[0:rows, j:j + 1], None, ALU.mult
                                      ).then_inc(p_ready, 1)

                for j in range(3 * H):
                    rows = TILES[j % 3][1]
                    n = DJ[f"sc{l}"] + j
                    dve.tensor_scalar(probs[0:rows, j, :], full(n)[0:rows, 0:MEM], DH ** -0.5, None, ALU.mult).then_inc(d_emptied, 1)
                    dve.wait_ge(d_emptied, n + 1)
                    dve.tensor_reduce(nmx[0:rows, j:j + 1], probs[0:rows, j, :], AX.X, ALU.max, negate=True).then_inc(mx_ready, 1)
                    if j >= 2:
                        normalise(j - 2)
                normalise(3 * H - 2)
                normalise(3 * H - 1)
                for n, h, k in av_order(l):
                    if k < 2:
                        dve.tensor_copy(probsT[:, h % 2, k, :], full(n)[:, 0:TOK]).then_inc(d_emptied, 1)
                    else:
                        dve.tensor_copy(uT[:, 2 * h + k - 2, :], full(n)[:, 0:TOK]).then_inc(d_emptied, 1)
                add_to_x(f"xo{l}")

            def best16(r, values):
                def each(op):
                    for t, (off, rows) in enumerate(TILES):
                        row_step.after(2)
                        row_step.mark(op(t, rows))

                each(lambda t, rows: dve.max(v16[0:rows, r, t, 0:8], values[0:rows, t, :]))
                each(lambda t, rows: dve.max_index(i16[0:rows, r, t, 0:8], v16[0:rows, r, t, 0:8], values[0:rows, t, :]))
                n = values.shape[-1]
                each(lambda t, rows: dve.match_replace(spare[0:rows, t, 0:n], v16[0:rows, r, t, 0:8], values[0:rows, t, :],
                                                       -3.0e38))
                each(lambda t, rows: dve.max(v16[0:rows, r, t, 8:16], spare[0:rows, t, 0:n]))
                each(lambda t, rows: dve.max_index(i16[0:rows, r, t, 8:16], v16[0:rows, r, t, 8:16], spare[0:rows, t, 0:n]))

            def choose(l):
                with dve.Fori(0, HP // 4) as i:
                    for r in range(4):
                        row_step.after(15)
                        bank = full(DJ[f"pq{l}"] + r, i, 4)[:, 0:3 * P].rearrange("p (t n) -> p t n", n=P)
                        row_step.mark(dve.tensor_copy(cur[:, r % 2, 0:2, :], bank[:, 0:2, :]))
                        row_step.mark(dve.tensor_copy(cur[0:NS, r % 2, 2, :], bank[0:NS, 2, :]))
                        row_step.after(0)
                        dve.sem_inc(d_emptied, 1)
                        best16(r, cur[:, r % 2])
                    row_step.after(0)
                    row_step.mark(dve.tensor_copy(sval[:, bass.ds(i * 4, 4)], v16))
                    row_step.mark(dve.tensor_copy(sidx[:, bass.ds(i * 4, 4)], i16))
                    row_step.restart()
                sv2 = sval.rearrange("p (h a) t k -> p h a t k", a=2)
                si2 = sidx16.rearrange("p (h a) t k -> p h a t k", a=2)
                with dve.Fori(0, PH) as i:
                    for t, (off, rows) in enumerate(TILES):
                        row_step.mark(dve.tensor_tensor(cand[0:rows, t, :].rearrange("p (a b) -> p a b", b=TOPK),
                                                        sv2[0:rows, i, 0, t, :].unsqueeze(2).to_broadcast([rows, TOPK, TOPK]),
                                                        sv2[0:rows, i, 1, t, :].unsqueeze(1).to_broadcast([rows, TOPK, TOPK]),
                                                        ALU.add))
                    best16(0, cand)
                    row_step.after(0)
                    row_step.mark(dve.tensor_copy(top[:, i], v16[:, 0]))
                    row_step.mark(dve.tensor_copy(tpos.bitcast(U32)[:, i], i16[:, 0]))
                    row_step.restart()
                for t, (off, rows) in enumerate(TILES):
                    gate = picked[0:rows, t, 2, :].rearrange("p (h k) -> p h k", k=TOPK)
                    dve.tensor_tensor(gate, top[0:rows, :, t, :], top[0:rows, :, t, 0:1].to_broadcast([rows, PH, TOPK]),
                                      ALU.subtract).then_inc(top_ready, 1)
                for t in range(3):
                    bits = cand.bitcast(U32)[:, t, :].rearrange("p (a h k) -> p a h k", a=2, k=TOPK)
                    tp = tpos.bitcast(U32)[:, :, t, :]
                    dve.tensor_scalar(bits[:, 0], tp, 4, None, ALU.logical_shift_right)
                    ins = dve.tensor_scalar(bits[:, 1], tp, 15, None, ALU.bitwise_and)
                step(ins)
                dve.tensor_copy(iota16, iota[:, 0:TOPK])
                dve.tensor_copy(sidx16, sidx)
                step(dve.tensor_copy(pij, cand.bitcast(U32).rearrange("p t (a h k) -> p t a h k", a=2, k=TOPK)))
                for t, (off, rows) in enumerate(TILES):
                    shape = [rows, 4, TOPK, TOPK]
                    for a in range(2):
                        for q in range(2):
                            hs = slice(4 * q, 4 * q + 4)
                            ins = dve.tensor_tensor(eq[0:rows, q], pij[0:rows, t, a, hs, :].unsqueeze(3).to_broadcast(shape),
                                                    iota16[0:rows].unsqueeze(1).unsqueeze(1).to_broadcast(shape),
                                                    ALU.is_equal)
                        step(ins)
                        for q in range(2):
                            hs = slice(4 * q, 4 * q + 4)
                            ins = dve.tensor_tensor(eq[0:rows, q], eq[0:rows, q],
                                                    si2[0:rows, hs, a, t, :].unsqueeze(2).to_broadcast(shape), ALU.mult)
                        step(ins)
                        for q in range(2):
                            hs = slice(4 * q, 4 * q + 4)
                            out = picked[0:rows, t, a, :].rearrange("p (h k) -> p h k", k=TOPK)[:, hs, :]
                            ins = dve.tensor_reduce(out, eq[0:rows, q], AX.X, ALU.add)
                        step(ins)

            def peer(l, norm):
                scale_rows(f"fn{l}", norm, 4 if l == 0 else 9)
                jobs = [(t, q) for t in range(3) for q in range(2)]
                for k in range(len(jobs) + 1):
                    if k < len(jobs):
                        (off, rows), q = TILES[jobs[k][0]], jobs[k][1]
                        bank = full(DJ[f"fn{l}"] + k).rearrange("p (b c) -> p b c", c=P)
                        step.mark(dve.tensor_copy(uT_hi[:, 4 * q:4 * q + 4, off:off + rows], bank[:, :, 0:rows]))
                    if k:
                        (off, rows), q = TILES[jobs[k - 1][0]], jobs[k - 1][1]
                        step.after(1 if k < len(jobs) else 0)
                        bank = psum[:, DBANKS[(DJ[f"fn{l}"] + k - 1) % 4], :].rearrange("p (b c) -> p b c", c=P)
                        dst = slice(4 * q, 4 * q + 4), slice(off, off + rows)
                        dve.tensor_tensor(uT_lo[:, dst[0], dst[1]], bank[:, :, 0:rows], uT_hi[:, dst[0], dst[1]].bitcast(F32),
                                          ALU.subtract).then_inc(d_emptied, 1)
                step(dve.memset(v16, 0.0))
                step(dve.memset(i16.bitcast(F32), 0.0))
                choose(l)
                for t, (off, rows) in enumerate(TILES):
                    dve.wait_ge(exp_ready, 3 * l + t + 1)
                    gate = picked[0:rows, t, 2, :].rearrange("p (h k) -> p h k", k=TOPK)
                    step(dve.tensor_reduce(sume[0:rows, t, 0:PH], gate, AX.X, ALU.add))
                    step(dve.reciprocal(sume[0:rows, t, PH:2 * PH], sume[0:rows, t, 0:PH]))
                    dve.tensor_tensor(gate, gate, sume[0:rows, t, PH:2 * PH].unsqueeze(2).to_broadcast([rows, PH, TOPK]), ALU.mult
                                      ).then_inc(picked_ready, 1)
                for t, (off, rows) in enumerate(TILES):
                    bank = full(DJ[f"slot{l}"] + t)[:, 0:3 * P].rearrange("p (a c) -> p a c", c=P)
                    dve.tensor_copy(slots[:, :, off:off + rows], bank[:, :, 0:rows]).then_inc(d_emptied, 1)
                dve.wait_ge(d_emptied, DJ[f"slot{l}"] + 3)
                with dve.Fori(0, 5) as i:
                    for c in range(64):
                        r, g, q = c // 16, (c % 16) // 4, c % 4
                        if q == 0:
                            before = 5 * r + G_JOBS[g - 2] if g >= 2 else 5 * (r - 1) + G_JOBS[g + 2]
                            dve.wait_ge(a_filled, i * 20 + (AJ[f"gb{l}"] + before + 1))
                            dve.tensor_tensor(ohJ[:, 4 * (g % 2):4 * (g % 2) + 4, :], iota.unsqueeze(1).to_broadcast([P, 4, P]),
                                              slots[:, 1, bass.ds(i * 64 + c, 4)].unsqueeze(2).to_broadcast([P, 4, P]),
                                              ALU.is_equal)
                        ti, tg = slots[:, 0, bass.ds(i * 64 + c, 1)], slots[:, 2, bass.ds(i * 64 + c, 1)]
                        dve.tensor_scalar(oh[:, c % 8, :], iota, ti, tg, ALU.is_equal, ALU.mult).then_inc(oh_ready, 1)
                step(dve.memset(phl[:, 0, 0:P].bitcast(F32), 0.0))
                dve.memset(vhl[:, 0, 0, 0:512].bitcast(F32), 0.0).then_inc(zero_ready, 1)
                dve.wait_ge(zero_ready, l + 1)

                def product_parts(i, r):
                    if r == 0:
                        dve.wait_ge(g_loaded, i * 16 + 16 * (16 * l + 1))
                    dve.wait_ge(a_emptied, i * 8 + (AJ[f"uv{l}"] + r + 1 - LAG))
                    dve.wait_ge(v_summed, i * 8 + ((NB + 2) * l + r + 1))
                    p, ph = pf[:, r % 2, :], phl[:, r % 2, :]
                    step(dve.tensor_tensor(p.rearrange("p (c t) -> p c t", t=GC),
                                           act8[:, i % (LAG // 8), r, :].rearrange("p (c t) -> p c t", t=GC),
                                           g_ring[:, i % 2, :, r * GC:(r + 1) * GC], ALU.mult))
                    step(dve.tensor_copy(ph[:, 0:TOK], p))
                    hi = ph[:, 0:TOK].bitcast(F32)
                    dve.tensor_tensor(ph[:, TOK:TOK + NS], p[:, NP_:TOK], hi[:, NP_:TOK], ALU.subtract)
                    dve.tensor_tensor(ph[:, TOK + NS:2 * TOK], p[:, 0:NP_], hi[:, 0:NP_], ALU.subtract).then_inc(p_split, 1)
                    dve.wait_ge(vhi_ready, i * 8 + (NB * l + r + 1))
                    dve.tensor_tensor(vhl[:, r % 2, 1, :], v_raw[(r // 2) % 2][:, r % 2, :],
                                      vhl[:, r % 2, 0, :].bitcast(F32), ALU.subtract).then_inc(v_split, 1)

                with dve.Fori(0, 16) as i:
                    step.loop(i, 16)
                    for r in range(8):
                        product_parts(i, r)
                step.done(16)
                dve.wait_ge(v_summed, (NB + 2) * (l + 1))
                for n in range(2):
                    dve.tensor_copy(acc_tmp[:, n, :], psum[:, 6 + n, :]).then_inc(acc_copied, 1)
                for t in range(2):
                    for n in range(2):
                        dst = x[:, t, n * 512:(n + 1) * 512]
                        dve.tensor_tensor(dst, psum[:, 2 + 2 * t + n, :], dst, ALU.add).then_inc(acc_emptied, 1)
                for n in range(2):
                    dst = x[0:NS, 2, n * 512:(n + 1) * 512]
                    dve.tensor_tensor(dst, full(DJ[f"fold{l}"] + n)[0:NS, :], dst, ALU.add).then_inc(d_emptied, 1)

            memory(0)
            attend(0, 1)
            peer(0, 2)
            dve.memset(u[NS:P, 2, :], 0.0).then_inc(prefix_clear, 1)
            scale_rows("mix1", 3, 5)
            for b in range(KD):
                dve.tensor_copy(plT[:, b, :], full(DJ["pool"] + b)[:, 0:TOK]).then_inc(d_emptied, 1)
            dve.wait_ge(gain_loaded[0], 16 * 4)
            for g in range(4):
                for t, (off, rows) in enumerate(TILES):
                    n = DJ["pool"] + KD + 3 * g + t
                    if 3 * g + t >= 2:
                        dve.wait_ge(pooled, 3 * g + t - 1)
                    tmp, dst = pool_tmp[0:rows, (3 * g + t) % 2, :], x[0:rows, t, g * DH:(g + 1) * DH]
                    dve.tensor_tensor(tmp, full(n)[0:rows, 0:DH], gain[0:rows, 0, g * DH:(g + 1) * DH], ALU.mult
                                      ).then_inc(d_emptied, 1)
                    dve.wait_ge(d_emptied, n + 1)
                    dve.tensor_tensor(dst, dst, tmp, ALU.add).then_inc(pooled, 1)
            memory(1)
            attend(1, 4)
            peer(1, 5)
            scale_rows("final", 6, 10)


def av_order(l):
    n = DJ[f"av{l}"]
    for h in range(H + 1):
        for k in ((0, 1) if h < H else ()):
            yield n, h, k
            n += 1
        for k in ((2, 3) if h >= 1 else ()):
            yield n, h - 1, k
            n += 1


def av_pt_done(l, h):
    return max(n for n, hh, k in av_order(l) if hh == h and k < 2) + 1


def split_base(l, block):
    return 4 * ((HP + NB) * l + block)


PQ_ORDER = [("q", 0)] + [x for m in range(7) for x in (("q", m + 1), ("s", m))] + [("s", 7)]


OUTPUTS = {"y_p": (NP_, D), "y_s": (NS, D), "Cn_p": (D, VA), "m_p": (1, H), "pool_p": (POOLST, D),
           "mem_k": (2, MEM, D), "mem_v": (2, MEM, D), "Cn_s": (D, VA), "m_s": (1, H), "pool_s": (POOLST, D)}


def chunks(w):
    return np.ascontiguousarray(w.reshape(KD, P, -1, 512).transpose(2, 1, 0, 3))


def layout(inp):
    a = {k: np.asarray(v) for k, v in inp.items()}
    w_in = a["w_mlstm_in"][0]
    t = {
        "x_prompt": a["x_prompt"], "x_sample": a["x_sample"],
        "w_qk": chunks(w_in[:, :2 * D]), "w_vo": chunks(w_in[:, 2 * D:4 * D]),
        "w_gates": w_in[:, 4 * D:].reshape(KD, P, 2 * H).transpose(1, 0, 2),
        "b_gates": np.stack([a["b_mlstm_i"][0], a["b_mlstm_f"][0]], axis=1),
        "state_m": a["state_mlstm_m"][0, 0], "state_Cn": np.concatenate([a["state_mlstm_C"].reshape(D, DH), a["state_mlstm_n"].reshape(D, 1)], axis=1),
        "state_pool": a["state_pool"][0, 0],
        "w_out": chunks(a["w_mlstm_out"][0]),
        "mem_prompt": a["mem_prompt"][0],
        "cache_kT": a["cache_mem_k"].reshape(2, MEM, D).transpose(0, 2, 1),
        "cache_v": a["cache_mem_v"].reshape(2, MEM, D),
        "gains": np.stack([a["g_mix"][0], a["g_mlstm_head"][0], a["g_mem"][0], a["g_xattn"][0], a["g_ffn"][0],
                           a["g_mix"][1], a["s_pool"][0], a["g_mem"][1], a["g_xattn"][1], a["g_ffn"][1], a["g_final"]]),
        "w_pool": a["w_pool"][0].reshape(4, 2, P, DH).transpose(2, 0, 1, 3),
        "peer_keys": a["peer_keys"].reshape(2, HP, NK, P).transpose(0, 3, 1, 2),
        "peer_u": a["peer_u"].reshape(2, NB // 2, 2, P, KD, P).transpose(0, 1, 5, 2, 4, 3),
        "peer_v": a["peer_v"].reshape(2, NB // 2, 2, P, D).transpose(0, 1, 3, 2, 4),
        "constants": constants(), "bands": bands(),
    }
    for name, key in (("w_xk", "w_xk"), ("w_xv", "w_xv"), ("w_xq", "w_xq"), ("w_xo", "w_xo"), ("w_pq", "w_peer_q")):
        t[name] = np.stack([chunks(a[key][l]) for l in range(2)])
    return {k: np.ascontiguousarray(v) for k, v in t.items()}


def results(r):
    def state(cn, m):
        return (cn[:, 0:DH].reshape(1, 1, H, DH, DH), cn[:, DH].reshape(1, 1, H, DH), m.reshape(1, 1, H))

    return (r["y_p"].reshape(1, NP_, D), r["y_s"].reshape(1, NS, D), *state(r["Cn_p"], r["m_p"]),
            r["pool_p"].reshape(1, 1, POOLST, D), r["mem_k"].reshape(2, 1, MEM, H, DH), r["mem_v"].reshape(2, 1, MEM, H, DH),
            *state(r["Cn_s"], r["m_s"]), r["pool_s"].reshape(1, 1, POOLST, D))


def kernel(**inputs):
    import concourse.bacc as bacc
    from concourse.bass_utils import run_bass_kernel_spmd

    nc = bacc.Bacc("TRN2", target_bir_lowering=False, num_devices=1)
    arrays = layout(inputs)
    t_in = {k: nc.dram_tensor(k, v.shape, F32, kind="ExternalInput").ap() for k, v in arrays.items()}
    t_out = {k: nc.dram_tensor(k, shape, F32, kind="ExternalOutput").ap() for k, shape in OUTPUTS.items()}
    build(nc, t_in, t_out)
    r = run_bass_kernel_spmd(nc, [arrays], core_ids=[0])
    return results(r.results[0])
```

```python
from contextlib import ExitStack

import numpy as np
import concourse.bass as bass
import concourse.mybir as mybir

F32, F32R, BF16, U32 = mybir.dt.float32, mybir.dt.float32r, mybir.dt.bfloat16, mybir.dt.uint32
ALU, ACT, AX = mybir.AluOpType, mybir.ActivationFunctionType, mybir.AxisListType

P = 128
D = 1024
KD = D // P
TOK = 320
TILES = ((0, 128), (128, 128), (256, 64))
NP_ = 256
NS = 64
H = 4
DH = D // H
VA = DH + 1
MEM = 256
PH = 8
HP = 2 * PH
NK = 128
TOPK = 16
NB = NK
LAG = 56
GB = 20
XU = 4
AHEAD = LAG - GB - XU
UV = (NB - LAG) // 8
GC = 16
NGC = TOK // GC
EPS = 1e-6
NEG = -1e30
POOLW = (2, 4, 8, 16)
POOLST = 15

STAGES = [
    ("mixn0", 6, 0), ("qk", 16, 0), ("gates", 2, 0), ("v", 6, 0), ("cols", 1, 0), ("rb", 4, 0),
    ("o", 0, 6), ("sel", 1, 0), ("qkt", 12, 0), ("ktok", 6, 0), ("mix", 20, 0), ("yT", 6, 0),
    ("state", 16, 0), ("out", 6, 0),
    ("memT0", 4, 0), ("memk0", 4, 0), ("memv0", 4, 0), ("memkT0", 4, 0),
    ("xn0", 6, 0), ("xq0", 8, 0), ("sc0", 12, 0), ("av0", 16, 0), ("xo0", 6, 0),
    ("fn0", 6, 0), ("pq0", HP, HP), ("up0", 0, AHEAD), ("slot0", 3, 0), ("gb0", 0, 5 * GB), ("ux0", 0, XU), ("uv0", 0, NB - LAG),
    ("fold0", 2, 0),
    ("pool", 20, 0),
    ("memT1", 4, 0), ("memk1", 4, 0), ("memv1", 4, 0), ("memkT1", 4, 0),
    ("xn1", 6, 0), ("xq1", 8, 0), ("sc1", 12, 0), ("av1", 16, 0), ("xo1", 6, 0),
    ("fn1", 6, 0), ("pq1", HP, HP), ("up1", 0, AHEAD), ("slot1", 3, 0), ("gb1", 0, 5 * GB), ("ux1", 0, XU), ("uv1", 0, NB - LAG),
    ("fold1", 2, 0),
]
DJ, AJ = {}, {}
_d = _a = 0
for _n, _dj, _aj in STAGES:
    DJ[_n], AJ[_n] = _d, _a
    _d, _a = _d + _dj, _a + _aj
DJ["end"], AJ["end"] = _d, _a
TURNED = {}
_n_turned = 0
for _n, _dj, _aj in STAGES:
    if _n in ("mixn0", "yT") or _n[:-1] in ("memT", "xn", "fn"):
        TURNED[_n] = _n_turned
        _n_turned += _dj
G_JOBS, U_JOB = (0, 1, 2, 4), 3
GB_UBANKS = (2, 3)
DBANKS = (2, 3, 4, 5)
ABANKS = (0, 1, 6, 7)

WEIGHTS = [("qk", 4), ("vo", 4), ("out", 2), ("memk0", 2), ("memv0", 2), ("xq0", 2), ("xo0", 2), ("pq0", 4),
           ("U0", 64), ("memk1", 2), ("memv1", 2), ("xq1", 2), ("xo1", 2), ("pq1", 4), ("U1", 64)]
WC = {}
_c = 0
for _n, _k in WEIGHTS:
    WC[_n] = _c
    _c += _k



def job_after(name, local):
    if name == "qk" or name[:2] == "xq":
        return "d", DJ[name] + 4 * (local + 1)
    if name == "vo":
        return ("d", DJ["v"] + 3 * (local + 1)) if local < 2 else ("a", AJ["o"] + 3 * (local - 1))
    if name[:3] == "mem":
        return "d", DJ[name] + 2 * (local + 1)
    if name[:2] == "pq":
        return "a", AJ[name] + 4 * (local + 1)
    return "d", DJ[name] + 3 * (local + 1)


def by_feature(name):
    return name == "qk" or name[1] == "q"


SPLIT = {}
_lo = _used = 0
_prev = None
for _n, _k in WEIGHTS:
    if _n[0] == "U":
        SPLIT[_n, 0] = _lo, _used, _prev
        _lo, _used, _prev = _lo + 4 * NB, _used + 3 * NB, ("a", AJ["uv" + _n[1]] + NB - LAG)
        continue
    for _i in range(_k):
        SPLIT[_n, _i] = _lo, _used, _prev
        _lo, _used, _prev = _lo + 16, _used + (12 if by_feature(_n) else 15), job_after(_n, _i)


def split_base(l, block):
    return SPLIT[f"pq{l}", 0][0] + 4 * block


def used_base(l, block):
    return SPLIT[f"pq{l}", 0][1] + 3 * block


GAINS = ("mix0", "head", "mem0", "xn0", "fn0", "mix1", "spool", "mem1", "xn1", "fn1", "final")


def tri():
    return np.where(np.tril(np.ones((P, P), bool)), np.float32(0), np.float32(NEG)).astype(np.float32)


def constants():
    eye = np.eye(P, dtype=np.float32)
    iota = np.broadcast_to(np.arange(P, dtype=np.float32), (P, P))
    sel4 = np.zeros((P, H, P), np.float32)
    for h in range(H):
        sel4[h, h] = 1
    last_p = np.zeros((P, P), np.float32)
    last_p[P - 1] = 1
    last_s = np.zeros((P, P), np.float32)
    last_s[NS - 1] = 1
    fold = np.concatenate([np.eye(NS), np.eye(NS)]).astype(np.float32)
    return np.concatenate([eye, iota, tri(), sel4.reshape(P, -1), last_p, last_s, fold], axis=1)


def bands():
    p = np.zeros((P, 4, 2, NP_), np.float32)
    s = np.zeros((P, 4, NS), np.float32)
    for g, w in enumerate(POOLW):
        for t in range(NP_):
            for a in range(max(0, t - w + 1), t + 1):
                p[a % P, g, a // P, t] += 1.0 / min(t + 1, w)
            p[t % P, g, t // P, t] -= 1
        for t in range(NS):
            for a in range(t - w + 1, t + 1):
                s[a if a >= 0 else NS + POOLST + a, g, t] += 1.0 / w
            s[t, g, t] -= 1
    return np.concatenate([p.reshape(P, -1), s.reshape(P, -1)], axis=1)


class Chain:

    def __init__(self, eng, sem):
        self.eng, self.sem, self.n, self.i, self.per, self.base = eng, sem, 0, None, 0, 0

    def __call__(self, ins):
        self.n += 1
        ins.then_inc(self.sem, 1)
        self.eng.wait_ge(self.sem, self.n if self.i is None else self.i * self.per + self.n)

    def after(self, back):
        if self.n > back:
            self.eng.wait_ge(self.sem, self.n - back)

    def mark(self, ins):
        self.n += 1
        ins.then_inc(self.sem, 1)

    def restart(self):
        self.after(0)
        self.eng.sem_clear(self.sem)
        self.n = 0

    def loop(self, i, per):
        self.i, self.per, self.base = i, per, self.n

    def done(self, iterations):
        assert self.n - self.base == self.per, (self.n - self.base, self.per)
        self.n, self.i = self.base + iterations * self.per, None


def build(nc, t_in, t_out):
    with ExitStack() as ctx:
        def sb(name, cols, dt=F32):
            return ctx.enter_context(nc.sbuf_tensor(name, [P, cols], dt))

        def sem(name):
            return ctx.enter_context(nc.semaphore(name))

        g_dram = [nc.dram_tensor(f"gates_{l}", (NGC, P, NK // 8, 8 * GC), F32, kind="Internal").ap() for l in range(2)]

        x_sb = sb("x_sb", 3 * D)
        uT_split = sb("uT_split", 2 * KD * TOK, F32R)
        w_split = sb("w_split", 4 * 2 * 2 * P, F32R)
        w_ring = sb("w_ring", 2 * KD * 512)
        p_hl = sb("p_hl", 2 * 2 * TOK, F32R)
        v_hl = sb("v_hl", 2 * 2 * D, F32R)
        gains = sb("gain_rows", 2 * D)
        cst = sb("cst", 3 * P + H * P + 2 * P + NS)
        shared = sb("shared", 9 * P + 3 * TOK + 2 * TOK)
        small = sb("small", 64)
        arena = sb("arena", 23104)
        psum = ctx.enter_context(nc.psum_tensor("psum", [P, 8, 512], F32))

        def view(t, off, *dims):
            n = int(np.prod(dims))
            a = t[:, off:off + n]
            if len(dims) == 2:
                return a.rearrange("p (a b) -> p a b", b=dims[1])
            if len(dims) == 3:
                return a.rearrange("p (a b c) -> p a b c", b=dims[1], c=dims[2])
            if len(dims) == 4:
                return a.rearrange("p (a b c d) -> p a b c d", b=dims[1], c=dims[2], d=dims[3])
            return a

        x = view(x_sb, 0, 3, D)
        uT = view(shared, 0, KD, TOK)
        uT_hi, uT_lo = view(uT_split, 0, KD, TOK), view(uT_split, KD * TOK, KD, TOK)
        wq_row = view(w_split, 0, 4, 2, 2 * P)
        wq = view(w_split, 0, 4, 2, 2, P)
        W = [view(w_ring, s * KD * 512, KD, 512) for s in range(2)]
        Ublk = [view(w_ring, s * KD * 512, 2, KD, P) for s in range(2)]
        v_raw = [view(w_ring, s * KD * 512 + 2 * D, 2, D) for s in range(2)]
        g_stage = [view(w_ring, s * KD * 512 + 2 * D, NK, GC) for s in range(2)]
        gain = view(gains, 0, 2, D)
        ident, iota, tri_m = cst[:, 0:P], cst[:, P:2 * P], cst[:, 2 * P:3 * P]
        sel4 = view(cst, 3 * P, H, P)
        last_p, last_s = cst[:, 7 * P:8 * P], cst[:, 8 * P:9 * P]
        fold = cst[:, 9 * P:9 * P + NS]
        ss, std, rstd = small[:, 0:3], small[:, 3:6], small[:, 6:9]
        mss, mstd, mrstd = small[:, 9:11], small[:, 11:13], small[:, 13:15]
        eps_c, one_c = small[:, 15:16], small[:, 16:17]
        nmx, rsum, rinv_p = small[:, 17:29], small[:, 29:41], small[:, 41:53]
        u = view(arena, 20032, 3, D)
        act4 = view(arena, 0, LAG // 4, 4, TOK)
        act8 = view(arena, 0, LAG // 8, 8, TOK)
        g_ring = view(arena, LAG * TOK, 2, NGC, 8 * GC)
        qT, kT = view(arena, 0, KD, TOK), view(arena, 2560, KD, TOK)
        kw = view(arena, 5120, 3, D)
        v_aug = view(arena, 8192, 3, H, VA)
        wts = view(arena, 11280, H, 448)
        swT = view(arena, 13072, 2, 448)
        hn = view(arena, 13968, 3, H, VA)
        C_new = view(arena, 0, KD, VA)
        C_aug = view(arena, 17056, KD, VA)
        R4 = view(arena, 13968, 6, TOK)
        wg = view(arena, 19112, KD, 2 * H)
        br, bm = view(arena, 19176, 3, 2 * H), view(arena, 19200, 3, 2 * H)
        m0c, inter, rmax, negm = (view(arena, 19224 + 12 * k, 3, H) for k in range(4))
        idiff, ainter, emneg, wsarg = (view(arena, 19272 + 12 * k, 3, H) for k in range(4))
        wscol, rinv, sdev, srec = (view(arena, 19320 + 12 * k, 3, H) for k in range(4))
        selev, blm, garg, gstate = arena[:, 19368:19384], view(arena, 19384, 2, H), arena[:, 19392:19396], arena[:, 19396:19400]
        mv = view(arena, 19400, 3, H, 2)
        nmean = view(arena, 19496, 3, H)
        bnst = view(arena, 19424, 3 * H, 6)
        qc_tmp = view(arena, 2560, 2, VA)
        b4 = arena[:, 19754:19756]
        mkT, mv_ = view(arena, 2560, KD, MEM), view(arena, 4608, 2, D)
        mk = view(arena, 6656, 2, D)
        skT, sv_ = view(arena, 8704, KD, MEM), view(arena, 10752, 2, D)
        probs = view(arena, 12800, H * 3, MEM)
        probsT = view(arena, 15872, 2, 2, TOK)
        memx = view(arena, 17152, 2, D)
        wpool = view(arena, 0, 4, 2, DH)
        bandp, bands_ = view(arena, 2048, 4, 2, NP_), view(arena, 4096, 4, NS)
        plT = view(arena, 4352, KD, TOK)
        pool_tmp = view(arena, 8192, 2, DH)
        pqT = view(arena, 0, KD, TOK)
        keysT = view(arena, 2560, HP, NK)
        top0 = AHEAD * TOK
        cur = view(arena, top0, 2, 3, NK)
        spare = view(arena, top0 + 768, 3, 2 * NK)
        v16, i16 = view(arena, top0 + 1536, 4, 3, TOPK), view(arena, top0 + 1728, 4, 3, TOPK).bitcast(U32)
        eq = arena[:, top0:top0 + 1024].bitcast(BF16).rearrange("p (q h k c) -> p q h k c", q=2, k=TOPK, c=TOPK)
        cand = view(arena, top0 + 2048, 3, TOPK * TOPK)
        sval, sidx = view(arena, top0 + 2816, HP, 3, TOPK), view(arena, top0 + 3584, HP, 3, TOPK)
        top, tpos = view(arena, top0 + 4352, PH, 3, TOPK), view(arena, top0 + 4736, PH, 3, TOPK)
        pij = arena[:, top0 + 5120:top0 + 5504].bitcast(BF16).rearrange("p (t a h k) -> p t a h k", t=3, a=2, k=TOPK)
        sidx16 = arena[:, top0 + 5504:top0 + 5888].bitcast(BF16).rearrange("p (g t k) -> p g t k", t=3, k=TOPK)
        iota16 = arena[:, top0 + 5936:top0 + 5944].bitcast(BF16)
        sume = view(arena, top0 + 5888, 3, 2 * PH)
        picked = view(shared, 0, 3, 3, P)
        oh = view(shared, 0, 8, P)
        ohJ = view(arena, LAG * TOK, 8, P)
        slots = view(shared, 9 * P, 3, TOK)
        acc_tmp = view(shared, 0, 2, 512)
        phl = view(p_hl, 0, 2, 2 * TOK)
        vhl = view(v_hl, 0, 2, 2, D)
        pf = view(shared, 9 * P + 3 * TOK, 2, TOK)

        x_loaded = [sem(f"x_loaded{t}") for t in range(3)]
        ident_loaded, tables_loaded, mix_loaded = sem("ident_loaded"), sem("tables_loaded"), sem("mix_loaded")
        w_loaded = [sem(f"w_loaded{s}") for s in range(2)]
        gain_loaded = [sem(f"gain_loaded{s}") for s in range(2)]
        mem_loaded, cache_loaded, pool_loaded, prefix_loaded, keys_loaded = (
            sem(n) for n in ("mem_loaded", "cache_loaded", "pool_loaded", "prefix_loaded", "keys_loaded"))
        v_loaded = [sem(f"v_loaded{s}") for s in range(2)]
        g_loaded = sem("g_loaded")
        g_stored = [sem(f"g_stored{s}") for s in range(2)]
        state_stored, mem_stored, pool_stored, y_stored = (
            sem(n) for n in ("state_stored", "mem_stored", "pool_stored", "y_stored"))
        d_filled, d_emptied, a_filled, a_emptied = (sem(n) for n in ("d_filled", "d_emptied", "a_filled", "a_emptied"))
        dve_step, dve_row_step, act_step = sem("dve_step"), sem("dve_row_step"), sem("act_step")
        init_done, std_ready, u_ready, mstd_ready, mu_ready = (
            sem(n) for n in ("init_done", "std_ready", "u_ready", "mstd_ready", "mu_ready"))
        gate_abs, gate_ln, gate_rows, m_ready, w_ready, mexp_ready = (
            sem(n) for n in ("gate_abs", "gate_ln", "gate_rows", "m_ready", "w_ready", "mexp_ready"))
        ws_arg, ws_ready, var_ready, sdev_ready, y_ready = (
            sem(n) for n in ("ws_arg", "ws_ready", "var_ready", "sdev_ready", "y_ready"))
        mx_ready, p_ready, pooled = (sem(n) for n in ("mx_ready", "p_ready", "pooled"))
        top_ready, exp_ready, picked_ready, oh_ready = (
            sem(n) for n in ("top_ready", "exp_ready", "picked_ready", "oh_ready"))
        w_hi_ready, w_lo_ready, quarter_used = (sem(n) for n in ("w_hi_ready", "w_lo_ready", "quarter_used"))
        vhi_ready, v_split, p_split, v_summed, acc_emptied, acc_copied = (
            sem(n) for n in ("vhi_ready", "v_split", "p_split", "v_summed", "acc_emptied", "acc_copied"))
        turned_hi = sem("turned_hi")
        norm_ready, z_ready = sem("norm_ready"), sem("z_ready")
        prefix_clear, zero_ready, u32_ready = sem("prefix_clear"), sem("zero_ready"), sem("u32_ready")

        block = ctx.enter_context(nc.Block())

        def at(i, per, n):
            return n if i is None else i * per + n

        filled_sem = {"d": d_filled, "a": a_filled}

        def chunk_quarter(name, local, i, q, part):
            raw = W[(WC[name] + local) % 2]
            if by_feature(name):
                return raw[:, 2 * q:2 * q + 2, bass.ds(i * P, P)], wq[:, q, part]
            return raw[:, i * 2 + q // 2, (q % 2) * 2 * P:(q % 2 + 1) * 2 * P], wq_row[:, q, part]

        def turned(stage, tiles):
            for k, (off, rows, q) in enumerate((off, rows, q) for off, rows in tiles for q in range(2)):
                n = DJ[stage] + k
                bank = psum[:, DBANKS[n % 4], :].rearrange("p (b c) -> p b c", c=P)[:, :, 0:rows]
                yield n, TURNED[stage] + k, bank, uT_hi[:, 4 * q:4 * q + 4, off:off + rows], uT_lo[:, 4 * q:4 * q + 4, off:off + rows]

        def lower_group(eng, name, local, i):
            for q in range(4):
                raw, dst = chunk_quarter(name, local, i, q, 1)
                eng.wait_ge(w_hi_ready, i * 4 + (SPLIT[name, local][0] + q + 1))
                eng.tensor_tensor(dst, raw, chunk_quarter(name, local, i, q, 0)[1].bitcast(F32), ALU.subtract
                                  ).then_inc(w_lo_ready, 1)

        def quarter(block, m, q):
            return block[:, 2 * q:2 * q + 2, m * P:(m + 1) * P] if block.shape[-1] == 512 else block[:, m, 2 * q:2 * q + 2, :]

        def x_ready(norm, t):
            if norm == "mix0":
                return x_loaded[t], 16
            if norm in ("xn0", "xn1"):
                return (d_emptied, DJ["out"] + 4 + t) if norm == "xn0" else (pooled, 9 + t + 1)
            if norm in ("fn0", "fn1"):
                return d_emptied, DJ["xo" + norm[2]] + 4 + t
            l = 0 if norm == "mix1" else 1
            return (acc_emptied, 4 * l + 2 * t + 2) if t < 2 else (d_emptied, DJ[f"fold{l}"] + 2)

        @block.sync
        def _(sp):
            for k, (off, rows) in enumerate(TILES):
                src = t_in["x_prompt"][0, off:off + rows] if k < 2 else t_in["x_sample"][0]
                sp.dma_start(x[0:rows, k, :], src).then_inc(x_loaded[k], 16)

            flat = [(n, k) for n, cnt in WEIGHTS for k in range(cnt)]

            def chunk(stage, local, src):
                c = WC[stage] + local
                if c >= 2:
                    name, k = flat[c - 2]
                    sp.wait_ge(w_lo_ready, SPLIT[name, 0][0] + (16 * (k + 1) if name[0] != "U" else 8 * (k + 1)))
                    if name[0] == "U":
                        sp.wait_ge(v_split, NB * (int(name[1]) + 1))
                sp.dma_start(W[c % 2], src).then_inc(w_loaded[c % 2], 16)

            def stage(name, src):
                for k in range(src.shape[0]):
                    chunk(name, k, src[k])

            stage("qk", t_in["w_qk"])
            stage("vo", t_in["w_vo"])
            stage("out", t_in["w_out"])
            for l in range(2):
                if l == 0:
                    sp.wait_ge(state_stored, 64)
                else:
                    sp.wait_ge(p_split, NB)
                    sp.dma_start(wpool, t_in["w_pool"]).then_inc(pool_loaded, 16)
                    sp.dma_start(arena[:, 2048:4352], t_in["bands"]).then_inc(pool_loaded, 16)
                    sp.wait_ge(prefix_clear, 1)
                    sp.dma_start(u[NS:NS + POOLST, 2, :], t_in["state_pool"]).then_inc(prefix_loaded, 16)
                sp.dma_start(memx, t_in["mem_prompt"].rearrange("(b p) d -> p b d", p=P)).then_inc(mem_loaded, 16)
                chunk(f"memk{l}", 0, t_in["w_xk"][l][0])
                sp.dma_start(skT, t_in["cache_kT"][l].rearrange("(b p) m -> p b m", p=P)).then_inc(cache_loaded, 16)
                sp.dma_start(sv_, t_in["cache_v"][l].rearrange("(b p) d -> p b d", p=P)).then_inc(cache_loaded, 16)
                chunk(f"memk{l}", 1, t_in["w_xk"][l][1])
                stage(f"memv{l}", t_in["w_xv"][l])
                stage(f"xq{l}", t_in["w_xq"][l])
                stage(f"xo{l}", t_in["w_xo"][l])
                stage(f"pq{l}", t_in["w_pq"][l])
                U, V = t_in["peer_u"][l], t_in["peer_v"][l]
                for k in range(2):
                    sp.wait_ge(w_lo_ready, split_base(l, 4 * (3 + k)))
                    sp.dma_start(Ublk[k], U[k]).then_inc(w_loaded[k], 16)
                ubase = split_base(l, HP)
                with sp.Fori(0, (LAG - XU) // 4) as i:
                    for s in range(2):
                        sp.wait_ge(w_lo_ready, i * 16 + (ubase + 8 * (s + 1)))
                        sp.dma_start(Ublk[s], U[i * 2 + (2 + s)]).then_inc(w_loaded[s], 16)

                def u_load(i, q):
                    sp.wait_ge(w_lo_ready, i * 32 + (ubase + 4 * LAG + 8 * (q + 1)))
                    sp.dma_start(Ublk[q % 2], U[i * 4 + (LAG // 2 + 2 + q)]).then_inc(w_loaded[q % 2], 16)

                def v_load(i, q):
                    sp.wait_ge(v_split, i * 8 + (NB * l + 2 * q + 2))
                    sp.dma_start(v_raw[q % 2], V[i * 4 + (2 + q)]).then_inc(v_loaded[q % 2], 16)

                def g_load(i):
                    sp.wait_ge(p_split, i * 8 + NB * l)
                    sp.wait_ge(g_loaded, i * 16 + 16 * (16 * l + 1))
                    sp.dma_start(g_ring[:, (i + 1) % 2], g_dram[l][:, :, i + 1].rearrange("c j x -> j c x")
                                 ).then_inc(g_loaded, 16)

                def round_loads(i, u_chunks):
                    for q in range(4):
                        if q < u_chunks:
                            u_load(i, q)
                        v_load(i, q)

                sp.wait_ge(g_stored[0], 16 * (NGC // 2) * (l + 1))
                sp.dma_start(v_raw[0], V[0]).then_inc(v_loaded[0], 16)
                sp.wait_ge(g_stored[1], 16 * (NGC // 2) * (l + 1))
                sp.dma_start(g_ring[:, 0], g_dram[l][:, :, 0].rearrange("c j x -> j c x")).then_inc(g_loaded, 16)
                sp.dma_start(v_raw[1], V[1]).then_inc(v_loaded[1], 16)
                for s in range(2):
                    sp.wait_ge(w_lo_ready, ubase + 4 * (LAG - XU) + 8 * (s + 1))
                    sp.dma_start(Ublk[s], U[LAG // 2 + s]).then_inc(w_loaded[s], 16)
                sp.wait_ge(g_loaded, 16 * (16 * l + 1))
                sp.dma_start(g_ring[:, 1], g_dram[l][:, :, 1].rearrange("c j x -> j c x")).then_inc(g_loaded, 16)
                round_loads(0, 4)
                with sp.Fori(1, UV - 1) as i:
                    g_load(i)
                    round_loads(i, 4)
                g_load(UV - 1)
                round_loads(UV - 1, 2)
                with sp.Fori(UV, 15) as i:
                    g_load(i)
                    round_loads(i, 0)
                for q in range(2):
                    v_load(15, q)

        @block.gpsimd
        def _(pool):
            pool.dma_start(ident, t_in["constants"][:, 0:P]).then_inc(ident_loaded, 16)

            def gain_load(k):
                if k >= 2:
                    sm, v = {"mix0": (u_ready, 3), "head": (y_ready, 12), "mem0": (mu_ready, 2), "xn0": (u_ready, 6),
                             "fn0": (u_ready, 9), "mix1": (u_ready, 12), "spool": (pooled, 12),
                             "mem1": (mu_ready, 4), "xn1": (u_ready, 15)}[GAINS[k - 2]]
                    pool.wait_ge(sm, v)
                pool.dma_start(gain[:, k % 2], t_in["gains"][k].partition_broadcast(P)).then_inc(gain_loaded[k % 2], 16)

            gain_load(0)
            pool.dma_start(wg, t_in["w_gates"]).then_inc(mix_loaded, 16)
            pool.dma_start(b4[0:4, :], t_in["b_gates"]).then_inc(mix_loaded, 16)
            pool.wait_ge(init_done, 1)
            pool.dma_start(cst[:, P:], t_in["constants"][:, P:]).then_inc(tables_loaded, 16)
            pool.dma_start(m0c[:, 2, :], t_in["state_m"].partition_broadcast(P)).then_inc(mix_loaded, 16)
            pool.dma_start(C_aug, t_in["state_Cn"].rearrange("(b p) e -> p b e", p=P)).then_inc(mix_loaded, 16)
            gain_load(1)

            def lower_chunk(name, local, first=0):
                with pool.Fori(first, 4) as i:
                    lower_group(pool, name, local, i)

            for name in ("qk", "vo"):
                for c in range(4):
                    lower_chunk(name, c)
            gain_load(2)
            lower_group(pool, "out", 0, 0)
            pool.wait_ge(d_emptied, DJ["state"] + 16)
            for buf, out in ((C_new, "Cn_p"), (C_aug, "Cn_s")):
                pool.dma_start(t_out[out].rearrange("(b p) e -> p b e", p=P), buf).then_inc(state_stored, 16)
            pool.dma_start(t_out["m_p"], selev[0:1, H:2 * H]).then_inc(state_stored, 16)
            pool.dma_start(t_out["m_s"], selev[0:1, 3 * H:4 * H]).then_inc(state_stored, 16)
            lower_chunk("out", 0, 1)
            gain_load(3)
            lower_chunk("out", 1)
            for l in range(2):
                if l == 0:
                    gain_load(4)
                else:
                    pool.wait_ge(u_ready, 12)
                    pool.dma_start(t_out["pool_p"], u[P - POOLST:P, 1, :]).then_inc(pool_stored, 16)
                    pool.dma_start(t_out["pool_s"], u[NS - POOLST:NS, 2, :]).then_inc(pool_stored, 16)
                    gain_load(7)
                    gain_load(8)
                    gain_load(9)
                lower_group(pool, f"memk{l}", 0, 0)
                pool.wait_ge(d_emptied, DJ[f"memk{l}"] + 4)
                pool.dma_start(t_out["mem_k"][l].rearrange("(b p) d -> p b d", p=P), mk).then_inc(mem_stored, 16)
                pool.wait_ge(d_emptied, DJ[f"memv{l}"] + 4)
                pool.dma_start(t_out["mem_v"][l].rearrange("(b p) d -> p b d", p=P), mv_).then_inc(mem_stored, 16)
                for c in range(2):
                    lower_chunk(f"xq{l}", c)
                pool.wait_ge(d_filled, DJ[f"sc{l}"] + 12)
                pool.dma_start(keysT, t_in["peer_keys"][l]).then_inc(keys_loaded, 16)
                for c in range(2):
                    lower_chunk(f"xo{l}", c)
                if l == 0:
                    gain_load(5)
                    gain_load(6)
                else:
                    gain_load(10)

                def lower_parts(i, per, block, raw, m):
                    for q in range(4):
                        pool.wait_ge(w_hi_ready, at(i, 4 * per, split_base(l, block) + q + 1))
                        pool.tensor_tensor(wq[:, q, 1], quarter(raw, m, q), wq[:, q, 0].bitcast(F32), ALU.subtract
                                           ).then_inc(w_lo_ready, 1)

                with pool.Fori(0, 2) as i:
                    for m in range(8):
                        lower_parts(i, 8, m, W[(WC[f"pq{l}"] + m // 4) % 2], m % 4)
                with pool.Fori(0, AHEAD // 4) as i:
                    for r in range(4):
                        lower_parts(i, 4, HP + r, Ublk[r // 2], r % 2)

                def store_gates(i, r):
                    pool.wait_ge(a_emptied, i * 20 + (AJ[f"gb{l}"] + 5 * r + 5))
                    pool.dma_start(g_dram[l][i * 4 + r], g_stage[r % 2].rearrange("p (a b) t -> p a (b t)", b=8)
                                   ).then_inc(g_stored[r % 2], 16)

                for r in range(4):
                    lower_parts(None, 0, HP + AHEAD + r, Ublk[r // 2], r % 2)
                    if r:
                        store_gates(0, r - 1)
                with pool.Fori(1, 5) as i:
                    for r in range(4):
                        lower_parts(i, 4, HP + AHEAD + r, Ublk[r // 2], r % 2)
                        store_gates(i if r else i - 1, (r - 1) % 4)
                store_gates(4, 3)
                with pool.Fori(0, (NB - LAG + XU) // 4) as i:
                    for r in range(4):
                        lower_parts(i, 4, HP + LAG - XU + r, Ublk[r // 2], r % 2)
            for t, (off, rows) in enumerate(TILES):
                pool.wait_ge(u_ready, 18 + t + 1)
                dst = t_out["y_p"][off:off + rows] if t < 2 else t_out["y_s"]
                pool.dma_start(dst, u[0:rows, t, :]).then_inc(y_stored, 16)
            pool.wait_ge(y_stored, 48)
            pool.wait_ge(mem_stored, 64)
            pool.wait_ge(pool_stored, 32)
            pool.wait_ge(state_stored, 64)

        @block.tensor
        def _(pe):
            def d_bank(n, i=None, per=0):
                if i is None:
                    if n >= 4:
                        pe.wait_ge(d_emptied, n - 3)
                else:
                    assert per % 4 == 0 and n >= 4
                    pe.wait_ge(d_emptied, i * per + (n - 3))
                return psum[:, DBANKS[n % 4], :]

            def a_bank(n, i=None, per=0):
                if i is None:
                    if n >= 4:
                        pe.wait_ge(a_emptied, n - 3)
                else:
                    assert per % 4 == 0 and n >= 4
                    pe.wait_ge(a_emptied, i * per + (n - 3))
                return psum[:, ABANKS[n % 4], :]

            def transposes(stage, src, tiles, n_ready, ready, first=0):
                n = DJ[stage]
                for t, (off, rows) in enumerate(tiles):
                    pe.wait_ge(ready, n_ready + t + 1)
                    for q in range(2):
                        bank = d_bank(n)
                        for b in range(4):
                            last = pe.transpose(bank[:, b * P:b * P + rows], src(t, rows, 4 * q + b), ident[0:rows, 0:rows])
                        last.then_inc(d_filled, 1)
                        n += 1

            def u_transposes(stage, norm):
                transposes(stage, lambda t, rows, b: u[0:rows, t, b * P:(b + 1) * P], TILES, 3 * norm, u_ready)

            def split_block(i, per, base, bank, filled=a_filled, quarters=range(4)):
                for q in quarters:
                    pe.wait_ge(w_lo_ready, at(i, 4 * per, base + q + 1))
                    for kk in range(2):
                        k = 2 * q + kk
                        hi, lo = wq[:, q, 0, kk, :], wq[:, q, 1, kk, :]
                        pe.matmul(bank[:, 0:TOK], hi, uT_hi[:, k, :], start=k == 0, stop=False)
                        pe.matmul(bank[:, 0:TOK], hi, uT_lo[:, k, :], start=False, stop=False)
                        last = pe.matmul(bank[:, 0:TOK], lo, uT_hi[:, k, :], start=False, stop=k == KD - 1)
                    last.then_inc(quarter_used if q < 3 else filled, 1)

            def feature_major(name, n_chunks):
                def pair(i):
                    for m in range(8):
                        split_block(i, 8, SPLIT[name, 0][0] + 4 * m, d_bank(DJ[name] + m, i, 8), d_filled)
                if n_chunks == 2:
                    pair(None)
                else:
                    with pe.Fori(0, n_chunks // 2) as i:
                        pair(i)

            def token_major(stage, name, local, tiles, bank_of=d_bank, filled=d_filled, jobs=DJ, base=0):
                banks = [None] * len(tiles)
                for r in range(16):
                    k, n = r // 2, r % 2
                    pe.wait_ge(w_lo_ready, SPLIT[name, local][0] + r + 1)
                    w_hi, w_lo = wq_row[:, r % 4, 0], wq_row[:, r % 4, 1]
                    for t, (off, rows) in enumerate(tiles):
                        if r == 0:
                            banks[t] = bank_of(jobs[stage] + base + t)
                        out = banks[t][0:rows, n * 2 * P:(n + 1) * 2 * P]
                        hi, lo = uT_hi[:, k, off:off + rows], uT_lo[:, k, off:off + rows]
                        for a, (lhs, rhs) in enumerate(((hi, w_hi), (hi, w_lo), (lo, w_hi))):
                            last = pe.matmul(out, lhs, rhs, start=r == 0 and a == 0, stop=k == KD - 1 and a == 2,
                                             skip_group_check=True)
                        if r == 15:
                            last.then_inc(filled, 1)
                    if r < 15:
                        last.then_inc(quarter_used, 1)

            pe.wait_ge(ident_loaded, 16)
            u_transposes("mixn0", 0)
            pe.wait_ge(d_emptied, DJ["mixn0"] + 6)
            feature_major("qk", 4)
            pe.wait_ge(u32_ready, 1)
            pe.wait_ge(mix_loaded, 64)
            for g in range(2):
                bank = d_bank(DJ["gates"] + g)
                for k in range(KD):
                    last = pe.matmul(bank[0:H, 0:TOK], wg[:, k, H * g:H * g + H], uT[:, k, :], start=k == 0, stop=k == KD - 1)
                last.then_inc(d_filled, 1)
            for c in range(2):
                token_major("v", "vo", c, TILES, base=3 * c)
            pe.wait_ge(gate_rows, 1)
            bank = d_bank(DJ["cols"])
            for t, (off, rows) in enumerate(TILES):
                for a in range(2):
                    last = pe.transpose(bank[0:rows, t * 8 + a * H:t * 8 + a * H + H], R4[0:H, 4 + a, off:off + rows], ident[0:H, 0:H])
            last.then_inc(d_filled, 1)
            pe.wait_ge(tables_loaded, 16)
            for h in range(H):
                bank = d_bank(DJ["rb"] + h)
                pe.matmul(bank[:, 0:TOK], sel4[0:H, h, :], R4[0:H, 5, :], start=True, stop=True).then_inc(d_filled, 1)
            for c in range(2):
                token_major("o", "vo", 2 + c, TILES, a_bank, a_filled, AJ, 3 * c)
            pe.wait_ge(m_ready, 1)
            bank = d_bank(DJ["sel"])
            pe.matmul(bank[:, 0:8], last_p, bm[:, 1, :], start=True, stop=True)
            pe.matmul(bank[:, 8:16], last_s[0:NS, :], bm[0:NS, 2, :], start=True, stop=True).then_inc(d_filled, 1)
            keys = ((0, 128), (0, 256), (256, 64))
            for h in range(H):
                for t, (off, rows) in enumerate(TILES):
                    bank = d_bank(DJ["qkt"] + 3 * h + t)
                    k0, kn = keys[t]
                    for d in range(2):
                        last = pe.matmul(bank[0:rows, 0:kn], qT[:, 2 * h + d, off:off + rows], kT[:, 2 * h + d, k0:k0 + kn],
                                         start=d == 0, stop=d == 1)
                    last.then_inc(d_filled, 1)
            n = DJ["ktok"]
            for t, (off, rows) in enumerate(TILES):
                for q in range(2):
                    bank = d_bank(n)
                    for b in range(4):
                        last = pe.transpose(bank[0:rows, b * P:(b + 1) * P], kT[:, 4 * q + b, off:off + rows], ident)
                    last.then_inc(d_filled, 1)
                    n += 1

            def mix_order():
                n = DJ["mix"]
                for h in range(H + 1):
                    if h < H:
                        yield n, h, 0
                        n += 1
                    if h >= 1:
                        for k in range(1, 5):
                            yield n, h - 1, k
                            n += 1

            pe.wait_ge(d_emptied, DJ["qkt"] + 12)
            swT_job = {}
            for n, h, k in mix_order():
                bank = d_bank(n)
                sT = swT[:, h % 2, :]
                if k == 0:
                    swT_job[h] = n
                    for dst, t, src in ((0, 0, 0), (128, 1, 128), (256, 1, 256)):
                        last = pe.transpose(bank[:, dst:dst + P], wts[:, h, src:src + P], ident)
                    last = pe.transpose(bank[0:NS, 384:448], wts[0:NS, h, 384:448], ident[0:NS, 0:NS])
                elif k == 1:
                    pe.wait_ge(d_emptied, swT_job[h] + 1)
                    last = pe.matmul(bank[:, 0:VA], sT[:, 0:P], v_aug[:, 0, h, :], start=True, stop=True)
                elif k == 2:
                    pe.matmul(bank[:, 0:VA], sT[:, P:2 * P], v_aug[:, 0, h, :], start=True, stop=False)
                    last = pe.matmul(bank[:, 0:VA], sT[:, 2 * P:3 * P], v_aug[:, 1, h, :], start=False, stop=True)
                elif k == 3:
                    for d in range(2):
                        last = pe.matmul(bank[0:NS, 0:VA], qT[:, 2 * h + d, NP_:TOK], C_aug[:, 2 * h + d, :],
                                         start=d == 0, stop=d == 1)
                else:
                    last = pe.matmul(bank[0:NS, 0:VA], sT[0:NS, 384:448], v_aug[0:NS, 2, h, :], start=True, stop=True)
                last.then_inc(d_filled, 1)
            n = DJ["yT"]
            for t, (off, rows) in enumerate(TILES):
                pe.wait_ge(y_ready, 4 * (t + 1))
                for q in range(2):
                    bank = d_bank(n)
                    for b in range(4):
                        h, c = (4 * q + b) // 2, b % 2
                        last = pe.transpose(bank[:, b * P:b * P + rows], hn[0:rows, t, h, c * P:(c + 1) * P], ident[0:rows, 0:rows])
                    last.then_inc(d_filled, 1)
                    n += 1
            for b in range(KD):
                bank = d_bank(DJ["state"] + b)
                for t in range(2):
                    last = pe.matmul(bank[:, 0:VA], kw[:, t, b * P:(b + 1) * P], v_aug[:, t, b // 2, :], start=t == 0, stop=t == 1)
                last.then_inc(d_filled, 1)
            for b in range(KD):
                bank = d_bank(DJ["state"] + KD + b)
                pe.matmul(bank[:, 0:VA], kw[0:NS, 2, b * P:(b + 1) * P], v_aug[0:NS, 2, b // 2, :], start=True, stop=True
                          ).then_inc(d_filled, 1)
            pe.wait_ge(d_emptied, DJ["yT"] + 6)
            for c in range(2):
                token_major("out", "out", c, TILES, base=3 * c)

            def memory(l):
                mt = ((0, P), (P, P))
                transposes(f"memT{l}", lambda t, rows, b: u[0:rows, t, b * P:(b + 1) * P], mt, 2 * l, mu_ready)
                pe.wait_ge(d_emptied, DJ[f"memT{l}"] + 4)
                for c in range(2):
                    token_major(f"memk{l}", f"memk{l}", c, mt, base=2 * c)
                for c in range(2):
                    token_major(f"memv{l}", f"memv{l}", c, mt, base=2 * c)
                pe.wait_ge(d_emptied, DJ[f"memk{l}"] + 4)
                for j in range(4):
                    bank = d_bank(DJ[f"memkT{l}"] + j)
                    for b in range(2):
                        for t in range(2):
                            last = pe.transpose(bank[:, b * MEM + t * P:b * MEM + (t + 1) * P],
                                                mk[:, t, (2 * j + b) * P:(2 * j + b + 1) * P], ident)
                    last.then_inc(d_filled, 1)

            def attend(l, norm):
                u_transposes(f"xn{l}", norm)
                pe.wait_ge(d_emptied, DJ[f"xn{l}"] + 6)
                feature_major(f"xq{l}", 2)
                pe.wait_ge(cache_loaded, 32 * (l + 1))
                for h in range(H):
                    pe.wait_ge(d_emptied, DJ[f"xq{l}"] + 2 * h + 2)
                    for t, (off, rows) in enumerate(TILES):
                        bank = d_bank(DJ[f"sc{l}"] + 3 * h + t)
                        kk = mkT if t < 2 else skT
                        for d in range(2):
                            last = pe.matmul(bank[0:rows, 0:MEM], qT[:, 2 * h + d, off:off + rows], kk[:, 2 * h + d, :],
                                             start=d == 0, stop=d == 1)
                        last.then_inc(d_filled, 1)
                for n, h, k in av_order(l):
                    bank = d_bank(n)
                    if k < 2:
                        pe.wait_ge(p_ready, 12 * l + 3 * h + 3)
                        for t, (off, rows) in enumerate(TILES):
                            last = pe.transpose(bank[:, off:off + rows], probs[0:rows, 3 * h + t, k * P:(k + 1) * P],
                                                ident[0:rows, 0:rows])
                    else:
                        pe.wait_ge(d_emptied, av_pt_done(l, h))
                        c0 = (2 * h + k - 2) * P
                        for vv, a, z in ((mv_, 0, NP_), (sv_, NP_, TOK)):
                            for m in range(2):
                                last = pe.matmul(bank[:, a:z], vv[:, m, c0:c0 + P], probsT[:, h % 2, m, a:z],
                                                 start=m == 0, stop=m == 1)
                    last.then_inc(d_filled, 1)
                pe.wait_ge(d_emptied, DJ[f"av{l}"] + 16)
                for c in range(2):
                    token_major(f"xo{l}", f"xo{l}", c, TILES, base=3 * c)

            def v_block(l, i, r):
                pe.wait_ge(p_split, i * 8 + (NB * l + r + 1))
                pe.wait_ge(v_split, i * 8 + (NB * l + r + 1))
                ph, vh = phl[:, r % 2], vhl[:, r % 2]
                for t in range(2):
                    hi, lo = ph[:, t * P:(t + 1) * P], ph[:, TOK + NS + t * P:TOK + NS + (t + 1) * P]
                    for lhs, part in ((hi, 0), (hi, 1), (lo, 0)):
                        for n in range(2):
                            pe.matmul(psum[:, 2 + 2 * t + n, :], lhs, vh[:, part, n * 512:(n + 1) * 512],
                                      start=False, stop=False, skip_group_check=True)
                for part in range(2):
                    for n in range(2):
                        last = pe.matmul(psum[:, 6 + n, :], ph[:, NP_:NP_ + P], vh[:, part, n * 512:(n + 1) * 512],
                                         start=False, stop=False, skip_group_check=True)
                last.then_inc(v_summed, 1)

            def peer(l, norm):
                u_transposes(f"fn{l}", norm)
                pe.wait_ge(d_emptied, DJ[f"fn{l}"] + 6)
                pe.wait_ge(keys_loaded, 16 * (l + 1))
                with pe.Fori(0, 2) as i:
                    for kind, m in PQ_ORDER:
                        if kind == "q":
                            split_block(i, 8, split_base(l, m), a_bank(AJ[f"pq{l}"] + m, i, 8))
                        else:
                            pe.wait_ge(a_emptied, i * 8 + (AJ[f"pq{l}"] + m + 1))
                            bank = d_bank(DJ[f"pq{l}"] + m, i, 8)
                            for t, (off, rows) in enumerate(TILES):
                                last = pe.matmul(bank[0:rows, t * P:(t + 1) * P], pqT[:, m, off:off + rows],
                                                 keysT[:, i * 8 + m, :], start=True, stop=True)
                            last.then_inc(d_filled, 1)
                pe.wait_ge(a_emptied, AJ[f"up{l}"])
                with pe.Fori(0, AHEAD // 4) as i:
                    for r in range(4):
                        split_block(i, 4, split_base(l, HP + r), a_bank(AJ[f"up{l}"] + r, i, 4))
                for t, (off, rows) in enumerate(TILES):
                    pe.wait_ge(picked_ready, 3 * l + t + 1)
                    bank = d_bank(DJ[f"slot{l}"] + t)
                    for a in range(3):
                        last = pe.transpose(bank[:, a * P:a * P + rows], picked[0:rows, t, a, :], ident[0:rows, 0:rows])
                    last.then_inc(d_filled, 1)
                pe.wait_ge(a_emptied, AJ[f"gb{l}"])
                pe.wait_ge(d_emptied, DJ[f"slot{l}"] + 3)
                with pe.Fori(0, 5) as i:
                    for r in range(4):
                        n = AJ[f"gb{l}"] + 5 * r
                        pe.wait_ge(a_emptied, i * 20 + (n + U_JOB - 10 + 1))
                        for g in range(4):
                            split_block(i, 4, split_base(l, HP + AHEAD + r), psum[:, GB_UBANKS[r % 2], :], quarters=(g,))
                            pe.wait_ge(a_emptied, i * 20 + (n + G_JOBS[g] - 5 + 1))
                            bank = psum[:, ABANKS[g], :]
                            pe.wait_ge(oh_ready, i * 64 + (TOK * l + 16 * r + 4 * g + 4))
                            for q in range(4):
                                s = (4 * g + q) % 8
                                last = pe.matmul(bank[:, q * P:(q + 1) * P], ohJ[:, s, :], oh[:, s, :], start=True, stop=True)
                            last.then_inc(a_filled, 1)
                pe.wait_ge(zero_ready, l + 1)
                pe.wait_ge(a_emptied, AJ[f"ux{l}"])
                for n in range(6):
                    last = pe.matmul(psum[:, 2 + n, :], phl[:, 0, 0:P], vhl[:, 0, 0, 0:512], start=True, stop=False,
                                     skip_group_check=True)
                last.then_inc(v_summed, 2)
                for r in range(XU):
                    if r >= 2:
                        pe.wait_ge(a_emptied, AJ[f"ux{l}"] + r - 1)
                    split_block(None, 0, split_base(l, HP + LAG - XU + r), psum[:, r % 2, :])
                with pe.Fori(0, UV) as i:
                    for r in range(8):
                        pe.wait_ge(a_emptied, i * 8 + (AJ[f"uv{l}"] + r - 1))
                        split_block(i, 8, split_base(l, HP + LAG + r), psum[:, r % 2, :])
                        v_block(l, i, r)
                with pe.Fori(UV, 16) as i:
                    for r in range(8):
                        v_block(l, i, r)
                pe.wait_ge(a_emptied, AJ[f"uv{l}"] + NB - LAG)
                for n in range(2):
                    pe.wait_ge(acc_copied, 2 * l + n + 1)
                    pe.matmul(psum[0:NS, n, :], fold, acc_tmp[:, n, :], start=True, stop=True).then_inc(d_filled, 1)

            memory(0)
            attend(0, 1)
            peer(0, 2)
            pe.wait_ge(pool_loaded, 32)
            pe.wait_ge(prefix_loaded, 16)
            pe.wait_ge(u_ready, 12)
            for b in range(KD):
                bank = d_bank(DJ["pool"] + b)
                for s in range(2):
                    pe.matmul(bank[:, 0:NP_], u[:, s, b * P:(b + 1) * P], bandp[:, b // 2, s, :], start=s == 0, stop=s == 1)
                pe.matmul(bank[:, NP_:TOK], u[:, 2, b * P:(b + 1) * P], bands_[:, b // 2, :], start=True, stop=True
                          ).then_inc(d_filled, 1)
            for g in range(4):
                pe.wait_ge(d_emptied, DJ["pool"] + 2 * g + 2)
                for t, (off, rows) in enumerate(TILES):
                    bank = d_bank(DJ["pool"] + KD + 3 * g + t)
                    for c in range(2):
                        last = pe.matmul(bank[0:rows, 0:DH], plT[:, 2 * g + c, off:off + rows], wpool[:, g, c, :],
                                         start=c == 0, stop=c == 1)
                    last.then_inc(d_filled, 1)
            memory(1)
            attend(1, 4)
            peer(1, 5)

        @block.scalar
        def _(act):
            step = Chain(act, act_step)

            def norm_stats(norm, index, extra=()):
                for sm, v in extra:
                    act.wait_ge(sm, v)
                for t, (off, rows) in enumerate(TILES):
                    sm, v = x_ready(norm, t)
                    act.wait_ge(sm, v)
                    step(act.activation(u[0:rows, t, :], x[0:rows, t, :], ACT.Square, accum_out=ss[0:rows, t:t + 1]))
                    act.activation(std[0:rows, t:t + 1], ss[0:rows, t:t + 1], ACT.Sqrt, bias=eps_c[0:rows, :], scale=1.0 / D
                                   ).then_inc(std_ready, 1)

            def copy_transposes(stage, tiles):
                for n, before, bank, hi, lo in turned(stage, tiles):
                    act.wait_ge(d_filled, n + 1)
                    act.activation(hi, bank, ACT.Copy).then_inc(turned_hi, 1)

            def mem_stats(l):
                if l == 0:
                    act.wait_ge(y_ready, 12)
                else:
                    act.wait_ge(d_filled, DJ["pool"] + 8)
                    act.wait_ge(pool_stored, 32)
                act.wait_ge(mem_loaded, 16 * (l + 1))
                for t in range(2):
                    step(act.activation(u[:, t, :], memx[:, t, :], ACT.Square, accum_out=mss[:, t:t + 1]))
                    act.activation(mstd[:, t:t + 1], mss[:, t:t + 1], ACT.Sqrt, bias=eps_c, scale=1.0 / D
                                   ).then_inc(mstd_ready, 1)

            def upper_chunk(name, local, part):
                base, used, prev = SPLIT[name, local]

                def group(i):
                    for q in range(4):
                        if part == 0:
                            if prev is not None:
                                act.wait_ge(quarter_used, used - 2 + q) if q < 3 else act.wait_ge(filled_sem[prev[0]], prev[1])
                        elif by_feature(name):
                            if q < 3:
                                act.wait_ge(quarter_used, i * 3 + (used - 2 + q))
                            else:
                                kind, after = job_after(name, local)
                                act.wait_ge(filled_sem[kind], i + (after - 4))
                        else:
                            act.wait_ge(quarter_used, i * 4 + (used - 3 + q))
                        raw, dst = chunk_quarter(name, local, i, q, 0)
                        act.activation(dst, raw, ACT.Copy).then_inc(w_hi_ready, 1)

                if part == 0:
                    c = WC[name] + local
                    act.wait_ge(w_loaded[c % 2], 16 * (c // 2 + 1))
                    group(0)
                else:
                    with act.Fori(1, 4) as i:
                        group(i)

            def upper(name, *local):
                for c in local:
                    upper_chunk(name, c, 0)
                    upper_chunk(name, c, 1)

            def output_gate(c):
                for t, (off, rows) in enumerate(TILES):
                    n = AJ["o"] + 3 * c + t
                    act.wait_ge(a_filled, n + 1)
                    act.activation(u[0:rows, t, c * 512:(c + 1) * 512], psum[0:rows, ABANKS[n % 4], :], ACT.Sigmoid
                                   ).then_inc(a_emptied, 1)

            act.wait_ge(init_done, 1)
            norm_stats("mix0", 0)
            copy_transposes("mixn0", TILES)
            upper("qk", 0, 1, 2, 3)
            upper_chunk("vo", 0, 0)
            act.wait_ge(gate_abs, 1)
            step(act.activation(R4[0:H, 2, :], R4[0:H, 2, :], ACT.Exp, scale=-1.0))
            act.activation(R4[0:H, 2, :], R4[0:H, 2, :], ACT.Ln, bias=one_c[0:H, :]).then_inc(gate_ln, 1)
            upper_chunk("vo", 0, 1)
            upper("vo", 1, 2)
            upper_chunk("vo", 3, 0)
            output_gate(0)

            def log_weights(h):
                for t, (off, rows) in enumerate(TILES):
                    a, z = ((0, 128), (128, 384), (384, 448))[t]
                    act.activation(wts[0:rows, h, a:z], wts[0:rows, h, a:z], ACT.Exp, bias=negm[0:rows, t, h:h + 1]
                                   ).then_inc(w_ready, 1)

            act.wait_ge(m_ready, 1)
            log_weights(0)
            log_weights(1)
            upper_chunk("vo", 3, 1)
            upper_chunk("out", 0, 0)
            output_gate(1)
            log_weights(2)
            log_weights(3)
            act.activation(ainter, idiff, ACT.Exp).then_inc(mexp_ready, 1)
            act.activation(emneg, negm, ACT.Exp).then_inc(mexp_ready, 1)
            act.wait_ge(ws_arg, 1)
            act.activation(wscol, wsarg, ACT.Exp).then_inc(ws_ready, 1)
            act.activation(gstate, garg, ACT.Exp).then_inc(ws_ready, 1)
            act.wait_ge(var_ready, 1)
            act.activation(sdev, sdev, ACT.Sqrt, bias=eps_c).then_inc(sdev_ready, 1)
            act.wait_ge(norm_ready, 1)
            for t, (off, rows) in enumerate(TILES):
                for h in range(H):
                    y = hn[0:rows, t, h, 0:DH]
                    act.activation(y, y, ACT.Identity, bias=nmean[0:rows, t, h:h + 1], scale=srec[0:rows, t, h:h + 1]
                                   ).then_inc(z_ready, 1)
            copy_transposes("yT", TILES)

            def attend(l):
                upper_chunk(f"xq{l}", 0, 0)
                copy_transposes(f"xn{l}", TILES)
                upper_chunk(f"xq{l}", 0, 1)
                upper(f"xq{l}", 1)
                upper_chunk(f"xo{l}", 0, 0)
                for j in range(3 * H):
                    rows = TILES[j % 3][1]
                    act.wait_ge(mx_ready, 12 * l + j + 1)
                    act.activation(probs[0:rows, j, :], psum[0:rows, DBANKS[(DJ[f"sc{l}"] + j) % 4], 0:MEM], ACT.Exp,
                                   bias=nmx[0:rows, j:j + 1], scale=DH ** -0.5,
                                   accum_out=rsum[0:rows, j:j + 1]).then_inc(d_emptied, 1)
                upper_chunk(f"xo{l}", 0, 1)
                upper(f"xo{l}", 1)

            def memory(l):
                upper_chunk(f"memk{l}", 0, 0)
                copy_transposes(f"memT{l}", ((0, P), (P, P)))
                upper_chunk(f"memk{l}", 0, 1)
                upper(f"memk{l}", 1)
                norm_stats(f"xn{l}", 1 + 3 * l, extra=((d_filled, DJ[f"memT{l}"] + 4),))
                upper(f"memv{l}", 0, 1)

            def peer(l):
                def upper_parts(i, per, block, raw, m, load, prev_job, prev_filled=a_filled, quarters=range(4)):
                    if load is not None and 0 in quarters:
                        c = load[1]
                        act.wait_ge(w_loaded[c % 2], at(i, load[0], 16 * (c // 2 + 1)))
                    for q in quarters:
                        if q < 3:
                            act.wait_ge(quarter_used, at(i, 3 * per, used_base(l, block) - 2 + q))
                        else:
                            act.wait_ge(prev_filled, at(i, prev_job[0], prev_job[1] + 1))
                        act.activation(wq[:, q, 0], quarter(raw, m, q), ACT.Copy).then_inc(w_hi_ready, 1)

                def upper_pq(m, prev):
                    c = WC[f"pq{l}"] + m // 4
                    upper_parts(None, 0, m, W[c % 2], m % 4, (0, c) if m % 4 == 0 else None, (0, prev),
                                d_filled if m == 0 else a_filled)

                def upper_u(i, per, r, at_block, prev, prev_per, quarters=range(4)):
                    b = at_block + r
                    upper_parts(i, per, HP + b, Ublk[(b // 2) % 2], b % 2,
                                (4 * per, WC[f"U{l}"] + b // 2) if b % 2 == 0 else None, (prev_per, prev),
                                quarters=quarters)

                upper_pq(0, DJ[f"xo{l}"] + 5)
                copy_transposes(f"fn{l}", TILES)
                for m in range(HP):
                    n = AJ[f"pq{l}"] + m
                    if m + 1 < HP:
                        upper_pq(m + 1, n)
                    else:
                        upper_u(None, 0, 0, 0, n, 0)
                    act.wait_ge(a_filled, n + 1)
                    act.activation(pqT[:, m % 8, :], psum[:, ABANKS[n % 4], 0:TOK], ACT.Copy).then_inc(a_emptied, 1)
                act.wait_ge(mem_stored, 32 * (l + 1))
                with act.Fori(0, AHEAD // 4) as i:
                    for r in range(4):
                        n = AJ[f"up{l}"] + r
                        upper_u(i, 4, r + 1, 0, n, 4)
                        act.wait_ge(a_filled, i * 4 + (n + 1))
                        act.activation(act4[:, i, r, :], psum[:, ABANKS[n % 4], 0:TOK], ACT.Gelu).then_inc(a_emptied, 1)
                for t, (off, rows) in enumerate(TILES):
                    act.wait_ge(top_ready, 3 * l + t + 1)
                    act.activation(picked[0:rows, t, 2, :], picked[0:rows, t, 2, :], ACT.Exp).then_inc(exp_ready, 1)
                def spread(i, first=False):
                    for r in range(4):
                        n = AJ[f"gb{l}"] + 5 * r
                        if not (first and r < 2):
                            act.wait_ge(g_stored[r % 2], i * 32 + 16 * (NGC // 2 * l + r // 2))
                        for g in range(4):
                            upper_u(i, 4, r + 1, AHEAD, n + U_JOB, 20, quarters=(g,))
                            if g == 3:
                                act.wait_ge(a_filled, i * 20 + (n + U_JOB + 1))
                                act.activation(act4[:, i + AHEAD // 4, r, :], psum[:, GB_UBANKS[r % 2], 0:TOK], ACT.Gelu
                                               ).then_inc(a_emptied, 1)
                            gn = n + G_JOBS[g]
                            act.wait_ge(a_filled, i * 20 + (gn + 1))
                            act.activation(g_stage[r % 2][:, :, 4 * g:4 * g + 4].rearrange("p i t -> p t i"),
                                           psum[:, ABANKS[g], :].rearrange("p (t i) -> p t i", i=NK), ACT.Copy
                                           ).then_inc(a_emptied, 1)

                spread(0, first=l == 0)
                with act.Fori(1, 5) as i:
                    spread(i)

                for r in range(XU):
                    n = AJ[f"ux{l}"] + r
                    upper_u(None, 0, r + 1, LAG - XU, n, 0)
                    act.wait_ge(a_filled, n + 1)
                    act.activation(act4[:, (LAG - XU) // 4, r, :], psum[:, r % 2, 0:TOK], ACT.Gelu).then_inc(a_emptied, 1)

                def vhi(i, r):
                    if r % 2 == 0:
                        act.wait_ge(v_loaded[(r // 2) % 2], i * 32 + 16 * (32 * l + r // 4 + 1))
                    act.wait_ge(v_summed, i * 8 + ((NB + 2) * l + r + 1))
                    act.activation(vhl[:, r % 2, 0, :], v_raw[(r // 2) % 2][:, r % 2, :], ACT.Copy).then_inc(vhi_ready, 1)

                def uv_round(i, last=False):
                    for r in range(8):
                        n = AJ[f"uv{l}"] + r
                        vhi(i, r)
                        if not (last and r == 7):
                            upper_u(i, 8, r + 1, LAG, n, 8)
                        act.wait_ge(a_filled, i * 8 + (n + 1))
                        act.wait_ge(p_split, i * 8 + (NB * l + r + 1))
                        act.activation(act8[:, i % (LAG // 8), r, :], psum[:, r % 2, 0:TOK], ACT.Gelu).then_inc(a_emptied, 1)

                with act.Fori(0, UV - 1) as i:
                    uv_round(i)
                uv_round(UV - 1, last=True)
                with act.Fori(UV, 16) as i:
                    for r in range(8):
                        vhi(i, r)

            upper_chunk("out", 0, 1)
            mem_stats(0)
            upper("out", 1)
            for l in range(2):
                if l:
                    norm_stats("mix1", 3)
                    mem_stats(1)
                memory(l)
                attend(l)
                norm_stats(f"fn{l}", 2 + 3 * l)
                peer(l)
            norm_stats("final", 6)

        @block.vector
        def _(dve):
            step = Chain(dve, dve_step)
            row_step = Chain(dve, dve_row_step)

            def full(n, i=None, per=0):
                dve.wait_ge(d_filled, n + 1 if i is None else i * per + (n + 1))
                return psum[:, DBANKS[n % 4], :]

            def scale_rows(norm, index, gidx):
                dve.wait_ge(gain_loaded[gidx % 2], 16 * (gidx // 2 + 1))
                for t, (off, rows) in enumerate(TILES):
                    dve.wait_ge(std_ready, 3 * index + t + 1)
                    step(dve.reciprocal(rstd[0:rows, t:t + 1], std[0:rows, t:t + 1]))
                    dve.scalar_tensor_tensor(out=u[0:rows, t, :], in0=x[0:rows, t, :], scalar=rstd[0:rows, t:t + 1],
                                             in1=gain[0:rows, gidx % 2, :], op0=ALU.mult, op1=ALU.mult).then_inc(u_ready, 1)

            def empty_transposes(stage, tiles):
                for n, before, bank, hi, lo in turned(stage, tiles):
                    dve.wait_ge(turned_hi, before + 1)
                    dve.tensor_tensor(lo, bank, hi.bitcast(F32), ALU.subtract).then_inc(d_emptied, 1)

            def add_to_x(stage, halves=(0, 1)):
                for c in halves:
                    for t, (off, rows) in enumerate(TILES):
                        dst = x[0:rows, t, c * 512:(c + 1) * 512]
                        dve.tensor_tensor(dst, full(DJ[stage] + 3 * c + t)[0:rows, :], dst, ALU.add).then_inc(d_emptied, 1)

            step(dve.memset(small[:], 1.0))
            step(dve.memset(eps_c, EPS))
            step(dve.memset(arena[:, 19176:19496], 0.0))
            step(dve.memset(hn[:, 2], 1.0))
            step(dve.memset(v_aug[:, :, :, DH:VA], 1.0))
            dve.memset(mv, 1.0).then_inc(init_done, 1)
            dve.wait_ge(init_done, 1)
            scale_rows("mix0", 0, 0)
            empty_transposes("mixn0", TILES)
            dve.wait_ge(d_emptied, DJ["mixn0"] + 6)
            dve.tensor_tensor(uT, uT_hi.bitcast(F32), uT_lo.bitcast(F32), ALU.add).then_inc(u32_ready, 1)
            with dve.Fori(0, 2) as i:
                for m in range(8):
                    bank = full(DJ["qk"] + m, i, 8)
                    dve.tensor_copy(view(arena, 0, 2, KD, TOK)[:, i, m, :], bank[:, 0:TOK]).then_inc(d_emptied, 1)
            dve.wait_ge(mix_loaded, 64)
            for g in range(2):
                dve.tensor_scalar(R4[0:H, g, :], full(DJ["gates"] + g)[0:H, 0:TOK], b4[0:H, g:g + 1], None, ALU.add
                                  ).then_inc(d_emptied, 1)
            dve.wait_ge(d_emptied, DJ["gates"] + 2)
            dve.scalar_tensor_tensor(out=R4[0:H, 2, :], in0=R4[0:H, 1, :], scalar=-1.0, in1=R4[0:H, 1, :], op0=ALU.mult, op1=ALU.max
                                     ).then_inc(gate_abs, 1)
            step(dve.tensor_scalar(R4[0:H, 3, :], R4[0:H, 1, :], 0.0, None, ALU.min))
            dve.wait_ge(gate_ln, 1)
            step(dve.tensor_tensor(R4[0:H, 3, :], R4[0:H, 3, :], R4[0:H, 2, :], ALU.subtract))
            step(dve.memset(R4[0:H, 2, :], 1.0))
            for a, z in ((0, NP_), (NP_, TOK)):
                step(dve.tensor_tensor_scan(out=R4[0:H, 4, a:z], data0=R4[0:H, 2, a:z], data1=R4[0:H, 3, a:z], initial=0.0,
                                            op0=ALU.mult, op1=ALU.add))
            dve.tensor_tensor(R4[0:H, 5, :], R4[0:H, 0, :], R4[0:H, 4, :], ALU.subtract).then_inc(gate_rows, 1)
            for c in range(2):
                for t, (off, rows) in enumerate(TILES):
                    bank = full(DJ["v"] + 3 * c + t)
                    dve.tensor_copy(v_aug[0:rows, t, 2 * c:2 * c + 2, 0:DH], bank[0:rows, :].rearrange("p (h e) -> p h e", e=DH)
                                    ).then_inc(d_emptied, 1)
            dve.wait_ge(tables_loaded, 16)
            bank = full(DJ["cols"])
            step(dve.tensor_copy(br[:, 0:2, :], bank[:, 0:16].rearrange("p (t c) -> p t c", c=8)))
            dve.tensor_copy(br[0:NS, 2, :], bank[0:NS, 16:24]).then_inc(d_emptied, 1)
            dve.wait_ge(d_emptied, DJ["cols"] + 1)
            for h in range(H):
                bank = full(DJ["rb"] + h)
                b0, b1, b2 = br[:, 0, h:h + 1], br[:, 1, h:h + 1], br[0:NS, 2, h:h + 1]
                dve.scalar_tensor_tensor(out=wts[:, h, 0:128], in0=bank[:, 0:128], scalar=b0, in1=tri_m, op0=ALU.add, op1=ALU.add)
                dve.tensor_scalar(wts[:, h, 128:256], bank[:, 0:128], b1, None, ALU.add)
                dve.scalar_tensor_tensor(out=wts[:, h, 256:384], in0=bank[:, 128:256], scalar=b1, in1=tri_m, op0=ALU.add, op1=ALU.add)
                dve.scalar_tensor_tensor(out=wts[0:NS, h, 384:448], in0=bank[0:NS, NP_:TOK], scalar=b2, in1=tri_m[0:NS, 0:NS],
                                         op0=ALU.add, op1=ALU.add).then_inc(d_emptied, 1)
            dve.wait_ge(d_emptied, DJ["rb"] + H)
            for h in range(H):
                for t, (off, rows) in enumerate(TILES):
                    a, z = ((0, 128), (128, 384), (384, 448))[t]
                    ins = dve.tensor_reduce(rmax[0:rows, t, h:h + 1], wts[0:rows, h, a:z], AX.X, ALU.max)
            step(ins)
            step(dve.tensor_tensor(inter, br[:, :, 0:H], m0c, ALU.add))
            step(dve.tensor_copy(bm[:, :, 0:H], br[:, :, 0:H]))
            step(dve.tensor_tensor(bm[:, :, H:2 * H], rmax, inter, ALU.max))
            step(dve.tensor_tensor(idiff, inter, bm[:, :, H:2 * H], ALU.subtract))
            dve.tensor_scalar(negm, bm[:, :, H:2 * H], -1.0, None, ALU.mult).then_inc(m_ready, 1)
            dve.wait_ge(gain_loaded[1], 16)
            for c in range(2):
                dve.wait_ge(a_emptied, AJ["o"] + 3 * (c + 1))
                for t, (off, rows) in enumerate(TILES):
                    dst = u[0:rows, t, c * 512:(c + 1) * 512]
                    ins = dve.tensor_tensor(dst, dst, gain[0:rows, 1, c * 512:(c + 1) * 512], ALU.mult)
            step(ins)
            bank = full(DJ["sel"])
            dve.tensor_copy(selev, bank[:, 0:16]).then_inc(d_emptied, 1)
            dve.wait_ge(d_emptied, DJ["sel"] + 1)
            se = selev.rearrange("p (g a h) -> p g a h", g=2, a=2)
            step(dve.tensor_tensor(blm, se[:, :, 0, :], se[:, :, 1, :], ALU.subtract))
            step(dve.tensor_tensor(wsarg[:, 0:2, :], br[:, 0:2, H:2 * H], blm[:, 0:1, :].to_broadcast([P, 2, H]), ALU.add))
            step(dve.tensor_tensor(wsarg[:, 2, :], br[:, 2, H:2 * H], blm[:, 1, :], ALU.add))
            dve.tensor_tensor(garg, blm[:, 1, :], m0c[:, 2, :], ALU.add).then_inc(ws_arg, 1)
            for h in range(H):
                for t, (off, rows) in enumerate(TILES):
                    a, z = ((0, 128), (128, 384), (384, 448))[t]
                    bank = full(DJ["qkt"] + 3 * h + t)
                    dve.wait_ge(w_ready, 3 * h + t + 1)
                    dve.scalar_tensor_tensor(out=wts[0:rows, h, a:z], in0=bank[0:rows, 0:z - a], scalar=DH ** -0.5,
                                             in1=wts[0:rows, h, a:z], op0=ALU.mult, op1=ALU.mult).then_inc(d_emptied, 1)
            n = DJ["ktok"]
            dve.wait_ge(ws_ready, 2)
            for t, (off, rows) in enumerate(TILES):
                for q in range(2):
                    bank = full(n)
                    for hh in range(2):
                        h = 2 * q + hh
                        ins = dve.tensor_scalar(kw[0:rows, t, h * DH:(h + 1) * DH], bank[0:rows, hh * DH:(hh + 1) * DH],
                                                wscol[0:rows, t, h:h + 1], DH ** -0.5, ALU.mult, ALU.mult)
                    ins.then_inc(d_emptied, 1)
                    n += 1
            def head_stats(h):
                for t, (off, rows) in enumerate(TILES):
                    step.mark(dve.bn_stats(bnst[0:rows, 4 * t + h, :], hn[0:rows, t, h, 0:DH]))

            dve.wait_ge(mexp_ready, 2)
            n = DJ["mix"]
            for hh in range(H + 1):
                if hh < H:
                    bank = full(n)
                    dve.tensor_copy(swT[:, hh % 2, 0:384], bank[:, 0:384])
                    dve.tensor_copy(swT[0:NS, hh % 2, 384:448], bank[0:NS, 384:448]).then_inc(d_emptied, 1)
                    n += 1
                if hh >= 1:
                    h = hh - 1
                    for t in range(2):
                        dve.tensor_copy(hn[:, t, h, :], full(n)[:, 0:VA]).then_inc(d_emptied, 1)
                        n += 1
                    dve.tensor_scalar(qc_tmp[0:NS, h % 2, :], full(n)[0:NS, 0:VA], ainter[0:NS, 2, h:h + 1], None, ALU.mult
                                      ).then_inc(d_emptied, 1)
                    n += 1
                    dve.wait_ge(d_emptied, n)
                    dve.tensor_tensor(hn[0:NS, 2, h, :], full(n)[0:NS, 0:VA], qc_tmp[0:NS, h % 2, :], ALU.add).then_inc(d_emptied, 1)
                    n += 1
                    if h:
                        head_stats(h - 1)
            dve.wait_ge(d_emptied, n)
            head_stats(H - 1)
            step(dve.scalar_tensor_tensor(out=rinv, in0=hn[:, :, :, DH], scalar=-1.0, in1=hn[:, :, :, DH], op0=ALU.mult, op1=ALU.max))
            step(dve.tensor_tensor(rinv, rinv, emneg, ALU.max))
            step(dve.reciprocal(rinv, rinv))
            for t, (off, rows) in enumerate(TILES):
                for h in range(H):
                    ins = dve.bn_aggr(mv[0:rows, t, h, :], bnst[0:rows, 4 * t + h, :])
            step(ins)
            step(dve.tensor_tensor(sdev, mv[:, :, :, 1], rinv, ALU.mult))
            dve.tensor_tensor(sdev, sdev, rinv, ALU.mult).then_inc(var_ready, 1)
            dve.wait_ge(sdev_ready, 1)
            step(dve.reciprocal(srec, sdev))
            step(dve.tensor_tensor(srec, srec, rinv, ALU.mult))
            dve.scalar_tensor_tensor(out=nmean, in0=mv[:, :, :, 0], scalar=-1.0, in1=srec, op0=ALU.mult, op1=ALU.mult
                                     ).then_inc(norm_ready, 1)
            for t, (off, rows) in enumerate(TILES):
                for h in range(H):
                    y = hn[0:rows, t, h, 0:DH]
                    dve.wait_ge(z_ready, 4 * t + h + 1)
                    dve.tensor_tensor(y, y, u[0:rows, t, h * DH:(h + 1) * DH], ALU.mult).then_inc(y_ready, 1)
            def memory_rows(l):
                gidx = 2 if l == 0 else 7
                dve.wait_ge(gain_loaded[gidx % 2], 16 * (gidx // 2 + 1))
                for t in range(2):
                    dve.wait_ge(mstd_ready, 2 * l + t + 1)
                    step(dve.reciprocal(mrstd[:, t:t + 1], mstd[:, t:t + 1]))
                    dve.scalar_tensor_tensor(out=u[:, t, :], in0=memx[:, t, :], scalar=mrstd[:, t:t + 1], in1=gain[:, gidx % 2, :],
                                             op0=ALU.mult, op1=ALU.mult).then_inc(mu_ready, 1)

            empty_transposes("yT", TILES)
            for b in range(KD):
                dve.tensor_copy(C_new[:, b, :], full(DJ["state"] + b)[:, 0:VA]).then_inc(d_emptied, 1)
            for b in range(KD):
                dve.scalar_tensor_tensor(out=C_aug[:, b, :], in0=C_aug[:, b, :], scalar=gstate[:, b // 2:b // 2 + 1],
                                         in1=full(DJ["state"] + KD + b)[:, 0:VA], op0=ALU.mult, op1=ALU.add
                                         ).then_inc(d_emptied, 1)
            add_to_x("out", (0,))
            memory_rows(0)
            add_to_x("out", (1,))

            def memory(l):
                order = [(f"memk{l}", 0, mk), (f"memk{l}", 1, mk), (f"memv{l}", 0, mv_), (f"memv{l}", 1, mv_)]
                empty_transposes(f"memT{l}", ((0, P), (P, P)))
                dve.wait_ge(w_lo_ready, SPLIT[f"memk{l}", 0][0] + 4)
                for k, (name, c, dst) in enumerate(order):
                    with dve.Fori(1, 4) as i:
                        lower_group(dve, name, c, i)
                    if k < 3:
                        lower_group(dve, order[k + 1][0], order[k + 1][1], 0)
                    else:
                        scale_rows(f"xn{l}", 1 + 3 * l, 3 if l == 0 else 8)
                    for t in range(2):
                        dve.tensor_copy(dst[:, t, c * 512:(c + 1) * 512], full(DJ[name] + 2 * c + t)).then_inc(d_emptied, 1)
                for j in range(4):
                    dve.tensor_copy(mkT[:, 2 * j:2 * j + 2, :], full(DJ[f"memkT{l}"] + j).rearrange("p (b m) -> p b m", m=MEM)
                                    ).then_inc(d_emptied, 1)

            def attend(l, norm):
                empty_transposes(f"xn{l}", TILES)
                for m in range(8):
                    dve.tensor_copy(qT[:, m, :], full(DJ[f"xq{l}"] + m)[:, 0:TOK]).then_inc(d_emptied, 1)

                def normalise(j):
                    rows = TILES[j % 3][1]
                    dve.wait_ge(d_emptied, DJ[f"sc{l}"] + j + 1)
                    step(dve.reciprocal(rinv_p[0:rows, j:j + 1], rsum[0:rows, j:j + 1]))
                    dve.tensor_scalar(probs[0:rows, j, :], probs[0:rows, j, :], rinv_p[0:rows, j:j + 1], None, ALU.mult
                                      ).then_inc(p_ready, 1)

                for j in range(3 * H):
                    rows = TILES[j % 3][1]
                    n = DJ[f"sc{l}"] + j
                    step(dve.tensor_reduce(nmx[0:rows, j:j + 1], full(n)[0:rows, 0:MEM], AX.X, ALU.max))
                    dve.tensor_scalar(nmx[0:rows, j:j + 1], nmx[0:rows, j:j + 1], -DH ** -0.5, None, ALU.mult).then_inc(mx_ready, 1)
                    if j >= 2:
                        normalise(j - 2)
                normalise(3 * H - 2)
                normalise(3 * H - 1)
                for n, h, k in av_order(l):
                    if k < 2:
                        dve.tensor_copy(probsT[:, h % 2, k, :], full(n)[:, 0:TOK]).then_inc(d_emptied, 1)
                    else:
                        b, bank = 2 * h + k - 2, full(n)[:, 0:TOK]
                        step(dve.tensor_copy(uT_hi[:, b, :], bank))
                        dve.tensor_tensor(uT_lo[:, b, :], bank, uT_hi[:, b, :].bitcast(F32), ALU.subtract).then_inc(d_emptied, 1)
                add_to_x(f"xo{l}")

            def best16(r, values):
                def each(op):
                    for t, (off, rows) in enumerate(TILES):
                        row_step.after(2)
                        row_step.mark(op(t, rows))

                each(lambda t, rows: dve.max(v16[0:rows, r, t, 0:8], values[0:rows, t, :]))
                each(lambda t, rows: dve.max_index(i16[0:rows, r, t, 0:8], v16[0:rows, r, t, 0:8], values[0:rows, t, :]))
                n = values.shape[-1]
                each(lambda t, rows: dve.match_replace(spare[0:rows, t, 0:n], v16[0:rows, r, t, 0:8], values[0:rows, t, :],
                                                       -3.0e38))
                each(lambda t, rows: dve.max(v16[0:rows, r, t, 8:16], spare[0:rows, t, 0:n]))
                each(lambda t, rows: dve.max_index(i16[0:rows, r, t, 8:16], v16[0:rows, r, t, 8:16], spare[0:rows, t, 0:n]))

            def choose(l):
                with dve.Fori(0, HP // 4) as i:
                    for r in range(4):
                        row_step.after(15)
                        bank = full(DJ[f"pq{l}"] + r, i, 4)[:, 0:3 * P].rearrange("p (t n) -> p t n", n=P)
                        row_step.mark(dve.tensor_copy(cur[:, r % 2, 0:2, :], bank[:, 0:2, :]))
                        row_step.mark(dve.tensor_copy(cur[0:NS, r % 2, 2, :], bank[0:NS, 2, :]))
                        row_step.after(0)
                        dve.sem_inc(d_emptied, 1)
                        best16(r, cur[:, r % 2])
                    row_step.after(0)
                    row_step.mark(dve.tensor_copy(sval[:, bass.ds(i * 4, 4)], v16))
                    row_step.mark(dve.tensor_copy(sidx[:, bass.ds(i * 4, 4)], i16))
                    row_step.restart()
                sv2 = sval.rearrange("p (h a) t k -> p h a t k", a=2)
                si2 = sidx16.rearrange("p (h a) t k -> p h a t k", a=2)
                with dve.Fori(0, PH) as i:
                    for t, (off, rows) in enumerate(TILES):
                        row_step.mark(dve.tensor_tensor(cand[0:rows, t, :].rearrange("p (a b) -> p a b", b=TOPK),
                                                        sv2[0:rows, i, 0, t, :].unsqueeze(2).to_broadcast([rows, TOPK, TOPK]),
                                                        sv2[0:rows, i, 1, t, :].unsqueeze(1).to_broadcast([rows, TOPK, TOPK]),
                                                        ALU.add))
                    best16(0, cand)
                    row_step.after(0)
                    row_step.mark(dve.tensor_copy(top[:, i], v16[:, 0]))
                    row_step.mark(dve.tensor_copy(tpos.bitcast(U32)[:, i], i16[:, 0]))
                    row_step.restart()
                for t, (off, rows) in enumerate(TILES):
                    gate = picked[0:rows, t, 2, :].rearrange("p (h k) -> p h k", k=TOPK)
                    dve.tensor_tensor(gate, top[0:rows, :, t, :], top[0:rows, :, t, 0:1].to_broadcast([rows, PH, TOPK]),
                                      ALU.subtract).then_inc(top_ready, 1)
                for t in range(3):
                    bits = cand.bitcast(U32)[:, t, :].rearrange("p (a h k) -> p a h k", a=2, k=TOPK)
                    tp = tpos.bitcast(U32)[:, :, t, :]
                    dve.tensor_scalar(bits[:, 0], tp, 4, None, ALU.logical_shift_right)
                    ins = dve.tensor_scalar(bits[:, 1], tp, 15, None, ALU.bitwise_and)
                step(ins)
                dve.tensor_copy(iota16, iota[:, 0:TOPK])
                dve.tensor_copy(sidx16, sidx)
                step(dve.tensor_copy(pij, cand.bitcast(U32).rearrange("p t (a h k) -> p t a h k", a=2, k=TOPK)))
                for t, (off, rows) in enumerate(TILES):
                    shape = [rows, 4, TOPK, TOPK]
                    for a in range(2):
                        for q in range(2):
                            hs = slice(4 * q, 4 * q + 4)
                            ins = dve.tensor_tensor(eq[0:rows, q], pij[0:rows, t, a, hs, :].unsqueeze(3).to_broadcast(shape),
                                                    iota16[0:rows].unsqueeze(1).unsqueeze(1).to_broadcast(shape),
                                                    ALU.is_equal)
                        step(ins)
                        for q in range(2):
                            hs = slice(4 * q, 4 * q + 4)
                            ins = dve.tensor_tensor(eq[0:rows, q], eq[0:rows, q],
                                                    si2[0:rows, hs, a, t, :].unsqueeze(2).to_broadcast(shape), ALU.mult)
                        step(ins)
                        for q in range(2):
                            hs = slice(4 * q, 4 * q + 4)
                            out = picked[0:rows, t, a, :].rearrange("p (h k) -> p h k", k=TOPK)[:, hs, :]
                            ins = dve.tensor_reduce(out, eq[0:rows, q], AX.X, ALU.add)
                        step(ins)

            def peer(l, norm):
                scale_rows(f"fn{l}", norm, 4 if l == 0 else 9)
                empty_transposes(f"fn{l}", TILES)
                step(dve.memset(v16, 0.0))
                step(dve.memset(i16.bitcast(F32), 0.0))
                choose(l)
                for t, (off, rows) in enumerate(TILES):
                    dve.wait_ge(exp_ready, 3 * l + t + 1)
                    gate = picked[0:rows, t, 2, :].rearrange("p (h k) -> p h k", k=TOPK)
                    step(dve.tensor_reduce(sume[0:rows, t, 0:PH], gate, AX.X, ALU.add))
                    step(dve.reciprocal(sume[0:rows, t, PH:2 * PH], sume[0:rows, t, 0:PH]))
                    dve.tensor_tensor(gate, gate, sume[0:rows, t, PH:2 * PH].unsqueeze(2).to_broadcast([rows, PH, TOPK]), ALU.mult
                                      ).then_inc(picked_ready, 1)
                for t, (off, rows) in enumerate(TILES):
                    bank = full(DJ[f"slot{l}"] + t)[:, 0:3 * P].rearrange("p (a c) -> p a c", c=P)
                    dve.tensor_copy(slots[:, :, off:off + rows], bank[:, :, 0:rows]).then_inc(d_emptied, 1)
                dve.wait_ge(d_emptied, DJ[f"slot{l}"] + 3)
                with dve.Fori(0, 5) as i:
                    for c in range(64):
                        r, g, q = c // 16, (c % 16) // 4, c % 4
                        if q == 0:
                            before = 5 * r + G_JOBS[g - 2] if g >= 2 else 5 * (r - 1) + G_JOBS[g + 2]
                            dve.wait_ge(a_filled, i * 20 + (AJ[f"gb{l}"] + before + 1))
                            dve.tensor_tensor(ohJ[:, 4 * (g % 2):4 * (g % 2) + 4, :], iota.unsqueeze(1).to_broadcast([P, 4, P]),
                                              slots[:, 1, bass.ds(i * 64 + c, 4)].unsqueeze(2).to_broadcast([P, 4, P]),
                                              ALU.is_equal)
                        ti, tg = slots[:, 0, bass.ds(i * 64 + c, 1)], slots[:, 2, bass.ds(i * 64 + c, 1)]
                        dve.tensor_scalar(oh[:, c % 8, :], iota, ti, tg, ALU.is_equal, ALU.mult).then_inc(oh_ready, 1)
                step(dve.memset(phl[:, 0, 0:P].bitcast(F32), 0.0))
                dve.memset(vhl[:, 0, 0, 0:512].bitcast(F32), 0.0).then_inc(zero_ready, 1)
                dve.wait_ge(zero_ready, l + 1)

                def product_parts(i, r):
                    if r == 0:
                        dve.wait_ge(g_loaded, i * 16 + 16 * (16 * l + 1))
                    dve.wait_ge(a_emptied, i * 8 + (AJ[f"uv{l}"] + r + 1 - LAG))
                    dve.wait_ge(v_summed, i * 8 + ((NB + 2) * l + r + 1))
                    p, ph = pf[:, r % 2, :], phl[:, r % 2, :]
                    step(dve.tensor_tensor(p.rearrange("p (c t) -> p c t", t=GC),
                                           act8[:, i % (LAG // 8), r, :].rearrange("p (c t) -> p c t", t=GC),
                                           g_ring[:, i % 2, :, r * GC:(r + 1) * GC], ALU.mult))
                    step(dve.tensor_copy(ph[:, 0:TOK], p))
                    hi = ph[:, 0:TOK].bitcast(F32)
                    dve.tensor_tensor(ph[:, TOK:TOK + NS], p[:, NP_:TOK], hi[:, NP_:TOK], ALU.subtract)
                    dve.tensor_tensor(ph[:, TOK + NS:2 * TOK], p[:, 0:NP_], hi[:, 0:NP_], ALU.subtract).then_inc(p_split, 1)
                    dve.wait_ge(vhi_ready, i * 8 + (NB * l + r + 1))
                    dve.tensor_tensor(vhl[:, r % 2, 1, :], v_raw[(r // 2) % 2][:, r % 2, :],
                                      vhl[:, r % 2, 0, :].bitcast(F32), ALU.subtract).then_inc(v_split, 1)

                with dve.Fori(0, 16) as i:
                    step.loop(i, 16)
                    for r in range(8):
                        product_parts(i, r)
                step.done(16)
                if l == 0:
                    dve.memset(u[NS:P, 2, :], 0.0).then_inc(prefix_clear, 1)
                dve.wait_ge(v_summed, (NB + 2) * (l + 1))
                for n in range(2):
                    dve.tensor_copy(acc_tmp[:, n, :], psum[:, 6 + n, :]).then_inc(acc_copied, 1)
                for t in range(2):
                    for n in range(2):
                        dst = x[:, t, n * 512:(n + 1) * 512]
                        dve.tensor_tensor(dst, psum[:, 2 + 2 * t + n, :], dst, ALU.add).then_inc(acc_emptied, 1)
                for n in range(2):
                    dst = x[0:NS, 2, n * 512:(n + 1) * 512]
                    full(DJ[f"fold{l}"] + n)
                    dve.tensor_tensor(dst, psum[0:NS, n, :], dst, ALU.add).then_inc(d_emptied, 1)

            memory(0)
            attend(0, 1)
            peer(0, 2)
            scale_rows("mix1", 3, 5)
            for b in range(KD):
                dve.tensor_copy(plT[:, b, :], full(DJ["pool"] + b)[:, 0:TOK]).then_inc(d_emptied, 1)
            dve.wait_ge(gain_loaded[0], 16 * 4)
            for g in range(4):
                if g == 3:
                    memory_rows(1)
                for t, (off, rows) in enumerate(TILES):
                    n = DJ["pool"] + KD + 3 * g + t
                    if 3 * g + t >= 2:
                        dve.wait_ge(pooled, 3 * g + t - 1)
                    tmp, dst = pool_tmp[0:rows, (3 * g + t) % 2, :], x[0:rows, t, g * DH:(g + 1) * DH]
                    dve.tensor_tensor(tmp, full(n)[0:rows, 0:DH], gain[0:rows, 0, g * DH:(g + 1) * DH], ALU.mult
                                      ).then_inc(d_emptied, 1)
                    dve.wait_ge(d_emptied, n + 1)
                    dve.tensor_tensor(dst, dst, tmp, ALU.add).then_inc(pooled, 1)
            memory(1)
            attend(1, 4)
            peer(1, 5)
            scale_rows("final", 6, 10)


def av_order(l):
    n = DJ[f"av{l}"]
    for h in range(H + 1):
        for k in ((0, 1) if h < H else ()):
            yield n, h, k
            n += 1
        for k in ((2, 3) if h >= 1 else ()):
            yield n, h - 1, k
            n += 1


def av_pt_done(l, h):
    return max(n for n, hh, k in av_order(l) if hh == h and k < 2) + 1


PQ_ORDER = [("q", 0)] + [x for m in range(7) for x in (("q", m + 1), ("s", m))] + [("s", 7)]


OUTPUTS = {"y_p": (NP_, D), "y_s": (NS, D), "Cn_p": (D, VA), "m_p": (1, H), "pool_p": (POOLST, D),
           "mem_k": (2, MEM, D), "mem_v": (2, MEM, D), "Cn_s": (D, VA), "m_s": (1, H), "pool_s": (POOLST, D)}


def chunks(w):
    return np.ascontiguousarray(w.reshape(KD, P, -1, 512).transpose(2, 1, 0, 3))


def layout(inp):
    a = {k: np.asarray(v) for k, v in inp.items()}
    w_in = a["w_mlstm_in"][0]
    t = {
        "x_prompt": a["x_prompt"], "x_sample": a["x_sample"],
        "w_qk": chunks(w_in[:, :2 * D]), "w_vo": chunks(w_in[:, 2 * D:4 * D]),
        "w_gates": w_in[:, 4 * D:].reshape(KD, P, 2 * H).transpose(1, 0, 2),
        "b_gates": np.stack([a["b_mlstm_i"][0], a["b_mlstm_f"][0]], axis=1),
        "state_m": a["state_mlstm_m"][0, 0], "state_Cn": np.concatenate([a["state_mlstm_C"].reshape(D, DH), a["state_mlstm_n"].reshape(D, 1)], axis=1),
        "state_pool": a["state_pool"][0, 0],
        "w_out": chunks(a["w_mlstm_out"][0]),
        "mem_prompt": a["mem_prompt"][0],
        "cache_kT": a["cache_mem_k"].reshape(2, MEM, D).transpose(0, 2, 1),
        "cache_v": a["cache_mem_v"].reshape(2, MEM, D),
        "gains": np.stack([a["g_mix"][0], a["g_mlstm_head"][0], a["g_mem"][0], a["g_xattn"][0], a["g_ffn"][0],
                           a["g_mix"][1], a["s_pool"][0], a["g_mem"][1], a["g_xattn"][1], a["g_ffn"][1], a["g_final"]]),
        "w_pool": a["w_pool"][0].reshape(4, 2, P, DH).transpose(2, 0, 1, 3),
        "peer_keys": a["peer_keys"].reshape(2, HP, NK, P).transpose(0, 3, 1, 2),
        "peer_u": a["peer_u"].reshape(2, NB // 2, 2, P, KD, P).transpose(0, 1, 5, 2, 4, 3),
        "peer_v": a["peer_v"].reshape(2, NB // 2, 2, P, D).transpose(0, 1, 3, 2, 4),
        "constants": constants(), "bands": bands(),
    }
    for name, key in (("w_xk", "w_xk"), ("w_xv", "w_xv"), ("w_xq", "w_xq"), ("w_xo", "w_xo"), ("w_pq", "w_peer_q")):
        t[name] = np.stack([chunks(a[key][l]) for l in range(2)])
    return {k: np.ascontiguousarray(v) for k, v in t.items()}


def results(r):
    def state(cn, m):
        return (cn[:, 0:DH].reshape(1, 1, H, DH, DH), cn[:, DH].reshape(1, 1, H, DH), m.reshape(1, 1, H))

    return (r["y_p"].reshape(1, NP_, D), r["y_s"].reshape(1, NS, D), *state(r["Cn_p"], r["m_p"]),
            r["pool_p"].reshape(1, 1, POOLST, D), r["mem_k"].reshape(2, 1, MEM, H, DH), r["mem_v"].reshape(2, 1, MEM, H, DH),
            *state(r["Cn_s"], r["m_s"]), r["pool_s"].reshape(1, 1, POOLST, D))


def kernel(**inputs):
    import concourse.bacc as bacc
    from concourse.bass_utils import run_bass_kernel_spmd

    nc = bacc.Bacc("TRN2", target_bir_lowering=False, num_devices=1)
    arrays = layout(inputs)
    t_in = {k: nc.dram_tensor(k, v.shape, F32, kind="ExternalInput").ap() for k, v in arrays.items()}
    t_out = {k: nc.dram_tensor(k, shape, F32, kind="ExternalOutput").ap() for k, shape in OUTPUTS.items()}
    build(nc, t_in, t_out)
    r = run_bass_kernel_spmd(nc, [arrays], core_ids=[0])
    return results(r.results[0])
```
